# Optimizing a Trainium2 kernel written in Bass

```python
import math
import jax, jax.numpy as jnp
from jax import lax
import numpy as np

D_MODEL = 1024
BATCH = 1
SEQ = 1024
DEPTH = 2

CTX_LEN = 256
GRID_W = 64

MLA_HEADS = 4
QK_NOPE = 64
QK_ROPE = 32
V_DIM = 64
Q_LORA = 256
KV_LORA = 128
ATTN_W = MLA_HEADS * V_DIM
Q_BLOCK = 128
ROPE_BASE = 10000.0
AXIS_DIM = QK_ROPE // 2
AXIS_FREQS = AXIS_DIM // 2

CONV_W = 256
CONV_K = 31

FOURIER_W = 256
FOURIER_GROUPS = 4
FOURIER_GDIM = FOURIER_W // FOURIER_GROUPS

SGU_W = 256
SGU_GROUPS = 4
SGU_GDIM = SGU_W // SGU_GROUPS
CHUNK = 128

MIX_W = ATTN_W + CONV_W + FOURIER_W + SGU_W

Q_OFF = 0
KV_OFF = Q_OFF + Q_LORA
ROPE_OFF = KV_OFF + KV_LORA
CONV_OFF = ROPE_OFF + QK_ROPE
FOUR_OFF = CONV_OFF + 2 * CONV_W
SGU_OFF = FOUR_OFF + FOURIER_W
GATE_OFF = SGU_OFF + 2 * SGU_W
IN_DIM = GATE_OFF + MIX_W

RMS_EPS = 1e-6
LN_EPS = 1e-5


def _rmsnorm(x, g):
    xf = x.astype(jnp.float32)
    y = xf * lax.rsqrt(jnp.mean(xf * xf, axis=-1, keepdims=True) + RMS_EPS)
    return (y * g.astype(jnp.float32)).astype(x.dtype)

def _layernorm(x, g, b):
    xf = x.astype(jnp.float32)
    mu = jnp.mean(xf, axis=-1, keepdims=True)
    var = jnp.mean(jnp.square(xf - mu), axis=-1, keepdims=True)
    y = (xf - mu) * lax.rsqrt(var + LN_EPS)
    return (y * g.astype(jnp.float32) + b.astype(jnp.float32)).astype(x.dtype)

def _axial_tables(n_tokens):
    rows = n_tokens // GRID_W
    row = jnp.broadcast_to(jnp.arange(rows)[:, None], (rows, GRID_W)).reshape(-1).astype(jnp.float32)
    col = jnp.broadcast_to(jnp.arange(GRID_W)[None, :], (rows, GRID_W)).reshape(-1).astype(jnp.float32)
    inv = ROPE_BASE ** (-jnp.arange(0, AXIS_DIM, 2, dtype=jnp.float32) / AXIS_DIM)
    ang = jnp.stack([row[:, None] * inv, col[:, None] * inv], axis=1)
    return jnp.cos(ang), jnp.sin(ang)

def _rope2d(x, cos, sin):
    shp = (1, cos.shape[0]) + (1,) * (x.ndim - 3) + (2, AXIS_FREQS)
    c = cos.reshape(shp)
    s = sin.reshape(shp)
    xr = x.astype(jnp.float32).reshape(x.shape[:-1] + (2, 2, AXIS_FREQS))
    x1, x2 = xr[..., 0, :], xr[..., 1, :]
    out = jnp.stack([x1 * c - x2 * s, x1 * s + x2 * c], axis=-2)
    return out.reshape(x.shape).astype(x.dtype)

def _mla_q(q_part, p):
    b, n, _ = q_part.shape
    c_q = _rmsnorm(q_part, p["q_norm_g"])
    return (c_q @ p["w_uq"]).reshape(b, n, MLA_HEADS, QK_NOPE + QK_ROPE)

def _mla_kv(kv_part, p):
    b, n, _ = kv_part.shape
    c_kv = _rmsnorm(kv_part[..., :KV_LORA], p["kv_norm_g"])
    kv = (c_kv @ p["w_ukv"]).reshape(b, n, MLA_HEADS, QK_NOPE + V_DIM)
    return kv[..., :QK_NOPE], kv_part[..., KV_LORA:], kv[..., QK_NOPE:]

def _assemble_k(k_nope, k_rope):
    k_r = jnp.broadcast_to(k_rope[:, :, None, :], k_nope.shape[:3] + (QK_ROPE,))
    return jnp.concatenate([k_nope, k_r], axis=-1)

def _attend(q, k, v):
    scale = 1.0 / math.sqrt(QK_NOPE + QK_ROPE)
    s = jnp.einsum("bqhd,bkhd->bhqk", q, k, preferred_element_type=jnp.float32) * scale
    pr = jax.nn.softmax(s, axis=-1)
    return jnp.einsum("bhqk,bkhd->bqhd", pr.astype(v.dtype), v)

def _block_attention(q, k, v):
    b, n, h, dk = q.shape
    nb = n // Q_BLOCK
    qb = q.reshape(b, nb, Q_BLOCK, h, dk).swapaxes(0, 1)
    ob = lax.map(lambda qq: _attend(qq, k, v), qb)
    return ob.swapaxes(0, 1).reshape(b, n, h * V_DIM)

def _conv_module(a, p):
    glu = a[..., :CONV_W] * jax.nn.sigmoid(a[..., CONV_W:])
    y = lax.conv_general_dilated(
        glu, p["conv_w"][:, None, :].astype(glu.dtype), window_strides=(1,),
        padding=[(CONV_K // 2, CONV_K // 2)], dimension_numbers=("NWC", "WIO", "NWC"),
        feature_group_count=CONV_W)
    y = y + p["conv_b"]
    y = jax.nn.silu(_layernorm(y, p["conv_ln_g"], p["conv_ln_b"]))
    return y @ p["w_pw"] + p["b_pw"]

def _fourier(f, p):
    b, n, _ = f.shape
    fg = f.astype(jnp.float32).reshape(b, n, FOURIER_GROUPS, FOURIER_GDIM)
    mixed = jnp.fft.fft2(fg, axes=(1, 3), norm="ortho").real.reshape(b, n, FOURIER_W).astype(f.dtype)
    return mixed @ p["w_fourier"] + p["b_fourier"]

def _spatial_gating(uv, p):
    u, v = uv[..., :SGU_W], uv[..., SGU_W:]
    v = _layernorm(v, p["sgu_ln_g"], p["sgu_ln_b"])
    b, n, _ = v.shape
    vc = v.reshape(b, n // CHUNK, CHUNK, SGU_GROUPS, SGU_GDIM)
    mixed = jnp.einsum("gij,bnjgc->bnigc", p["w_s"], vc) + p["b_s"].T[None, None, :, :, None]
    return u * mixed.reshape(b, n, SGU_W)

def _branches(hp, attn, p):
    conv = _conv_module(hp[..., CONV_OFF:FOUR_OFF], p)
    four = _fourier(hp[..., FOUR_OFF:SGU_OFF], p)
    sgu = _spatial_gating(hp[..., SGU_OFF:GATE_OFF], p)
    y = jnp.concatenate([attn, conv, four, sgu], axis=-1) * jax.nn.silu(hp[..., GATE_OFF:])
    return y @ p["w_out"]

def _layer(x, xc, c, c_ctx, p, cos, sin, need_ctx_out):
    shift, scale, gate = jnp.split(jax.nn.silu(c) @ p["w_ada"] + p["b_ada"], 3, axis=-1)
    shift_c, scale_c, gate_c = jnp.split(jax.nn.silu(c_ctx) @ p["w_ada"] + p["b_ada"], 3, axis=-1)
    h = _rmsnorm(x, p["norm_g"]) * (1.0 + scale[:, None, :]) + shift[:, None, :]
    hc = _rmsnorm(xc, p["norm_g"]) * (1.0 + scale_c) + shift_c

    hp = h @ p["w_in"]
    if need_ctx_out:
        hpc = hc @ p["w_in"]
        ctx_kv = hpc[..., KV_OFF:CONV_OFF]
    else:
        ctx_kv = hc @ p["w_in"][:, KV_OFF:CONV_OFF]

    kn_c, kr_c, v_c = _mla_kv(ctx_kv, p)
    k_c = _assemble_k(kn_c, kr_c)

    q = _mla_q(hp[..., Q_OFF:KV_OFF], p)
    q = jnp.concatenate([q[..., :QK_NOPE], _rope2d(q[..., QK_NOPE:], cos, sin)], axis=-1)
    kn, kr, v = _mla_kv(hp[..., KV_OFF:CONV_OFF], p)
    k = _assemble_k(kn, _rope2d(kr, cos, sin))
    k_all = jnp.concatenate([k, k_c], axis=1)
    v_all = jnp.concatenate([v, v_c], axis=1)
    attn = _block_attention(q, k_all, v_all)

    x = x + gate[:, None, :] * _branches(hp, attn, p)

    if need_ctx_out:
        q_c = _mla_q(hpc[..., Q_OFF:KV_OFF], p)
        b, l = xc.shape[0], xc.shape[1]
        attn_c = _attend(q_c, k_c, v_c).reshape(b, l, ATTN_W)
        xc = xc + gate_c * _branches(hpc, attn_c, p)
    return x, xc

def first_inputs(seed: int = 0) -> dict:
    key = jax.random.key(seed)
    ks = iter(jax.random.split(key, 40))
    f32 = jnp.float32

    def nrm(shape, s):
        return jax.random.normal(next(ks), shape, f32) * s

    def gain(shape):
        return 1.0 + 0.02 * jax.random.normal(next(ks), shape, f32)

    L = DEPTH
    return {
        "x": nrm((BATCH, SEQ, D_MODEL), 1.0),
        "c": nrm((BATCH, D_MODEL), 1.0),
        "ctx": nrm((BATCH, CTX_LEN, D_MODEL), 1.0),
        "c_ctx": nrm((D_MODEL,), 1.0),
        "w_ada": nrm((L, D_MODEL, 3 * D_MODEL), 0.5 * D_MODEL ** -0.5),
        "b_ada": nrm((L, 3 * D_MODEL), 0.01),
        "norm_g": gain((L, D_MODEL)),
        "w_in": nrm((L, D_MODEL, IN_DIM), D_MODEL ** -0.5),
        "q_norm_g": gain((L, Q_LORA)),
        "w_uq": nrm((L, Q_LORA, MLA_HEADS * (QK_NOPE + QK_ROPE)), Q_LORA ** -0.5),
        "kv_norm_g": gain((L, KV_LORA)),
        "w_ukv": nrm((L, KV_LORA, MLA_HEADS * (QK_NOPE + V_DIM)), KV_LORA ** -0.5),
        "conv_w": nrm((L, CONV_K, CONV_W), CONV_K ** -0.5),
        "conv_b": nrm((L, CONV_W), 0.01),
        "conv_ln_g": gain((L, CONV_W)),
        "conv_ln_b": nrm((L, CONV_W), 0.01),
        "w_pw": nrm((L, CONV_W, CONV_W), CONV_W ** -0.5),
        "b_pw": nrm((L, CONV_W), 0.01),
        "w_fourier": nrm((L, FOURIER_W, FOURIER_W), FOURIER_W ** -0.5),
        "b_fourier": nrm((L, FOURIER_W), 0.01),
        "sgu_ln_g": gain((L, SGU_W)),
        "sgu_ln_b": nrm((L, SGU_W), 0.01),
        "w_s": nrm((L, SGU_GROUPS, CHUNK, CHUNK), 0.5 * CHUNK ** -0.5),
        "b_s": 1.0 + nrm((L, SGU_GROUPS, CHUNK), 0.1),
        "w_out": nrm((L, MIX_W, D_MODEL), MIX_W ** -0.5),
        "final_g": gain((D_MODEL,)),
    }

def first_block(x, c, ctx, c_ctx, w_ada, b_ada, norm_g, w_in, q_norm_g, w_uq, kv_norm_g, w_ukv,
              conv_w, conv_b, conv_ln_g, conv_ln_b, w_pw, b_pw, w_fourier, b_fourier,
              sgu_ln_g, sgu_ln_b, w_s, b_s, w_out, final_g):
    n_tokens = x.shape[1]
    cos, sin = _axial_tables(n_tokens)
    xc = ctx
    for i in range(DEPTH):
        p = {
            "w_ada": w_ada[i], "b_ada": b_ada[i], "norm_g": norm_g[i], "w_in": w_in[i],
            "q_norm_g": q_norm_g[i], "w_uq": w_uq[i], "kv_norm_g": kv_norm_g[i], "w_ukv": w_ukv[i],
            "conv_w": conv_w[i], "conv_b": conv_b[i], "conv_ln_g": conv_ln_g[i], "conv_ln_b": conv_ln_b[i],
            "w_pw": w_pw[i], "b_pw": b_pw[i], "w_fourier": w_fourier[i], "b_fourier": b_fourier[i],
            "sgu_ln_g": sgu_ln_g[i], "sgu_ln_b": sgu_ln_b[i], "w_s": w_s[i], "b_s": b_s[i],
            "w_out": w_out[i],
        }
        x, xc = _layer(x, xc, c, c_ctx, p, cos, sin, need_ctx_out=(i < DEPTH - 1))
    return _rmsnorm(x, final_g)


DEPTH_2 = 1

MEM_LEN = 256
A_HEADS = 4
A_QK_DIM = 64
A_V_DIM = 2 * A_QK_DIM
B_HEADS = 4
B_HEAD_DIM = 64
DILATED_PATTERNS = ((128, 1), (512, 4), (2048, 16))
DILATED_BLK = 128
C_HEADS = 4
C_HEAD_DIM = 64
IDX_HEADS = 8
IDX_DIM = 64
TOPK_MAX = 256
IN_SPLITS = (
    A_HEADS * 2 * A_QK_DIM,
    A_HEADS * 2 * A_QK_DIM,
    A_HEADS * A_V_DIM,
    B_HEADS * B_HEAD_DIM,
    B_HEADS * B_HEAD_DIM,
    B_HEADS * B_HEAD_DIM,
    C_HEADS * C_HEAD_DIM,
    C_HEADS * C_HEAD_DIM,
    C_HEADS * C_HEAD_DIM,
    IDX_HEADS * IDX_DIM,
    IDX_DIM,
    IDX_HEADS,
)
N_IN = 3656
MIX_WIDTH = A_HEADS * A_V_DIM + B_HEADS * B_HEAD_DIM + C_HEADS * C_HEAD_DIM
REL_BUCKETS = 32
REL_MAX_DIST = 2048
N_BIAS_HEADS = A_HEADS + B_HEADS + C_HEADS
MEM_HEADS = 4
MEM_HEAD_DIM = D_MODEL // MEM_HEADS
D_FF = 2816
CONV_WIDTH = 3

Q_BLK = 128
EPS = 1e-6
NEG = -1e30


def rmsnorm(x, g):
    x32 = x.astype(jnp.float32)
    y = x32 * lax.rsqrt(jnp.mean(x32 * x32, axis=-1, keepdims=True) + EPS)
    return (y * g.astype(jnp.float32)).astype(x.dtype)

def rel_bucket(dist):
    n = jnp.maximum(dist, 0)
    max_exact = REL_BUCKETS // 2
    nf = jnp.maximum(n, 1).astype(jnp.float32)
    large = max_exact + (jnp.log(nf / max_exact) / math.log(REL_MAX_DIST / max_exact)
                         * (REL_BUCKETS - max_exact)).astype(jnp.int32)
    large = jnp.minimum(large, REL_BUCKETS - 1)
    return jnp.where(n < max_exact, n, large)

def diff_attention(q, k, v, lam, lam_init, subln_g, table):
    Bn, S, H, _, d = q.shape
    nb = S // Q_BLK
    scale = d ** -0.5
    kpos = jnp.arange(S, dtype=jnp.int32)
    v32 = v.astype(jnp.float32)

    def block(args):
        qb, start = args
        qpos = start + jnp.arange(Q_BLK, dtype=jnp.int32)
        s = jnp.einsum('bqhmd,bkhmd->bhmqk', qb, k).astype(jnp.float32) * scale
        dist = qpos[:, None] - kpos[None, :]
        bias = jnp.transpose(table[rel_bucket(dist)].astype(jnp.float32), (2, 0, 1))
        s = jnp.where(dist >= 0, s + bias[None, :, None], NEG)
        p = jax.nn.softmax(s, axis=-1)
        attn = p[:, :, 0] - lam * p[:, :, 1]
        return jnp.einsum('bhqk,bkhd->bqhd', attn, v32)

    qb = jnp.moveaxis(q.reshape(Bn, nb, Q_BLK, H, 2, d), 1, 0)
    starts = jnp.arange(nb, dtype=jnp.int32) * Q_BLK
    o = lax.map(block, (qb, starts))
    o = jnp.moveaxis(o, 0, 1).reshape(Bn, S, H, v.shape[-1])
    return rmsnorm(o, subln_g) * (1.0 - lam_init)

def dilated_branch(q, k, v, window, r, table, scale):
    Bn, S, H, d = q.shape
    n_back = window // r
    unit = r * DILATED_BLK
    S_pad = -(-S // unit) * unit
    nb = S_pad // unit
    pad = ((0, 0), (0, S_pad - S), (0, 0), (0, 0))
    qb = jnp.pad(q, pad).reshape(Bn, nb, DILATED_BLK, r, H, d)
    kb = jnp.pad(k, pad).reshape(Bn, nb, DILATED_BLK, r, H, d)
    vb = jnp.pad(v, pad).reshape(Bn, nb, DILATED_BLK, r, H, d)

    def with_prev(t):
        prev = jnp.pad(t, ((0, 0), (1, 0), (0, 0), (0, 0), (0, 0), (0, 0)))[:, :nb]
        return jnp.concatenate([prev, t], axis=2)

    kk = with_prev(kb)
    vv = with_prev(vb).astype(jnp.float32)
    s = jnp.einsum('bnqchd,bnkchd->bnchqk', qb, kk).astype(jnp.float32) * scale
    qi = jnp.arange(DILATED_BLK, dtype=jnp.int32)[:, None]
    ki = jnp.arange(2 * DILATED_BLK, dtype=jnp.int32)[None, :]
    dist_m = qi + DILATED_BLK - ki
    m_q = jnp.arange(nb, dtype=jnp.int32)[:, None, None] * DILATED_BLK + qi[None]
    mask = (dist_m >= 0) & (dist_m <= n_back) & (m_q - dist_m >= 0)
    bias = jnp.transpose(table[rel_bucket(dist_m * r)].astype(jnp.float32), (2, 0, 1))
    s = jnp.where(mask[None, :, None, None], s + bias, NEG)
    lse = jax.nn.logsumexp(s, axis=-1)
    p = jnp.exp(s - lse[..., None])
    o = jnp.einsum('bnchqk,bnkchd->bnqchd', p, vv).reshape(Bn, S_pad, H, d)[:, :S]
    lse = jnp.transpose(lse, (0, 1, 4, 2, 3)).reshape(Bn, S_pad, H)[:, :S]
    return o, lse

def dilated_attention(q, k, v, table):
    scale = q.shape[-1] ** -0.5
    outs, lses = [], []
    for window, r in DILATED_PATTERNS:
        o, lse = dilated_branch(q, k, v, window, r, table, scale)
        outs.append(o)
        lses.append(lse)
    wts = jax.nn.softmax(jnp.stack(lses, 0), axis=0)
    return jnp.einsum('pbsh,pbshd->bshd', wts, jnp.stack(outs, 0))

def dsa_attention(q, k, v, iq, ik, iw, table):
    Bn, S, H, d = q.shape
    nb = S // Q_BLK
    topk = min(TOPK_MAX, S // 4)
    scale = d ** -0.5
    kpos = jnp.arange(S, dtype=jnp.int32)
    iw = iw.astype(jnp.float32) * (IDX_HEADS ** -0.5)

    def block(args):
        qb, iqb, iwb, start = args
        qpos = start + jnp.arange(Q_BLK, dtype=jnp.int32)
        logits = jnp.einsum('bqhd,bkd->bqhk', iqb, ik).astype(jnp.float32) * (IDX_DIM ** -0.5)
        score = jnp.einsum('bqhk,bqh->bqk', jax.nn.relu(logits), iwb)
        score = jnp.where(kpos[None, None, :] <= qpos[None, :, None], score, NEG)
        _, idx = lax.top_k(score, topk)
        valid = idx <= qpos[None, :, None]
        flat = idx.reshape(Bn, Q_BLK * topk)
        ks = jax.vmap(lambda kb, ib: kb[ib])(k, flat).reshape(Bn, Q_BLK, topk, H, d)
        vs = jax.vmap(lambda vb, ib: vb[ib])(v, flat).reshape(Bn, Q_BLK, topk, H, d)
        s = jnp.einsum('bqhd,bqkhd->bhqk', qb, ks).astype(jnp.float32) * scale
        bias = jnp.transpose(table[rel_bucket(qpos[None, :, None] - idx)].astype(jnp.float32), (0, 3, 1, 2))
        s = jnp.where(valid[:, None], s + bias, NEG)
        p = jax.nn.softmax(s, axis=-1)
        return jnp.einsum('bhqk,bqkhd->bqhd', p, vs.astype(jnp.float32))

    qb = jnp.moveaxis(q.reshape(Bn, nb, Q_BLK, H, d), 1, 0)
    iqb = jnp.moveaxis(iq.reshape(Bn, nb, Q_BLK, IDX_HEADS, IDX_DIM), 1, 0)
    iwb = jnp.moveaxis(iw.reshape(Bn, nb, Q_BLK, IDX_HEADS), 1, 0)
    starts = jnp.arange(nb, dtype=jnp.int32) * Q_BLK
    o = lax.map(block, (qb, iqb, iwb, starts))
    return jnp.moveaxis(o, 0, 1).reshape(Bn, S, H, d)

def hybrid_mixer(h, w_in, lam_q1, lam_k1, lam_q2, lam_k2, subln_g, w_out, rel_bias, layer_idx):
    Bn, S, _ = h.shape
    proj = h @ w_in
    (aq, ak, av, bq, bk, bv, cq, ck, cv, iq, ik, iw) = jnp.split(
        proj, np.cumsum(IN_SPLITS)[:-1].tolist(), axis=-1)
    lam_init = 0.8 - 0.6 * math.exp(-0.3 * layer_idx)
    lam = (jnp.exp(jnp.sum(lam_q1.astype(jnp.float32) * lam_k1.astype(jnp.float32)))
           - jnp.exp(jnp.sum(lam_q2.astype(jnp.float32) * lam_k2.astype(jnp.float32))) + lam_init)
    o_a = diff_attention(aq.reshape(Bn, S, A_HEADS, 2, A_QK_DIM), ak.reshape(Bn, S, A_HEADS, 2, A_QK_DIM),
                         av.reshape(Bn, S, A_HEADS, A_V_DIM), lam, lam_init, subln_g,
                         rel_bias[:, :A_HEADS])
    o_b = dilated_attention(bq.reshape(Bn, S, B_HEADS, B_HEAD_DIM), bk.reshape(Bn, S, B_HEADS, B_HEAD_DIM),
                            bv.reshape(Bn, S, B_HEADS, B_HEAD_DIM),
                            rel_bias[:, A_HEADS:A_HEADS + B_HEADS])
    o_c = dsa_attention(cq.reshape(Bn, S, C_HEADS, C_HEAD_DIM), ck.reshape(Bn, S, C_HEADS, C_HEAD_DIM),
                        cv.reshape(Bn, S, C_HEADS, C_HEAD_DIM), iq.reshape(Bn, S, IDX_HEADS, IDX_DIM),
                        ik, iw, rel_bias[:, A_HEADS + B_HEADS:])
    o = jnp.concatenate([o_a.reshape(Bn, S, -1), o_b.reshape(Bn, S, -1), o_c.reshape(Bn, S, -1)],
                        axis=-1).astype(h.dtype)
    return o @ w_out

def memory_attention(h, mem_n, w_mq, w_mkv, w_mo):
    Bn, S, D = h.shape
    q = (h @ w_mq).reshape(Bn, S, MEM_HEADS, MEM_HEAD_DIM)
    k, v = jnp.split(mem_n @ w_mkv, 2, axis=-1)
    k = k.reshape(Bn, -1, MEM_HEADS, MEM_HEAD_DIM)
    v = v.reshape(Bn, -1, MEM_HEADS, MEM_HEAD_DIM)
    s = jnp.einsum('bqhd,bkhd->bhqk', q, k).astype(jnp.float32) * (MEM_HEAD_DIM ** -0.5)
    p = jax.nn.softmax(s, axis=-1)
    o = jnp.einsum('bhqk,bkhd->bqhd', p, v.astype(jnp.float32)).astype(h.dtype).reshape(Bn, S, D)
    return o @ w_mo

def conv_ffn(h, w_up, conv_w, conv_b, w_down):
    S = h.shape[1]
    u = h @ w_up
    u_p = jnp.pad(u, ((0, 0), (CONV_WIDTH - 1, 0), (0, 0)))
    c = conv_b
    for j in range(CONV_WIDTH):
        c = c + conv_w[j] * u_p[:, j:j + S]
    gate, val = jnp.split(c, 2, axis=-1)
    return (jax.nn.silu(gate) * val) @ w_down

def second_inputs(seed: int = 0) -> dict:
    key = jax.random.key(seed)
    ks = jax.random.split(key, 24)

    def nrm(k, shape, scale):
        return jax.random.normal(k, shape, jnp.float32) * scale

    L, D, F = DEPTH_2, D_MODEL, D_FF
    return {
        "x": nrm(ks[0], (BATCH, SEQ, D), 1.0),
        "mem": nrm(ks[1], (BATCH, MEM_LEN, D), 1.0),
        "rel_bias": nrm(ks[2], (REL_BUCKETS, N_BIAS_HEADS), 0.2),
        "norm_mix": 1.0 + nrm(ks[3], (L, D), 0.1),
        "w_in": nrm(ks[4], (L, D, N_IN), D ** -0.5),
        "lam_q1": nrm(ks[5], (L, A_QK_DIM), 0.1),
        "lam_k1": nrm(ks[6], (L, A_QK_DIM), 0.1),
        "lam_q2": nrm(ks[7], (L, A_QK_DIM), 0.1),
        "lam_k2": nrm(ks[8], (L, A_QK_DIM), 0.1),
        "subln": 1.0 + nrm(ks[9], (L, A_V_DIM), 0.1),
        "w_out": nrm(ks[10], (L, MIX_WIDTH, D), MIX_WIDTH ** -0.5),
        "norm_mem": 1.0 + nrm(ks[11], (L, D), 0.1),
        "norm_memkv": 1.0 + nrm(ks[12], (L, D), 0.1),
        "w_mq": nrm(ks[13], (L, D, D), D ** -0.5),
        "w_mkv": nrm(ks[14], (L, D, 2 * D), D ** -0.5),
        "w_mo": nrm(ks[15], (L, D, D), D ** -0.5),
        "norm_ffn": 1.0 + nrm(ks[16], (L, D), 0.1),
        "w_up": nrm(ks[17], (L, D, 2 * F), D ** -0.5),
        "conv_w": nrm(ks[18], (L, CONV_WIDTH, 2 * F), CONV_WIDTH ** -0.5),
        "conv_b": nrm(ks[19], (L, 2 * F), 0.02),
        "w_down": nrm(ks[20], (L, F, D), F ** -0.5),
        "norm_final": 1.0 + nrm(ks[21], (D,), 0.1),
    }

def second_block(x, mem, rel_bias, norm_mix, w_in, lam_q1, lam_k1, lam_q2, lam_k2, subln, w_out,
              norm_mem, norm_memkv, w_mq, w_mkv, w_mo, norm_ffn, w_up, conv_w, conv_b, w_down,
              norm_final):
    for l in range(DEPTH_2):
        h = rmsnorm(x, norm_mix[l])
        x = x + hybrid_mixer(h, w_in[l], lam_q1[l], lam_k1[l], lam_q2[l], lam_k2[l], subln[l],
                             w_out[l], rel_bias, l)
        h = rmsnorm(x, norm_mem[l])
        x = x + memory_attention(h, rmsnorm(mem, norm_memkv[l]), w_mq[l], w_mkv[l], w_mo[l])
        h = rmsnorm(x, norm_ffn[l])
        x = x + conv_ffn(h, w_up[l], conv_w[l], conv_b[l], w_down[l])
    return rmsnorm(x, norm_final)


def setup_inputs(seed=0):
    out = dict(first_inputs(seed))
    for name, value in second_inputs(seed + 1).items():
        if name != "x":
            out[name + "_2"] = value
    return out


def reference(
    x, c, ctx, c_ctx, w_ada, b_ada, norm_g, w_in, q_norm_g, w_uq, kv_norm_g, w_ukv, conv_w,
    conv_b, conv_ln_g, conv_ln_b, w_pw, b_pw, w_fourier, b_fourier, sgu_ln_g, sgu_ln_b, w_s,
    b_s, w_out, final_g, mem_2, rel_bias_2, norm_mix_2, w_in_2, lam_q1_2, lam_k1_2, lam_q2_2,
    lam_k2_2, subln_2, w_out_2, norm_mem_2, norm_memkv_2, w_mq_2, w_mkv_2, w_mo_2, norm_ffn_2,
    w_up_2, conv_w_2, conv_b_2, w_down_2, norm_final_2,
):
    x = first_block(
        x, c, ctx, c_ctx, w_ada, b_ada, norm_g, w_in, q_norm_g, w_uq, kv_norm_g, w_ukv, conv_w,
        conv_b, conv_ln_g, conv_ln_b, w_pw, b_pw, w_fourier, b_fourier, sgu_ln_g, sgu_ln_b, w_s,
        b_s, w_out, final_g,
    )
    return second_block(
        x, mem_2, rel_bias_2, norm_mix_2, w_in_2, lam_q1_2, lam_k1_2, lam_q2_2, lam_k2_2,
        subln_2, w_out_2, norm_mem_2, norm_memkv_2, w_mq_2, w_mkv_2, w_mo_2, norm_ffn_2, w_up_2,
        conv_w_2, conv_b_2, w_down_2, norm_final_2,
    )


_drawn_inputs = setup_inputs


def setup_inputs(seed=0):
    import zlib

    import numpy as np

    out = dict(_drawn_inputs(seed))
    spreads = {}
    factors = {'ctx': 8.0,
     'c_ctx': 3.421,
     'b_ada': 4.029,
     'norm_g': 5.925,
     'q_norm_g': 8.0,
     'w_uq': 3.15,
     'kv_norm_g': 8.0,
     'conv_b': 8.0,
     'conv_ln_g': 8.0,
     'conv_ln_b': 8.0,
     'b_pw': 8.0,
     'b_fourier': 8.0,
     'sgu_ln_g': 8.0,
     'sgu_ln_b': 8.0,
     'b_s': 2.747,
     'lam_q1_2': 6.112,
     'lam_k1_2': 5.173,
     'norm_mem_2': 5.234,
     'norm_memkv_2': 3.687,
     'conv_b_2': 11.74,
     'lam_q2_2': 4.678,
     'lam_k2_2': 3.669}
    for name, (base, spread) in spreads.items():
        noise = np.random.default_rng([zlib.crc32(name.encode()), seed]).standard_normal(out[name].shape)
        drawn = base * np.exp(spread * noise) if base else spread * noise
        out[name] = __import__('jax').numpy.asarray(drawn.astype(out[name].dtype))
    for name, factor in factors.items():
        out[name] = (out[name] * factor).astype(out[name].dtype)
    return out
```

```python
import math
from contextlib import ExitStack

import numpy as np
import concourse.bass as bass
from concourse import mybir

ALU = mybir.AluOpType
ACT = mybir.ActivationFunctionType
AX = mybir.AxisListType
F32 = mybir.dt.float32

P = 128
D = 1024
N = 1024
L = 256
T = N + L
KD = D // P
LAYERS = 2
CHUNKS = ((0, 512), (512, 512), (1024, 256))
QT = N // P
CT = L // P
HEADS = 4
TAPS = 31
HALF = TAPS // 2
EPS_RMS, EPS_LN = 1e-6, 1e-5
MLA_SCALE = 1.0 / math.sqrt(96)
LAM_INIT = 0.2
NEG = -1e30
TAKEN = -3e38
TOPK = 256
FF = 22
FGROUPS = ((0, 8), (8, 8), (16, 6))
VEC = N + P - 1

W_IN_BLOCKS = 22

VCOL = {}


def _layout_vectors():
    n = 0
    for l in range(LAYERS):
        for name, width in (("b_ada", 24), ("norm_g", 8), ("q_norm_g", 2), ("kv_norm_g", 1), ("conv_w", 62),
                            ("conv_b", 2), ("conv_ln_g", 2), ("conv_ln_b", 2), ("b_pw", 2), ("b_fourier", 2)):
            VCOL[name, l] = n
            n += width
    for name, width in (("c", 16), ("final_g", 8), ("norm_mix", 8), ("norm_mem", 8), ("norm_memkv", 8),
                        ("norm_ffn", 8), ("norm_final", 8), ("subln", 1), ("conv_w2", 132), ("conv_b2", 44)):
        VCOL[name] = n
        n += width
    return n


NV = _layout_vectors()

X0 = 0
H0 = 8 * T
Y0 = 16 * T
S0 = 24 * T
SLOTS = 4
TOP = 53208
RING0 = TOP - SLOTS * 1024
IDENT0 = RING0 - P
ONES0 = IDENT0 - P
CD0 = ONES0 - 256
VEC0 = CD0 - NV
MOD0 = VEC0 - 112
AM0 = MOD0 - 16
SQ0 = AM0 - 1024
RR0 = SQ0 - T
SM0 = RR0 - 204
BSB0 = SM0 - 256
S_END = BSB0
VCH = ((0, 512), (512, 512), (1024, VEC - 1024))

MQ0, MKV0, MV0 = S0, S0 + 2 * T, S0 + 3 * T
KH0 = MV0 + 10 * 256
CS0 = KH0 + 2 * T
AO0 = CS0 + N
RT0 = AO0 + 10 * 256
QH0, PR0, PT0 = Y0 + 2 * T, Y0 + 4 * T, Y0 + 6 * T
GW = T + 4 * HALF
CW = GW - 2 * HALF
GLU0, CV0 = S0, S0 + 2 * GW
FM0 = CV0 + 2 * CW
SIG0 = FM0 + 2 * T
LNG0 = SIG0 + 1024
YT0 = LNG0 + 512
UU0, VN0 = GLU0, GLU0 + 2 * T
H20, Y20, Z0 = H0, H0 + KD * N, H0 + 2 * KD * N
SEL_AT = {t: Z0 + P * sum(range(3, t + 1)) for t in range(2, QT)}
Q20 = Z0 + P * sum(range(3, QT + 1))
K20, V20, STRIP0 = Q20 + 2048, Q20 + 4096, Q20 + 6144
IQ0, IK0, IR0 = Q20, Q20 + 4096, Q20 + 5120
SC0 = STRIP0 + 4096
PT20, OT20 = SC0 + 2048, SC0 + 3072
SC1 = Y20 + 6 * N
QM0 = Z0
KM0, VM0, MEM0, PM0 = QM0 + 8192, QM0 + 10240, QM0 + 12288, QM0 + 14336
PMT0 = PM0 + 1024
ACT0, UW = Y20, N + 2
UB0 = ACT0 + 16 * N
CB0 = UB0 + 4 * UW

assert max(RT0 + 1024, YT0 + 5120, OT20 + 512, PMT0 + 2048, CB0 + 4 * N) <= S_END
assert UU0 + 4 * T <= FM0 and PT0 + 2 * T <= S0


def gcol(c):
    return CHUNKS[c][0] + (HALF if c < 2 else 3 * HALF)


def ccol(c):
    return CHUNKS[c][0] + (0 if c < 2 else 2 * HALF)


def c_of(t):
    return min(t // 4, 2)


def units(l):
    return [(h, t) for h in range(HEADS) for t in range(QT + (CT if l == 0 else 0))]


def units2(br):
    return [(t, h) for t in range(QT) for h in range(2 if br < 2 else 4)]


def own_chunks(l):
    return CHUNKS if l == 0 else CHUNKS[:2]


class Steps:

    def __init__(self, sems, known):
        self.sems, self.known, self.count, self.at = sems, known, {}, {}

    def reach(self, name, key, by):
        self.count[name] = self.count.get(name, 0) + by
        if key is not None:
            assert key not in self.at, key
            self.at[key] = (name, self.count[name])
        return self.sems[name], by

    def value(self, key):
        name, value = self.known[key] if self.known and key is not None else ("tensor_done", 0)
        return self.sems[name], value


class Engine:

    def __init__(self, steps, name, raw):
        self.steps, self.name, self.raw, self.reached = steps, name, raw, {}

    def step(self, key=None):
        return self.steps.reach(self.name, key, 1)

    def wait_ge(self, semaphore, value):
        if value > self.reached.get(semaphore.name, 0):
            self.reached[semaphore.name] = value
            self.raw.wait_ge(semaphore, value)


class Psum:

    def __init__(self, tensor, steps):
        self.tensor, self.steps, self.next, self.reader, self.bank = tensor, steps, 0, {}, {}

    def take(self, e, key, reader, n=1):
        if self.next + n > 8:
            self.next = 0
        b = self.next
        self.next = (b + n) % 8
        for i in range(b, b + n):
            for step in self.reader.get(i, []):
                e.wait_ge(*self.steps.value(step))
            self.reader[i] = reader if isinstance(reader, list) else [reader]
        self.bank[key] = b
        return self.at(key)

    def at(self, key):
        return self.tensor[:, self.bank[key] * 512:8 * 512]


class Ring:

    def __init__(self, tensor, steps):
        self.tensor, self.steps, self.loads = tensor, steps, []

    def take(self, e, name, index, width, release, parts=P):
        n = len(self.loads)
        slot = n % SLOTS
        self.loads.append((name, index, width, slot, release, parts))
        e.wait_ge(*self.steps.value(("loaded", n)))
        a = RING0 + slot * 1024
        return self.tensor[0:parts, a:a + width]



LOADS = ("consts_loaded", "rope_loaded", "gate_bias_loaded", "strips_loaded", "mem_loaded", "lambda_loaded")
STORES = ("vec_stored", "rows_stored", "out_stored")


def program(nc, A, known):
    stack = ExitStack()
    sems = {}
    for name in ("tensor_done", "scalar_done", "vector_done", "pool_done") + LOADS + STORES + tuple(
            f"tile{i}_loaded" for i in range(SLOTS)):
        sems[name] = stack.enter_context(nc.semaphore(name))
    steps = Steps(sems, known)
    S = stack.enter_context(nc.sbuf_tensor("sb", [P, TOP], F32))
    PS = stack.enter_context(nc.psum_tensor("ps", [P, 8 * 512], F32))
    psum, ring = Psum(PS, steps), Ring(S, steps)
    at = steps.value

    def loads(name, key):
        return steps.reach(name, key, 16)

    vec_dram = nc.dram_tensor("vec_dram", (12, VEC), F32, kind="Internal").ap()
    rows_dram = nc.dram_tensor("rows_dram", (12, P, VEC), F32, kind="Internal").ap()

    def view(at, a, b=None):
        v = S[:, at:at + a * (b or 1)]
        return v.rearrange("p (a b) -> p a b", b=b) if b else v

    X, H, Y = view(X0, KD, T), view(H0, KD, T), view(Y0, KD, T)
    ident, ones, cd = view(IDENT0, P), view(ONES0, P), view(CD0, 256)
    mod, silu_c, am = view(MOD0, 48, 2), view(MOD0 + 96, KD, 2), view(AM0, KD, 2)
    sq, rr, small, bsb = view(SQ0, 2, 512), view(RR0, T), view(SM0, 204), view(BSB0, 2, P)
    eps_rms, eps_ln, ln_scale = small[:, 60:61], small[:, 61:62], small[:, 62:63]
    mq, mkv, mv = view(MQ0, 2, T), view(MKV0, T), view(MV0, 10, 256)
    kh, qh, cs = view(KH0, 2, T), view(QH0, 2, T), view(CS0, N)
    ao, rt, prob, pt = view(AO0, 10, 256), view(RT0, 2, 512), view(PR0, 2, T), view(PT0, 2, T)
    glu, cv, fm = view(GLU0, 2, GW), view(CV0, 2, CW), view(FM0, 2, T)
    lng, lnb, yt = view(LNG0, 256), view(LNG0 + 256, 256), view(YT0, 20, 256)
    uu, vn = view(UU0, 2, T), view(VN0, 10, 256)
    vec_tmp = view(S0, 3, VEC)
    H2, Y2 = view(H20, KD, N), view(Y20, KD, N)
    q2, k2, v2, strip = view(Q20, 2, N), view(K20, 2, N), view(V20, QT, 256), view(STRIP0, 4, N)
    sc, sc1, pt2, ot2 = view(SC0, 2, N), view(SC1, 2, N), view(PT20, QT, P), view(OT20, 2, 256)
    iq, ik, ir = view(IQ0, 4, N), view(IK0, N), view(IR0, 2, N)
    iw, table = small[:, 64:128], small[0:33, 128:140]
    lam_in, neg_lam, subln8, top8 = view(PT20, 4, 64), small[:, 40:41], small[:, 41:42], small[:, 48:56]
    qm, km, vm, mem = view(QM0, KD, N), view(KM0, KD, 256), view(VM0, 2, N), view(MEM0, KD, 256)
    pm, pmt = view(PM0, 4, 256), view(PMT0, 4, 512)
    actv, ub, cb = view(ACT0, 16, N), view(UB0, 4, UW), view(CB0, 4, N)

    def sel(t):
        return view(SEL_AT[t], (t + 1) * P)

    def vec(name, i=0, n=1):
        a = VEC0 + VCOL[name] + i
        return S[:, a:a + n]

    def h_keys(l, c):
        return [(l, "h", c, k) for k in range(KD)]

    def y_keys(l, c):
        return [(l, "attn", t) for t in tiles_of(c)] + [(l, "y", k, c) for k in range(2, 8)]

    def tiles_of(c):
        return range(CHUNKS[c][0] // P, (CHUNKS[c][0] + CHUNKS[c][1]) // P)

    def tensor_program(raw):
        e = Engine(steps, "tensor_done", raw)
        mm, transpose = nc.tensor.matmul, nc.tensor.transpose

        def sums(key, rhs_of, nk, width, reader, after):
            ps = psum.take(e, key, reader)
            for k in range(nk):
                for needed in after(k):
                    e.wait_ge(*at(needed))
                mm(ps[:, 0:width], ones, rhs_of(k), start=(k == 0), stop=(k == nk - 1)).then_inc(*e.step((key, "read", k)))

        def norm_sums(tag, chunks, nk=KD):
            for c in chunks:
                tn = CHUNKS[c][1]
                sums((tag, "ms", c), lambda k: sq[:, k % 2, 0:tn], nk, tn, (tag, "ln", c), lambda k: [(tag, "sq", c, k)])

        def linear(key, name, index, src, nk, chunks, reader, after):
            w = ring.take(e, name, index, nk * P, (key, len(chunks) - 1, "mm")).rearrange("p (k m) -> p k m", m=P)
            for c, (t0, tn) in enumerate(chunks):
                for needed in after(c):
                    e.wait_ge(*at(needed))
                ps = psum.take(e, (key, c), reader(c))
                for k in range(nk):
                    ins = mm(ps[:, 0:tn], w[:, k, :], src(k, t0, tn), start=(k == 0), stop=(k == nk - 1))
                ins.then_inc(*e.step((key, c, "mm")))

        def ada(l, m):
            w = ring.take(e, f"w_ada{l}", m, 1024, (l, "ada", m)).rearrange("p (k m) -> p k m", m=P)
            ps = psum.take(e, (l, "ada ps", m), (l, "ada ev", m))
            for k in range(KD):
                ins = mm(ps[:, 0:2], w[:, k, :], silu_c[:, k, :], start=(k == 0), stop=(k == KD - 1))
            ins.then_inc(*e.step((l, "ada", m)))

        def project(l, h):
            wq, wk = mla_weights
            for c, (t0, tn) in enumerate(own_chunks(l)):
                e.wait_ge(*at((l, "cq", c, 0)))
                e.wait_ge(*at((l, "cq", c, 1)))
                readers = [(l, "qh", h, c, "ev")] + ([(l, "qh", h, c, "sin")] if c < 2 else [])
                ps = psum.take(e, (l, "qh", h, c, "ps"), readers)
                for k in range(2):
                    ins = mm(ps[:, 0:tn], wq[:, k, h, :], mq[:, k, t0:t0 + tn], start=(k == 0), stop=(k == 1))
                ins.then_inc(*e.step((l, "qh", h, c)))
            for c, (t0, tn) in enumerate(CHUNKS):
                e.wait_ge(*at((l, "ckv", c, 0)))
                ps = psum.take(e, (l, "kh", h, c, "ps"), (l, "kh", h, c, "ev"))
                mm(ps[0:64, 0:tn], wk[:, h * 64:(h + 1) * 64], mkv[:, t0:t0 + tn], start=True, stop=True).then_inc(*e.step((l, "kh", h, c)))

        def scores(l, u, h, t):
            keys0, nk = (0, T) if t < QT else (N, L)
            c = c_of(t)
            for i in range(3):
                e.wait_ge(*at((l, "kh", h, i, "ev")))
            for i in range(3):
                for j in range(2):
                    e.wait_ge(*at((l, "kr", i, j)))
            e.wait_ge(*at((l, "qh", h, c, "ev")))
            if c < 2:
                e.wait_ge(*at((l, "qh", h, c, "rope")))
            ps = psum.take(e, (l, "s", u), (l, "exp", u), (nk + 511) // 512)
            for b in range(0, nk, 512):
                w = min(512, nk - b)
                ins = mm(ps[:, b:b + w], qh[0:96, h % 2, t * P:(t + 1) * P], kh[0:96, h % 2, keys0 + b:keys0 + b + w],
                         start=True, stop=True)
            ins.then_inc(*e.step((l, "scores", u)))

        def turn(l, u, h, t):
            first, n = (0, 10) if t < QT else (QT, 2)
            e.wait_ge(*at((l, "exp", u)))
            for g in range(0, n, 4):
                ps = psum.take(e, (l, "pT", u, g), (l, "pT ev", u, g))
                for j in range(g, min(g + 4, n)):
                    ins = transpose(ps[:, (j - g) * P:(j - g + 1) * P], prob[:, u % 2, j * P:(j + 1) * P], ident)
                ins.then_inc(*e.step((l, "turned", u, g)))
            ps = psum.take(e, (l, "o", u), (l, "o ev", u))
            for j in range(n):
                e.wait_ge(*at((l, "v ev", first + j)))
                e.wait_ge(*at((l, "pT ev", u, j // 4 * 4)))
                ins = mm(ps[:, 0:64], pt[:, u % 2, j * P:(j + 1) * P], mv[:, first + j, h * 64:(h + 1) * 64],
                         start=(j == 0), stop=(j == n - 1))
            ins.then_inc(*e.step((l, "pv", u)))

        mla_weights = []

        def attention(l):
            us = units(l)
            w = ring.take(e, f"w_ukv{l}", 1, 256, (l, "v", 9))
            for t in range(10):
                e.wait_ge(*at((l, "ckv", c_of(t), 0)))
                ps = psum.take(e, (l, "v ps", t), (l, "v ev", t))
                mm(ps[:, 0:256], mkv[:, t * P:(t + 1) * P], w, start=True, stop=True).then_inc(*e.step((l, "v", t)))
            last = len(own_chunks(l)) - 1
            wq = ring.take(e, f"w_uq{l}", 0, 1024, (l, "qh", 3, last)).rearrange("p (k h m) -> p k h m", k=2, h=4)
            wk = ring.take(e, f"w_ukv{l}", 0, 256, (l, "kh", 3, 2))
            mla_weights[:] = [wq, wk]
            project(l, 0)
            for u, (h, t) in enumerate(us):
                scores(l, u, h, t)
                if u >= 1:
                    turn(l, u - 1, *us[u - 1])
                if t == 0 and h + 1 < HEADS:
                    project(l, h + 1)
            turn(l, len(us) - 1, *us[-1])
            for t in range(QT + (CT if l == 0 else 0)):
                e.wait_ge(*at((l, "o ev", us.index((HEADS - 1, t)))))
                ps = psum.take(e, (l, "aT", t), (l, "attn", t))
                for b in range(2):
                    ins = transpose(ps[:, b * P:(b + 1) * P], ao[:, t, b * P:(b + 1) * P], ident)
                ins.then_inc(*e.step((l, "aT mm", t)))

        def first_block(l):
            own = own_chunks(l)
            oc = range(len(own))
            nt = 10 if l == 0 else 8

            def w_in(b, key, chunks=own, readers=None):
                linear((l, key), f"w_in{l}", b, lambda k, t0, tn: H[:, k, t0:t0 + tn], KD, chunks,
                       readers or (lambda c: (l, key, "ev", c)), lambda c: h_keys(l, c))

            norm_sums((l, "n"), range(3))
            w_in(0, "q0")
            w_in(1, "q1")
            w_in(2, "kv", CHUNKS)
            w_in(3, "rope", CHUNKS, lambda c: (l, "rope", "ev", c) if c < 2 else (l, "kr", 2, 1))
            w_in(10, "g0")
            w_in(11, "g1")
            norm_sums((l, "qn"), oc, 2)
            norm_sums((l, "kn"), range(3), 1)
            attention(l)
            for i, key in enumerate(("s0", "a0", "s1", "a1", "f0", "f1")):
                w_in(4 + i, key)
            for g in range(2, 8):
                w_in(10 + g, f"g{g}")
                if l == 0:
                    for m in range(4 * (g - 2), 4 * (g - 1)):
                        ada(1, m)
            for c in oc:
                tn = CHUNKS[c][1]
                sums((l, "cmu", c), lambda k: cv[:, k, ccol(c):ccol(c) + tn], 2, tn, (l, "centre", c, 1),
                     lambda k: [(l, "conv", k)])
            norm_sums((l, "cn"), oc, 2)
            for t in range(nt):
                ps = psum.take(e, (l, "ft", t), (l, "yt", t))
                for b in range(2):
                    e.wait_ge(*at((l, f"f{b}", "ev", c_of(t))))
                    ins = mm(ps[:, b * 256:(b + 1) * 256], fm[:, b, t * P:(t + 1) * P], cd, start=True, stop=True)
                ins.then_inc(*e.step((l, "ft mm", t)))
            for b in range(2):
                linear((l, "pw", b), f"w_pw{l}", b, lambda k, t0, tn: cv[:, k, ccol(c_of(t0 // P)):ccol(c_of(t0 // P)) + tn],
                       2, own, lambda c: (l, "y", 2 + b, c), lambda c: [(l, "csilu", k, c) for k in range(2)])
            for c, (t0, tn) in enumerate(own):
                first, n = (0, 8) if c < 2 else (8, 2)
                out = [psum.take(e, (l, "mix", c, b), (l, "mix ev", c, b)) for b in range(2)]
                for t in range(n):
                    w = ring.take(e, "dft" if c < 2 else "dft_ctx", c * 8 + t if c < 2 else t, 2 * tn,
                                  (l, "mix mm", c, t))
                    e.wait_ge(*at((l, "yt", first + t)))
                    for b in range(2):
                        for s in range(2):
                            ins = mm(out[b][:, 0:tn], yt[:, 2 * (first + t) + b, s * P:(s + 1) * P],
                                     w[:, s * tn:(s + 1) * tn], start=(t == 0 and s == 0), stop=(t == n - 1 and s == 1))
                    ins.then_inc(*e.step((l, "mix mm", c, t)))
            w_in(18, "u0")
            w_in(19, "u1")
            for b in range(2):
                linear((l, "four", b), f"w_fourier{l}", b, lambda k, t0, tn: fm[:, k, t0:t0 + tn], 2, own,
                       lambda c: (l, "y", 4 + b, c), lambda c: [(l, "mix ev", c, k) for k in range(2)])
            wv = [ring.take(e, f"w_in{l}", 20 + i, 1024, (l, "sv mm", nt - 1)).rearrange("p (k m) -> p k m", m=P)
                  for i in range(2)]
            for t in range(nt):
                ps = psum.take(e, (l, "sv", t), (l, "sv ev", t))
                for i in range(2):
                    for k in range(KD):
                        ins = mm(ps[:, i * P:(i + 1) * P], H[:, k, t * P:(t + 1) * P], wv[i][:, k, :],
                                 start=(k == 0), stop=(k == KD - 1))
                ins.then_inc(*e.step((l, "sv mm", t)))
            ws = ring.take(e, f"w_s{l}", 0, 512, (l, "sg mm", len(own) - 1, 1)).rearrange("p (g i) -> p g i", g=4)
            for c, (t0, tn) in enumerate(own):
                for b in range(2):
                    ps = psum.take(e, (l, "sg", c, b), (l, "sg ev", c, b))
                    for j in range(tn // P):
                        e.wait_ge(*at((l, "vn", t0 // P + j)))
                        for g in range(2):
                            a = (2 * b + g) * 64
                            ins = mm(ps[g * 64:(g + 1) * 64, j * P:(j + 1) * P], vn[:, t0 // P + j, a:a + 64],
                                     ws[:, 2 * b + g, :], start=True, stop=True)
                    ins.then_inc(*e.step((l, "sg mm", c, b)))
            for m in range(8):
                linear((l, "out", m), f"w_out{l}", m, lambda k, t0, tn: Y[:, k, t0:t0 + tn], KD, own,
                       lambda c: (l, "x", m, c), lambda c: y_keys(l, c))

        e.wait_ge(*at("consts"))
        for br in range(3):
            for c, (a, w) in enumerate(VCH):
                oh = ring.take(e, f"bucket{br}", c, w, ("vec mm", br, c), 33)
                ps = psum.take(e, ("vec ps", br, c), ("vec ev", br, c))
                mm(ps[0:4, 0:w], table[:, 4 * br:4 * br + 4], oh, start=True, stop=True).then_inc(*e.step(("vec mm", br, c)))
        e.wait_ge(*at("silu_c"))
        for m in range(24):
            ada(0, m)
        for l in range(LAYERS):
            first_block(l)
        norm_sums("fin1", range(2))
        norm_sums("mix", range(2))

        def from_h2(k, t0, tn):
            return H2[:, k, t0:t0 + tn]

        def w_in2(b, key):
            linear(key, "w_in2", b, from_h2, KD, CHUNKS[:2], lambda c: (key, "ev", c),
                   lambda c: [("mix", "h", c, k) for k in range(KD)])

        for i in range(4):
            w_in2(i, f"iq{i}")
        w_in2(4, "ik")
        w = ring.take(e, "w_iw", 0, 64, ("iw mm", QT - 1)).rearrange("p (k m) -> p k m", m=8)
        ps = psum.take(e, "iw ps", "iw")
        for t in range(QT):
            for k in range(KD):
                ins = mm(ps[:, 8 * t:8 * t + 8], H2[:, k, t * P:(t + 1) * P], w[:, k, :], start=(k == 0), stop=(k == KD - 1))
            ins.then_inc(*e.step(("iw mm", t)))
        for t in range(2, QT):
            n = (t + 1) * P
            for h in range(8):
                a = 64 * (h % 2)
                e.wait_ge(*at((f"iq{h // 2}", "ev", t // 4)))
                e.wait_ge(*at(("ik", "ev", t // 4)))
                e.wait_ge(*at(("ik", "ev", 0)))
                ps = psum.take(e, ("is", t, h), ("relu", t, h), (n + 511) // 512)
                for b in range(0, n, 512):
                    w = min(512, n - b)
                    ins = mm(ps[:, b:b + w], iq[a:a + 64, h // 2, t * P:(t + 1) * P], ik[a:a + 64, b:b + w],
                             start=True, stop=True)
                ins.then_inc(*e.step(("is mm", t, h)))

        def scores2(br, u, t, h):
            n = (t + 1) * P
            maps = 2 if br < 2 else 1
            for m in range(maps):
                f = (h * maps + m) * 64
                a, blk = f % P, f // P
                e.wait_ge(*at((f"q{blk}{br}", "ev", t // 4)))
                e.wait_ge(*at((f"k{blk}{br}", "ev", t // 4)))
                e.wait_ge(*at((f"k{blk}{br}", "ev", 0)))
                ps = psum.take(e, ("s2", br, u, m), ("biased", br, u, m), (n + 511) // 512)
                for b in range(0, n, 512):
                    w = min(512, n - b)
                    ins = mm(ps[:, b:b + w], q2[a:a + 64, blk, t * P:(t + 1) * P], k2[a:a + 64, blk, b:b + w],
                             start=True, stop=True)
                ins.then_inc(*e.step(("s2 mm", br, u, m)))

        def turn2(br, u, t, h):
            dh = 128 if br < 2 else 64
            e.wait_ge(*at(("prob", br, u)))
            for g in range(0, t + 1, 4):
                ps = psum.take(e, ("pT2", br, u, g), ("pT2 ev", br, u, g))
                for j in range(g, min(g + 4, t + 1)):
                    ins = transpose(ps[:, (j - g) * P:(j - g + 1) * P], sc[:, u % 2, j * P:(j + 1) * P], ident)
                ins.then_inc(*e.step(("turned2", br, u, g)))
            ps = psum.take(e, ("o2", br, u), ("o2 ev", br, u))
            for j in range(t + 1):
                e.wait_ge(*at(("v2 ev", br, j)))
                e.wait_ge(*at(("pT2 ev", br, u, j // 4 * 4)))
                ins = mm(ps[:, 0:dh], pt2[:, j, :], v2[:, j, h * dh:(h + 1) * dh], start=(j == 0), stop=(j == t))
            ins.then_inc(*e.step(("pv2", br, u)))

        def back2(br, t):
            e.wait_ge(*at(("o2 ev", br, units2(br).index((t, units2(br)[-1][1])))))
            ps = psum.take(e, ("oT2", br, t), ("y2", br, t))
            for b in range(2):
                ins = transpose(ps[:, b * P:(b + 1) * P], ot2[:, t % 2, b * P:(b + 1) * P], ident)
            ins.then_inc(*e.step(("oT2 mm", br, t)))

        for br in range(4):
            for i in range(4):
                w_in2(5 + 6 * br + i, f"{'qk'[i // 2]}{i % 2}{br}")
            wv = [ring.take(e, "w_in2", 9 + 6 * br + i, 1024, ("v2 mm", br, QT - 1)).rearrange("p (k m) -> p k m", m=P)
                  for i in range(2)]
            for t in range(QT):
                ps = psum.take(e, ("v2 ps", br, t), ("v2 ev", br, t))
                for i in range(2):
                    for k in range(KD):
                        ins = mm(ps[:, i * P:(i + 1) * P], H2[:, k, t * P:(t + 1) * P], wv[i][:, k, :],
                                 start=(k == 0), stop=(k == KD - 1))
                ins.then_inc(*e.step(("v2 mm", br, t)))
            us = units2(br)
            for u, (t, h) in enumerate(us):
                scores2(br, u, t, h)
                if u >= 2 and us[u - 2][1] == us[-1][1]:
                    back2(br, us[u - 2][0])
                if u >= 1:
                    turn2(br, u - 1, *us[u - 1])
            turn2(br, len(us) - 1, *us[-1])
            back2(br, QT - 1)
        for m in range(8):
            linear(("out2", m), "w_out2", m, lambda k, t0, tn: Y2[:, k, t0:t0 + tn], KD, CHUNKS[:2],
                   lambda c: ("x2", m, c), lambda c: [("y2", br, t) for br in range(4) for t in tiles_of(c)])
        sums(("memn", "ms", 0), lambda k: sq[:, k % 2, 0:L], KD, L, ("memn", "ln", 0), lambda k: [("memn", "sq", 0, k)])
        for m in range(8):
            linear(("km", m), "w_mkv", m, lambda k, t0, tn: mem[:, k, t0:t0 + tn], KD, ((0, L),),
                   lambda c: ("km ev", m), lambda c: [("memn", "h", 0, k) for k in range(KD)])
        for m in range(8):
            w = ring.take(e, "w_mkv", 8 + m, 1024, ("vm mm", m)).rearrange("p (k m) -> p k m", m=P)
            ps = psum.take(e, ("vm ps", m), ("vm ev", m))
            for t in range(2):
                for k in range(KD):
                    ins = mm(ps[:, t * P:(t + 1) * P], mem[:, k, t * P:(t + 1) * P], w[:, k, :],
                             start=(k == 0), stop=(k == KD - 1))
            ins.then_inc(*e.step(("vm mm", m)))
        norm_sums("memq", range(2))
        for m in range(8):
            linear(("qm", m), "w_mq", m, from_h2, KD, CHUNKS[:2], lambda c: ("qm ev", m, c),
                   lambda c: [("memq", "h", c, k) for k in range(KD)])

        def mem_turn(h, t):
            e.wait_ge(*at(("mprob", h, t)))
            ps = psum.take(e, ("mT", h, t), ("mT ev", h, t))
            for j in range(2):
                ins = transpose(ps[:, j * P:(j + 1) * P], pm[:, t % 4, j * P:(j + 1) * P], ident)
            ins.then_inc(*e.step(("mT mm", h, t)))
            if t % 4 == 3:
                c = t // 4
                for b in range(2):
                    ps = psum.take(e, ("mo", h, c, b), ("mo ev", h, c, b))
                    for i in range(4):
                        e.wait_ge(*at(("mT ev", h, 4 * c + i)))
                    e.wait_ge(*at(("vm ev", 2 * h + b)))
                    for j in range(2):
                        ins = mm(ps[:, 0:512], vm[:, j, (2 * h + b) * P:(2 * h + b + 1) * P], pmt[:, 2 * c + j, :],
                                 start=(j == 0), stop=(j == 1))
                    ins.then_inc(*e.step(("mo mm", h, c, b)))

        us = [(h, t) for h in range(4) for t in range(QT)]
        for u, (h, t) in enumerate(us):
            for i in range(2):
                e.wait_ge(*at(("km ev", 2 * h + i)))
            for i in range(2):
                e.wait_ge(*at(("qm ev", 2 * h + i, t // 4)))
            ps = psum.take(e, ("ms", h, t), ("mexp", h, t))
            for i in range(2):
                ins = mm(ps[:, 0:L], qm[:, 2 * h + i, t * P:(t + 1) * P], km[:, 2 * h + i, :], start=(i == 0), stop=(i == 1))
            ins.then_inc(*e.step(("ms mm", h, t)))
            if u >= 2:
                mem_turn(*us[u - 2])
        mem_turn(*us[-2])
        mem_turn(*us[-1])
        for m in range(8):
            linear(("mo2", m), "w_mo", m, lambda k, t0, tn: Y2[:, k, t0:t0 + tn], KD, CHUNKS[:2],
                   lambda c: ("x3", m, c), lambda c: [("mo ev", h, c, b) for h in range(4) for b in range(2)])
        norm_sums("ffn", range(2))

        def down(g):
            f0, fn = FGROUPS[g]
            for m in range(8):
                linear(("down", g, m), "w_down", 8 * g + m, lambda k, t0, tn: actv[:, 8 * (g % 2) + k, t0:t0 + tn], fn,
                       CHUNKS[:2], lambda c: ("x4", g, m, c), lambda c: [("act", f0 + k) for k in range(fn)])

        for g, (f0, fn) in enumerate(FGROUPS):
            for f in range(f0, f0 + fn):
                for s in range(2):
                    linear(("up", f, s), "w_up", 2 * f + s, from_h2, KD, CHUNKS[:2], lambda c: ("up ev", f, s, c),
                           lambda c: [("ffn", "h", c, k) for k in range(KD)])
            if g >= 1:
                down(g - 1)
        down(len(FGROUPS) - 1)
        norm_sums("fin2", range(2))

    def scalar_program(raw):
        e = Engine(steps, "scalar_done", raw)
        act = nc.scalar.activation
        rr_read = {}
        sq_read = {}

        def copy(out, in_, scale=1.0, func=ACT.Copy):
            return act(out, in_, func, scale=scale)

        def norm(tag, chunks, src, nk, after, eps=eps_rms, bias=0.0, spans=CHUNKS):
            for c in chunks:
                t0, tn = spans[c]
                for k in range(nk):
                    for needed in after(c, k):
                        e.wait_ge(*at(needed))
                    e.wait_ge(*at(sq_read.get(k % 2)))
                    act(sq[:, k % 2, 0:tn], src(k, t0, tn), ACT.Square).then_inc(*e.step((tag, "sq", c, k)))
                    sq_read[k % 2] = ((tag, "ms", c), "read", k)
                e.wait_ge(*at(((tag, "ms", c), "read", nk - 1)))
                for needed in rr_read.get(c, []):
                    e.wait_ge(*at(needed))
                r = rr[:, CHUNKS[c][0]:CHUNKS[c][0] + tn]
                act(r, psum.at((tag, "ms", c))[:, 0:tn], ACT.Ln, bias=eps,
                             scale=1.0 / (nk * P)).then_inc(*e.step((tag, "ln", c)))
                e.wait_ge(*at((tag, "ln", c)))
                act(r, r, ACT.Exp, bias=bias, scale=-0.5).then_inc(*e.step((tag, "rr", c)))
                rr_read[c] = [(tag, "used", c, k) for k in range(nk)]

        def ada(l, m):
            e.wait_ge(*at((l, "ada", m)))
            act(mod[:, 24 * l + m, :], psum.at((l, "ada ps", m))[:, 0:2], ACT.Identity, bias=vec(("b_ada", l), m)).then_inc(*e.step((l, "ada ev", m)))

        def evict(key, b, out, chunks, func=ACT.Copy, free=()):
            for c, (t0, tn) in enumerate(chunks):
                e.wait_ge(*at((key, c, "mm")))
                for needed in free:
                    e.wait_ge(*at(needed))
                copy(out(b, c, t0, tn), psum.at((key, c))[:, 0:tn], func=func).then_inc(*e.step((*key, "ev", c) if isinstance(key, tuple) else (key, "ev", c)))

        def project(l, h):
            free = [(l, "scores", len([x for x in units(l) if x[0] <= h - 2]) - 1)] if h >= 2 else []
            for c, (t0, tn) in enumerate(own_chunks(l)):
                r = 64 if c < 2 else 96
                e.wait_ge(*at((l, "qh", h, c)))
                for needed in free:
                    e.wait_ge(*at(needed))
                copy(qh[0:r, h % 2, t0:t0 + tn], psum.at((l, "qh", h, c, "ps"))[0:r, 0:tn]).then_inc(*e.step((l, "qh", h, c, "ev")))
            for c, (t0, tn) in enumerate(CHUNKS):
                e.wait_ge(*at((l, "kh", h, c)))
                copy(kh[0:64, h % 2, t0:t0 + tn], psum.at((l, "kh", h, c, "ps"))[0:64, 0:tn]).then_inc(*e.step((l, "kh", h, c, "ev")))

        def turn(l, u, h, t):
            n = 10 if t < QT else 2
            for g in range(4, n, 4):
                w = min(4, n - g) * P
                e.wait_ge(*at((l, "turned", u, g)))
                if u >= 2:
                    e.wait_ge(*at((l, "pv", u - 2)))
                copy(pt[:, u % 2, g * P:g * P + w], psum.at((l, "pT", u, g))[:, 0:w]).then_inc(*e.step((l, "pT ev", u, g)))

        def attention(l):
            us = units(l)
            for t in range(10):
                e.wait_ge(*at((l, "v", t)))
                copy(mv[:, t, :], psum.at((l, "v ps", t))[:, 0:256]).then_inc(*e.step((l, "v ev", t)))
            project(l, 0)
            for u, (h, t) in enumerate(us):
                nk, s = (T if t < QT else L), 8 * (u % 4)
                e.wait_ge(*at((l, "max", u)))
                if u >= 2:
                    pt_n = 10 if us[u - 2][1] < QT else 2
                    e.wait_ge(*at((l, "turned", u - 2, (pt_n - 1) // 4 * 4)))
                if u >= 4:
                    e.wait_ge(*at((l, "o ev", u - 4)))
                act(prob[:, u % 2, 0:nk], psum.at((l, "s", u))[:, 0:nk], ACT.Exp, bias=small[:, s:s + 1],
                           accum_out=small[:, s + 1:s + 2]).then_inc(*e.step((l, "exp", u)))
                if u >= 1:
                    turn(l, u - 1, *us[u - 1])
                if t == 0 and h + 1 < HEADS:
                    project(l, h + 1)
            turn(l, len(us) - 1, *us[-1])

        def first_block(l):
            own = own_chunks(l)
            oc = range(len(own))
            nt = 10 if l == 0 else 8
            if l:
                for m in range(8):
                    for c in range(3):
                        e.wait_ge(*at((l - 1, "x", m, c)))
            raw.dma_start(cs[64:128, :], A["rope"]).then_inc(*loads("rope_loaded", (l, "cs")))
            norm((l, "n"), range(3), lambda k, t0, tn: X[:, k, t0:t0 + tn], KD,
                 lambda c, k: [(l - 1, "x", k, min(c, 2))] if l else ["consts"])
            for c, (t0, tn) in enumerate(CHUNKS):
                for k in range(KD):
                    e.wait_ge(*at(((l, "n"), "h", c, k)))
                    act(H[:, k, t0:t0 + tn], H[:, k, t0:t0 + tn], ACT.Identity,
                               bias=mod[:, 24 * l + k, c // 2:c // 2 + 1]).then_inc(*e.step((l, "h", c, k)))
            free = [("vec stored", br) for br in range(3)] if l == 0 else []
            evict((l, "q0"), 0, lambda b, c, t0, tn: mq[:, 0, t0:t0 + tn], own, free=free)
            evict((l, "q1"), 1, lambda b, c, t0, tn: mq[:, 1, t0:t0 + tn], own)
            evict((l, "kv"), 0, lambda b, c, t0, tn: mkv[:, t0:t0 + tn], CHUNKS)
            e.wait_ge(*at(((l, "rope"), 2, "mm")))
            for j in range(2):
                copy(kh[64:96, j, N:T], psum.at(((l, "rope"), 2))[64:96, 0:L]).then_inc(*e.step((l, "kr", 2, j)))
            for g in range(2):
                evict((l, f"g{g}"), g, lambda b, c, t0, tn: Y[:, b, t0:t0 + tn], own, ACT.Silu)
            norm((l, "qn"), oc, lambda k, t0, tn: mq[:, k, t0:t0 + tn], 2, lambda c, k: [(l, f"q{k}", "ev", c)],
                 bias=ln_scale)
            norm((l, "kn"), range(3), lambda k, t0, tn: mkv[:, t0:t0 + tn], 1, lambda c, k: [(l, "kv", "ev", c)])
            attention(l)
            e.wait_ge(*at((l, "qh", 3, 1, "sin")))
            if l:
                e.wait_ge(*at((l - 1, "y", 7, len(own_chunks(l - 1)) - 1)))
            e.wait_ge(*at((l, "aT mm", QT + (1 if l == 0 else -1))))
            for out, name in ((lng, "sgu_g"), (lnb, "sgu_b")):
                raw.dma_start(out, A[name][l:l + 1, :].to_broadcast((P, 256))).then_inc(*loads("gate_bias_loaded", None))
            for b in range(2):
                for g in range(2):
                    raw.dma_start(bsb[64 * g:64 * g + 64, b, :],
                                             A["b_s"][4 * l + 2 * b + g:4 * l + 2 * b + g + 1, :].to_broadcast((64, P))).then_inc(*loads("gate_bias_loaded", (l, "gate vectors") if b and g else None))
            for i in range(2):
                evict((l, f"s{i}"), i, lambda b, c, t0, tn: glu[:, b, gcol(c):gcol(c) + tn], own, ACT.Sigmoid)
            for i in range(2):
                evict((l, f"f{i}"), i, lambda b, c, t0, tn: fm[:, b, t0:t0 + tn], own)
            for g in range(2, 8):
                evict((l, f"g{g}"), g, lambda b, c, t0, tn: Y[:, b, t0:t0 + tn], own, ACT.Silu)
                if l == 0:
                    for m in range(4 * (g - 2), 4 * (g - 1)):
                        ada(1, m)
            norm((l, "cn"), oc, lambda k, t0, tn: cv[:, k, t0:t0 + tn], 2, lambda c, k: [(l, "centre", c, k)], eps_ln,
                 spans=tuple((ccol(c), CHUNKS[c][1]) for c in range(3)))
            for t in range(nt):
                e.wait_ge(*at((l, "ft mm", t)))
                copy(yt[:, 2 * t:2 * t + 2, :], psum.at((l, "ft", t))[:, 0:512].rearrange("p (a b) -> p a b", b=256)).then_inc(*e.step((l, "yt", t)))
            for c, (t0, tn) in enumerate(own):
                for k in range(2):
                    v = cv[:, k, ccol(c):ccol(c) + tn]
                    e.wait_ge(*at(((l, "cn"), "h", c, k)))
                    act(v, v, ACT.Silu, bias=vec(("conv_ln_b", l), k)).then_inc(*e.step((l, "csilu", k, c)))
            for c, (t0, tn) in enumerate(own):
                n = 8 if c < 2 else 2
                for b in range(2):
                    e.wait_ge(*at((l, "mix mm", c, n - 1)))
                    copy(fm[:, b, t0:t0 + tn], psum.at((l, "mix", c, b))[:, 0:tn]).then_inc(*e.step((l, "mix ev", c, b)))
            for t in range(nt):
                s = 140 + 16 * (t % 4)
                e.wait_ge(*at((l, "sv stats", t)))
                act(small[:, s + 8:s + 9], small[:, s + 7:s + 8], ACT.Ln, bias=eps_ln).then_inc(*e.step((l, "sv ln", t)))
                e.wait_ge(*at((l, "sv ln", t)))
                act(small[:, s + 8:s + 9], small[:, s + 8:s + 9], ACT.Exp, scale=-0.5).then_inc(*e.step((l, "sv rstd", t)))

        e.wait_ge(*at("consts"))
        e.wait_ge(*at("small"))
        for br in range(3):
            for c, (a, w) in enumerate(VCH):
                e.wait_ge(*at(("vec mm", br, c)))
                copy(vec_tmp[0:4, br, a:a + w], psum.at(("vec ps", br, c))[0:4, 0:w]).then_inc(*e.step(("vec ev", br, c)))
            for c in range(3):
                e.wait_ge(*at(("vec ev", br, c)))
            raw.dma_start(vec_dram[4 * br:4 * br + 4, :], vec_tmp[0:4, br, :]).then_inc(*loads("vec_stored", ("vec stored", br)))
        for br in range(3):
            e.wait_ge(*at(("vec stored", br)))
        src = bass.AP(tensor=vec_dram.tensor, offset=0, ap=[[VEC, 12], [0, P], [1, VEC]])
        raw.dma_start(rows_dram, src).then_inc(*loads("rows_stored", "rows stored"))
        act(silu_c, vec("c", 0, 16).rearrange("p (a b) -> p a b", b=2), ACT.Silu).then_inc(*e.step("silu_c"))
        for m in range(24):
            ada(0, m)
        for l in range(LAYERS):
            first_block(l)
        for m in range(8):
            e.wait_ge(*at(((1, "out", m), 0, "mm")))
        for c in range(2):
            e.wait_ge(*at((1, "x", 7, c)))
        raw.dma_start(lam_in, A["lam"].to_broadcast((P, 256)).rearrange("p (a b) -> p a b", b=64)).then_inc(*loads("lambda_loaded", "lam in"))
        norm("fin1", range(2), lambda k, t0, tn: X[:, k, t0:t0 + tn], KD, lambda c, k: [(1, "x", k, c)])
        norm("mix", range(2), lambda k, t0, tn: X[:, k, t0:t0 + tn], KD, lambda c, k: [("fin1", "h", c, k)])
        e.wait_ge(*at("lam sums"))
        act(small[:, 44:46], small[:, 42:44], ACT.Exp).then_inc(*e.step("lam exp"))
        for i in range(4):
            for c in range(2):
                t0, tn = CHUNKS[c]
                e.wait_ge(*at((f"iq{i}", c, "mm")))
                copy(iq[:, i, t0:t0 + tn], psum.at((f"iq{i}", c))[:, 0:tn]).then_inc(*e.step((f"iq{i}", "ev", c)))
        for c in range(2):
            t0, tn = CHUNKS[c]
            e.wait_ge(*at(("ik", c, "mm")))
            copy(ik[:, t0:t0 + tn], psum.at(("ik", c))[:, 0:tn]).then_inc(*e.step(("ik", "ev", c)))
        e.wait_ge(*at(("iw mm", QT - 1)))
        copy(iw, psum.at("iw ps")[:, 0:64], scale=8 ** -0.5).then_inc(*e.step("iw"))
        for t in range(2, QT):
            n = (t + 1) * P
            for h in range(8):
                i = 8 * (t - 2) + h
                e.wait_ge(*at(("is mm", t, h)))
                if i >= 2:
                    e.wait_ge(*at(("weighted", i - 2)))
                copy(ir[:, i % 2, 0:n], psum.at(("is", t, h))[:, 0:n], scale=0.125, func=ACT.Relu).then_inc(*e.step(("relu", t, h)))
        e.wait_ge(*at(("weighted", 47)))
        for br in range(4):
            us = units2(br)
            maps = 2 if br < 2 else 1
            hs = us[-1][1] + 1
            h0 = (0, 2, 4, 8)[br]
            if br:
                for m in range(2 if br < 3 else 1):
                    e.wait_ge(*at(("biased", br - 1, len(units2(br - 1)) - 1, m)))
            e.wait_ge(*at("rows stored"))
            src = bass.AP(tensor=rows_dram.tensor, offset=h0 * P * VEC + P - 1, ap=[[VEC - 1, P], [P * VEC, hs], [1, N]])
            raw.dma_start(strip[:, 0:hs, :], src).then_inc(*loads("strips_loaded", ("strip", br)))
            for i in range(4):
                key = f"{'qk'[i // 2]}{i % 2}{br}"
                for c in range(2):
                    t0, tn = CHUNKS[c]
                    e.wait_ge(*at((key, c, "mm")))
                    copy((q2, k2)[i // 2][:, i % 2, t0:t0 + tn], psum.at((key, c))[:, 0:tn]).then_inc(*e.step((key, "ev", c)))
            for t in range(QT):
                e.wait_ge(*at(("v2 mm", br, t)))
                copy(v2[:, t, :], psum.at(("v2 ps", br, t))[:, 0:256]).then_inc(*e.step(("v2 ev", br, t)))

            def post(u, t, h):
                for g in range(4, t + 1, 4):
                    w = min(4, t + 1 - g) * P
                    e.wait_ge(*at(("turned2", br, u, g)))
                    if u >= 1:
                        e.wait_ge(*at(("pv2", br, u - 1)))
                    copy(pt2[:, g:g + w // P, :], psum.at(("pT2", br, u, g))[:, 0:w].rearrange("p (a b) -> p a b", b=P)).then_inc(*e.step(("pT2 ev", br, u, g)))
                if br < 2:
                    s = 8 * (u % 4) + 6
                    e.wait_ge(*at(("pv2", br, u)))
                    act(sq[:, 0, 0:P], psum.at(("o2", br, u))[:, 0:P], ACT.Square, accum_out=small[:, s:s + 1]).then_inc(*e.step(("o2 sq", br, u)))
                    e.wait_ge(*at(("o2 sq", br, u)))
                    act(small[:, s + 1:s + 2], small[:, s:s + 1], ACT.Ln, bias=eps_rms, scale=1.0 / P).then_inc(*e.step(("o2 ln", br, u)))
                    e.wait_ge(*at(("o2 ln", br, u)))
                    act(small[:, s + 1:s + 2], small[:, s + 1:s + 2], ACT.Exp, scale=-0.5).then_inc(*e.step(("o2 rstd", br, u)))

            def back(t):
                e.wait_ge(*at(("oT2 mm", br, t)))
                e.wait_ge(*at("subln8"))
                out = Y2[:, 2 * br:2 * br + 2, t * P:(t + 1) * P]
                in_ = psum.at(("oT2", br, t))[:, 0:256].rearrange("p (a b) -> p a b", b=P)
                if br < 2:
                    act(out, in_, ACT.Copy, scale=subln8).then_inc(*e.step(("y2", br, t)))
                else:
                    copy(out, in_).then_inc(*e.step(("y2", br, t)))

            for u, (t, h) in enumerate(us):
                n = (t + 1) * P
                for m in range(maps):
                    s = 8 * (u % 4) + 3 * m
                    buf = (sc, sc1)[m][:, u % 2, 0:n]
                    e.wait_ge(*at(("max2", br, u, m)))
                    if u >= 4:
                        e.wait_ge(*at(("o2 ev", br, u - 4)))
                    key = ("prob", br, u) if br >= 2 else ("exp2", br, u, m)
                    act(buf, buf, ACT.Exp, bias=small[:, s:s + 1], accum_out=small[:, s + 1:s + 2]).then_inc(*e.step(key))
                if u >= 2 and us[u - 2][1] == us[-1][1]:
                    back(us[u - 2][0])
                if u >= 1:
                    post(u - 1, *us[u - 1])
            post(len(us) - 1, *us[-1])
            back(QT - 1)
        for u in (len(units2(3)) - 1,):
            e.wait_ge(*at(("biased", 3, u, 0)))
        e.wait_ge(*at(("o2 ev", 3, len(units2(3)) - 1)))
        e.wait_ge(*at(("y2", 3, QT - 1)))
        e.wait_ge(*at(("oT2 mm", 3, QT - 1)))
        raw.dma_start(mem, A["mem"]).then_inc(*loads("mem_loaded", "mem"))
        norm("memn", (0,), lambda k, t0, tn: mem[:, k, 0:L], KD, lambda c, k: ["mem"], spans=((0, L),))
        for m in range(8):
            e.wait_ge(*at((("km", m), 0, "mm")))
            copy(km[:, m, :], psum.at((("km", m), 0))[:, 0:L]).then_inc(*e.step(("km ev", m)))
        for m in range(8):
            e.wait_ge(*at(("vm mm", m)))
            copy(vm[:, :, m * P:(m + 1) * P], psum.at(("vm ps", m))[:, 0:256].rearrange("p (a b) -> p a b", b=P)).then_inc(*e.step(("vm ev", m)))
        norm("memq", range(2), lambda k, t0, tn: X[:, k, t0:t0 + tn], KD, lambda c, k: [("x2", k, c)])
        for m in range(8):
            for c, (t0, tn) in enumerate(CHUNKS[:2]):
                e.wait_ge(*at((("qm", m), c, "mm")))
                copy(qm[:, m, t0:t0 + tn], psum.at((("qm", m), c))[:, 0:tn], scale=1.0 / 16).then_inc(*e.step(("qm ev", m, c)))

        def mem_post(h, t):
            if t % 4 == 3:
                c = t // 4
                for b in range(2):
                    e.wait_ge(*at(("mo mm", h, c, b)))
                    copy(Y2[:, 2 * h + b, 512 * c:512 * c + 512], psum.at(("mo", h, c, b))[:, 0:512]).then_inc(*e.step(("mo ev", h, c, b)))

        us = [(h, t) for h in range(4) for t in range(QT)]
        for u, (h, t) in enumerate(us):
            s = 8 * (u % 4)
            e.wait_ge(*at(("mmax", h, t)))
            if u >= 4:
                e.wait_ge(*at(("mT mm", *us[u - 4])))
            act(pm[:, t % 4, :], psum.at(("ms", h, t))[:, 0:L], ACT.Exp, bias=small[:, s:s + 1],
                       accum_out=small[:, s + 1:s + 2]).then_inc(*e.step(("mexp", h, t)))
            if u >= 3:
                mem_post(*us[u - 3])
        for v in us[-3:]:
            mem_post(*v)
        norm("ffn", range(2), lambda k, t0, tn: X[:, k, t0:t0 + tn], KD, lambda c, k: [("x3", k, c)])
        for f in range(FF):
            for s in range(2):
                i = 2 * (f % 2) + s
                for c, (t0, tn) in enumerate(CHUNKS[:2]):
                    e.wait_ge(*at((("up", f, s), c, "mm")))
                    e.wait_ge(*at("up pads"))
                    if f >= 2:
                        e.wait_ge(*at(("conv2", f - 2, s)))
                    copy(ub[:, i, 2 + t0:2 + t0 + tn], psum.at((("up", f, s), c))[:, 0:tn]).then_inc(*e.step(("up ev", f, s, c)))
                if s == 0:
                    e.wait_ge(*at(("conv2", f, 0)))
                    act(cb[:, i, :], cb[:, i, :], ACT.Silu).then_inc(*e.step(("ffn gate", f)))
        norm("fin2", range(2), lambda k, t0, tn: X[:, k, t0:t0 + tn], KD,
             lambda c, k: [("x4", len(FGROUPS) - 1, k, c)])

    def vector_program(raw):
        e = Engine(steps, "vector_done", raw)
        v = nc.vector
        stt = v.scalar_tensor_tensor

        def scale_rows(tag, chunks, nk, src, out, gain, spans=CHUNKS):
            for c in chunks:
                t0, tn = spans[c]
                r0 = CHUNKS[c][0]
                e.wait_ge(*at((tag, "rr", c)))
                for k in range(nk):
                    ins = stt(out=out(k, t0, tn), in0=src(k, t0, tn), scalar=gain(k, c), in1=rr[:, r0:r0 + tn],
                              op0=ALU.mult, op1=ALU.mult)
                    ins.then_inc(*e.step((tag, "h", c, k)))
                    steps.at[tag, "used", c, k] = steps.at[tag, "h", c, k]

        def rope_products(ps, c, tn, free, cos_key, sin_key):
            for needed in free:
                e.wait_ge(*at(needed))
            t0 = CHUNKS[c][0]
            v.tensor_tensor(rt[64:96, 0, 0:tn], ps[64:96, 0:tn], cs[64:96, t0:t0 + tn], ALU.mult).then_inc(*e.step(cos_key))
            v.tensor_tensor(rt[64:96, 1, 0:tn], ps[96:128, 0:tn], cs[96:128, t0:t0 + tn], ALU.mult).then_inc(*e.step(sin_key))

        rope_read = [None]

        def project(l, h):
            for c in range(2):
                e.wait_ge(*at((l, "qh", h, c)))
                e.wait_ge(*at((l, "cs")))
                rope_products(psum.at((l, "qh", h, c, "ps")), c, 512, [rope_read[0]], (l, "qh", h, c, "cos"),
                              (l, "qh", h, c, "sin"))
                rope_read[0] = (l, "qh", h, c, "rope")

        def turn(l, u, h, t):
            s = 8 * (u % 4)
            w = (4 if t < QT else 2) * P
            e.wait_ge(*at((l, "turned", u, 0)))
            if u >= 2:
                e.wait_ge(*at((l, "pv", u - 2)))
            v.tensor_copy(pt[:, u % 2, 0:w], psum.at((l, "pT", u, 0))[:, 0:w]).then_inc(*e.step((l, "pT ev", u, 0)))
            e.wait_ge(*at((l, "exp", u)))
            v.reciprocal(small[:, s + 2:s + 3], small[:, s + 1:s + 2]).then_inc(*e.step((l, "recip", u)))
            e.wait_ge(*at((l, "recip", u)))
            e.wait_ge(*at((l, "pv", u)))
            v.tensor_scalar(ao[:, t, h * 64:(h + 1) * 64], psum.at((l, "o", u))[:, 0:64], small[:, s + 2:s + 3],
                                   None, ALU.mult).then_inc(*e.step((l, "o ev", u)))

        def attention(l):
            us = units(l)
            project(l, 0)
            for u, (h, t) in enumerate(us):
                nk, s = (T if t < QT else L), 8 * (u % 4)
                e.wait_ge(*at((l, "scores", u)))
                v.tensor_reduce(small[:, s:s + 1], psum.at((l, "s", u))[:, 0:nk], AX.X, ALU.max, negate=True).then_inc(*e.step((l, "max", u)))
                if u >= 1:
                    turn(l, u - 1, *us[u - 1])
                if t == 0 and h + 1 < HEADS:
                    project(l, h + 1)
            turn(l, len(us) - 1, *us[-1])
            for t in range(QT + (CT if l == 0 else 0)):
                e.wait_ge(*at((l, "aT mm", t)))
                e.wait_ge(*at((l, "g0", "ev", c_of(t))))
                e.wait_ge(*at((l, "g1", "ev", c_of(t))))
                y = Y[:, 0:2, t * P:(t + 1) * P]
                v.tensor_tensor(y, psum.at((l, "aT", t))[:, 0:256].rearrange("p (a b) -> p a b", b=P), y, ALU.mult).then_inc(*e.step((l, "attn", t)))

        def first_block(l):
            own = own_chunks(l)
            oc = range(len(own))
            nt = 10 if l == 0 else 8
            for m in range(24):
                e.wait_ge(*at((l, "ada ev", m)))
            for j in range(2):
                stt(out=am[:, :, j], in0=mod[:, 24 * l + 8:24 * l + 16, j], scalar=1.0,
                             in1=vec(("norm_g", l), 0, 8), op0=ALU.add, op1=ALU.mult).then_inc(*e.step((l, "am", j)))
                e.wait_ge(*at((l, "am", j)))
            scale_rows((l, "n"), range(3), KD, lambda k, t0, tn: X[:, k, t0:t0 + tn],
                       lambda k, t0, tn: H[:, k, t0:t0 + tn], lambda k, c: am[:, k, c // 2:c // 2 + 1])
            for c in range(2):
                e.wait_ge(*at(((l, "rope"), c, "mm")))
                e.wait_ge(*at((l, "cs")))
                rope_products(psum.at(((l, "rope"), c)), c, 512, [rope_read[0]], None, (l, "rope", "ev", c))
                rope_read[0] = (l, "kr", c, 1)
            scale_rows((l, "qn"), oc, 2, lambda k, t0, tn: mq[:, k, t0:t0 + tn], lambda k, t0, tn: mq[:, k, t0:t0 + tn],
                       lambda k, c: vec(("q_norm_g", l), k))
            scale_rows((l, "kn"), range(3), 1, lambda k, t0, tn: mkv[:, t0:t0 + tn], lambda k, t0, tn: mkv[:, t0:t0 + tn],
                       lambda k, c: vec(("kv_norm_g", l)))
            for c in range(3):
                if c < len(own):
                    for k in range(2):
                        steps.at[l, "cq", c, k] = steps.at[(l, "qn"), "h", c, k]
                steps.at[l, "ckv", c, 0] = steps.at[(l, "kn"), "h", c, 0]
            attention(l)
            for i in range(2):
                for c, (t0, tn) in enumerate(own):
                    g = glu[:, i, gcol(c):gcol(c) + tn]
                    e.wait_ge(*at((l, f"s{i}", "ev", c)))
                    e.wait_ge(*at(((l, f"a{i}"), c, "mm")))
                    v.tensor_tensor(g, psum.at(((l, f"a{i}"), c))[:, 0:tn], g, ALU.mult).then_inc(*e.step((l, f"a{i}", "ev", c)))
            wide = CW if l == 0 else N
            e.wait_ge(*at((l, "pads")))
            for i in range(2):
                for c in oc:
                    e.wait_ge(*at((l, f"a{i}", "ev", c)))
            for j in range(TAPS):
                for b in range(2):
                    w = vec(("conv_w", l), b * TAPS + j)
                    out, src = cv[:, b, 0:wide], glu[:, b, j:j + wide]
                    if j == 0:
                        ins = v.tensor_scalar(out, src, w, vec(("conv_b", l), b), ALU.mult, ALU.add)
                    else:
                        e.wait_ge(*at((l, "tap", b, j - 1)))
                        ins = stt(out=out, in0=src, scalar=w, in1=out, op0=ALU.mult, op1=ALU.add)
                    ins.then_inc(*e.step((l, "tap", b, j)))
            for b in range(2):
                steps.at[l, "conv", b] = steps.at[l, "tap", b, TAPS - 1]
            for c, (t0, tn) in enumerate(own):
                e.wait_ge(*at(((l, "cmu", c), "read", 1)))
                for k in range(2):
                    y = cv[:, k, ccol(c):ccol(c) + tn]
                    stt(out=y, in0=psum.at((l, "cmu", c))[:, 0:tn], scalar=-1.0 / 256, in1=y, op0=ALU.mult,
                               op1=ALU.add).then_inc(*e.step((l, "centre", c, k)))
            spans = tuple((ccol(c), CHUNKS[c][1]) for c in range(3))
            scale_rows((l, "cn"), oc, 2, lambda k, t0, tn: cv[:, k, t0:t0 + tn], lambda k, t0, tn: cv[:, k, t0:t0 + tn],
                       lambda k, c: vec(("conv_ln_g", l), k), spans)

            def branch_out(key, block, c, tn, bias):
                t0 = CHUNKS[c][0]
                y = Y[:, block, t0:t0 + tn]
                e.wait_ge(*at((key, c, "mm")))
                e.wait_ge(*at((l, f"g{block}", "ev", c)))
                stt(out=y, in0=psum.at((key, c))[:, 0:tn], scalar=bias, in1=y, op0=ALU.add, op1=ALU.mult).then_inc(*e.step((l, "y", block, c)))

            for b in range(2):
                for c, (t0, tn) in enumerate(own):
                    branch_out((l, "pw", b), 2 + b, c, tn, vec(("b_pw", l), b))
            for b in range(2):
                for c, (t0, tn) in enumerate(own):
                    e.wait_ge(*at(((l, f"u{b}"), c, "mm")))
                    e.wait_ge(*at((l, f"g{6 + b}", "ev", c)))
                    for i in range(2):
                        e.wait_ge(*at(((l, "pw", i), c, "mm")))
                    v.tensor_tensor(uu[:, b, t0:t0 + tn], psum.at(((l, f"u{b}"), c))[:, 0:tn],
                                           Y[:, 6 + b, t0:t0 + tn], ALU.mult).then_inc(*e.step((l, f"u{b}", "ev", c)))
            for b in range(2):
                for c, (t0, tn) in enumerate(own):
                    branch_out((l, "four", b), 4 + b, c, tn, vec(("b_fourier", l), b))

            def normed(t):
                s = 140 + 16 * (t % 4)
                e.wait_ge(*at((l, "sv rstd", t)))
                v.tensor_scalar(vn[:, t, :], psum.at((l, "sv", t))[:, 0:256], small[:, s + 6:s + 7],
                                       small[:, s + 8:s + 9], ALU.subtract, ALU.mult).then_inc(*e.step((l, "sv ev", t)))

            for t in range(nt):
                s = 140 + 16 * (t % 4)
                e.wait_ge(*at((l, "sv mm", t)))
                v.bn_stats(small[:, s:s + 6], psum.at((l, "sv", t))[:, 0:256]).then_inc(*e.step((l, "sv bn", t)))
                e.wait_ge(*at((l, "sv bn", t)))
                v.bn_aggr(small[:, s + 6:s + 8], small[:, s:s + 6]).then_inc(*e.step((l, "sv stats", t)))
                if t >= 1:
                    normed(t - 1)
            normed(nt - 1)
            e.wait_ge(*at((l, "gate vectors")))
            for c, (t0, tn) in enumerate(own):
                for b in range(2):
                    e.wait_ge(*at((l, "sg mm", c, b)))
                    n = tn // P
                    out = Y[:, 6 + b, t0:t0 + tn].rearrange("p (a b) -> p a b", b=P)
                    in0 = psum.at((l, "sg", c, b))[:, 0:tn].rearrange("p (a b) -> p a b", b=P)
                    v.tensor_tensor(out, in0, bsb[:, b:b + 1, :].to_broadcast((P, n, P)), ALU.add).then_inc(*e.step((l, "sg ev", c, b)))
            for m in range(8):
                for c, (t0, tn) in enumerate(own):
                    e.wait_ge(*at(((l, "out", m), c, "mm")))
                    x = X[:, m, t0:t0 + tn]
                    stt(out=x, in0=psum.at(((l, "out", m), c))[:, 0:tn],
                               scalar=mod[:, 24 * l + 16 + m, c // 2:c // 2 + 1], in1=x, op0=ALU.mult, op1=ALU.add).then_inc(*e.step((l, "x", m, c)))

        e.wait_ge(*at("consts"))
        e.wait_ge(*at("small"))
        for l in range(LAYERS):
            first_block(l)

        def x_of(k, t0, tn):
            return X[:, k, t0:t0 + tn]

        def h2_of(k, t0, tn):
            return H2[:, k, t0:t0 + tn]

        scale_rows("fin1", range(2), KD, x_of, x_of, lambda k, c: vec("final_g", k))
        e.wait_ge(*at("lam in"))
        for i in range(2):
            v.tensor_tensor(lam_in[:, 2 * i, :], lam_in[:, 2 * i, :], lam_in[:, 2 * i + 1, :], ALU.mult).then_inc(*e.step(("lam", i)))
            e.wait_ge(*at(("lam", i)))
            v.tensor_reduce(small[:, 42 + i:43 + i], lam_in[:, 2 * i, :], AX.X, ALU.add).then_inc(*e.step("lam sums" if i else None))
        scale_rows("mix", range(2), KD, x_of, h2_of, lambda k, c: vec("norm_mix", k))
        e.wait_ge(*at("lam exp"))
        v.tensor_tensor(neg_lam, small[:, 45:46], small[:, 44:45], ALU.subtract).then_inc(*e.step("lam diff"))
        e.wait_ge(*at("lam diff"))
        v.tensor_scalar(neg_lam, neg_lam, -LAM_INIT, None, ALU.add).then_inc(*e.step("neg lam"))
        e.wait_ge(*at("neg lam"))
        v.tensor_scalar(subln8, vec("subln"), 1.0 - LAM_INIT, None, ALU.mult).then_inc(*e.step("subln8"))
        e.wait_ge(*at("iw"))
        for t in range(2, QT):
            for h in range(8):
                i = 8 * (t - 2) + h
                w, x = iw[:, 8 * t + h:8 * t + h + 1], ir[:, i % 2, 0:(t + 1) * P]
                e.wait_ge(*at(("relu", t, h)))
                if h == 0:
                    ins = v.tensor_scalar(sel(t), x, w, None, ALU.mult)
                else:
                    ins = stt(out=sel(t), in0=x, scalar=w, in1=sel(t), op0=ALU.mult, op1=ALU.add)
                ins.then_inc(*e.step(("weighted", i)))
                e.wait_ge(*at(("weighted", i)))

        def top_k():
            for t in range(2, QT):
                e.wait_ge(*at(("causal", t)))
                for r in range(TOPK // 8):
                    v.max(top8, sel(t)).then_inc(*e.step(("top8", t, r)))
                    e.wait_ge(*at(("top8", t, r)))
                    v.match_replace(sel(t), top8, sel(t), TAKEN).then_inc(*e.step(("taken", t, r)))
                    e.wait_ge(*at(("taken", t, r)))
                    yield
                v.tensor_scalar(sel(t), sel(t), TAKEN / 2, NEG, ALU.is_gt, ALU.mult).then_inc(*e.step(("sel", t)))
                e.wait_ge(*at(("sel", t)))

        rounds = top_k()
        for br in range(4):
            us = units2(br)
            maps = 2 if br < 2 else 1
            dh = 128 if br < 2 else 64
            e.wait_ge(*at(("strip", br)))

            def post(u, t, h):
                w = min(4, t + 1) * P
                s = 8 * (u % 4)
                e.wait_ge(*at(("turned2", br, u, 0)))
                if u >= 1:
                    e.wait_ge(*at(("pv2", br, u - 1)))
                v.tensor_copy(pt2[:, 0:w // P, :], psum.at(("pT2", br, u, 0))[:, 0:w].rearrange(
                    "p (a b) -> p a b", b=P)).then_inc(*e.step(("pT2 ev", br, u, 0)))
                if br < 2:
                    r = small[:, s + 7:s + 8]
                    e.wait_ge(*at(("o2 rstd", br, u)))
                else:
                    r = small[:, s + 2:s + 3]
                    e.wait_ge(*at(("prob", br, u)))
                    v.reciprocal(r, small[:, s + 1:s + 2]).then_inc(*e.step(("recip2", br, u)))
                    e.wait_ge(*at(("recip2", br, u)))
                e.wait_ge(*at(("pv2", br, u)))
                if h == 0 and t >= 2:
                    e.wait_ge(*at(("oT2 mm", br, t - 2)))
                v.tensor_scalar(ot2[:, t % 2, h * dh:(h + 1) * dh], psum.at(("o2", br, u))[:, 0:dh], r, None,
                                       ALU.mult).then_inc(*e.step(("o2 ev", br, u)))

            def combine(u, t):
                n, s = (t + 1) * P, 8 * (u % 4)
                e.wait_ge(*at(("exp2", br, u, 0)))
                e.wait_ge(*at(("exp2", br, u, 1)))
                v.reciprocal(small[:, s + 2:s + 3], small[:, s + 1:s + 2]).then_inc(*e.step(None))
                v.reciprocal(small[:, s + 5:s + 6], small[:, s + 4:s + 5]).then_inc(*e.step(("recips", br, u)))
                e.wait_ge(*at(("recips", br, u)))
                v.tensor_scalar(small[:, s + 5:s + 6], small[:, s + 5:s + 6], neg_lam, None, ALU.mult).then_inc(*e.step(("lam recip", br, u)))
                e.wait_ge(*at(("lam recip", br, u)))
                p1 = sc1[:, u % 2, 0:n]
                v.tensor_scalar(p1, p1, small[:, s + 5:s + 6], None, ALU.mult).then_inc(*e.step(("p1", br, u)))
                e.wait_ge(*at(("p1", br, u)))
                p0 = sc[:, u % 2, 0:n]
                stt(out=p0, in0=p0, scalar=small[:, s + 2:s + 3], in1=p1, op0=ALU.mult, op1=ALU.add).then_inc(*e.step(("prob", br, u)))

            for u, (t, h) in enumerate(us):
                n, s = (t + 1) * P, 8 * (u % 4)
                for m in range(maps):
                    buf = (sc, sc1)[m][:, u % 2, 0:n]
                    e.wait_ge(*at(("s2 mm", br, u, m)))
                    if u >= 2:
                        tp = us[u - 2][0]
                        e.wait_ge(*at(("turned2", br, u - 2, tp // 4 * 4)))
                        e.wait_ge(*at(("prob", br, u - 2)))
                    stt(out=buf, in0=psum.at(("s2", br, u, m))[:, 0:n], scalar=0.125,
                                 in1=strip[:, h, 896 - P * t:896 - P * t + n], op0=ALU.mult, op1=ALU.add).then_inc(*e.step(("biased", br, u, m)))
                    e.wait_ge(*at(("biased", br, u, m)))
                    if br == 3 and t >= 2:
                        e.wait_ge(*at(("sel", t)))
                        v.tensor_tensor(buf, buf, sel(t), ALU.add).then_inc(*e.step(("selected", u)))
                        e.wait_ge(*at(("selected", u)))
                    v.tensor_reduce(small[:, s + 3 * m:s + 3 * m + 1], buf, AX.X, ALU.max, negate=True).then_inc(*e.step(("max2", br, u, m)))
                if br < 2 and u >= 1:
                    combine(u - 1, us[u - 1][0])
                if br < 3:
                    for _ in range(3):
                        next(rounds, None)
                if u >= 1:
                    post(u - 1, *us[u - 1])
            if br < 2:
                combine(len(us) - 1, QT - 1)
            if br == 2:
                for _ in rounds:
                    pass
            post(len(us) - 1, *us[-1])
        for m in range(8):
            for c, (t0, tn) in enumerate(CHUNKS[:2]):
                e.wait_ge(*at((("out2", m), c, "mm")))
                x = X[:, m, t0:t0 + tn]
                v.tensor_tensor(x, psum.at((("out2", m), c))[:, 0:tn], x, ALU.add).then_inc(*e.step(("x2", m, c)))
        scale_rows("memn", (0,), KD, lambda k, t0, tn: mem[:, k, 0:L], lambda k, t0, tn: mem[:, k, 0:L],
                   lambda k, c: vec("norm_memkv", k), ((0, L),))
        scale_rows("memq", range(2), KD, x_of, h2_of, lambda k, c: vec("norm_mem", k))
        us = [(h, t) for h in range(4) for t in range(QT)]

        def mem_turned(u, h, t):
            e.wait_ge(*at(("mT mm", h, t)))
            if u >= 8:
                e.wait_ge(*at(("mo mm", us[u - 8][0], us[u - 8][1] // 4, 1)))
            c = t // 4
            v.tensor_copy(pmt[:, 2 * c:2 * c + 2, (t % 4) * P:(t % 4 + 1) * P],
                                 psum.at(("mT", h, t))[:, 0:256].rearrange("p (a b) -> p a b", b=P)).then_inc(*e.step(("mT ev", h, t)))

        def mem_max(u):
            h, t = us[u]
            s = 8 * (u % 4)
            e.wait_ge(*at(("ms mm", h, t)))
            v.tensor_reduce(small[:, s:s + 1], psum.at(("ms", h, t))[:, 0:L], AX.X, ALU.max, negate=True).then_inc(*e.step(("mmax", h, t)))

        def mem_prob(u):
            h, t = us[u]
            s = 8 * (u % 4)
            e.wait_ge(*at(("mexp", h, t)))
            v.reciprocal(small[:, s + 2:s + 3], small[:, s + 1:s + 2]).then_inc(*e.step(("mrecip", u)))
            e.wait_ge(*at(("mrecip", u)))
            v.tensor_scalar(pm[:, t % 4, :], pm[:, t % 4, :], small[:, s + 2:s + 3], None, ALU.mult).then_inc(*e.step(("mprob", h, t)))

        for u in range(len(us)):
            mem_max(u)
            if u >= 1:
                mem_prob(u - 1)
            if u >= 2:
                mem_turned(u - 2, *us[u - 2])
        mem_prob(len(us) - 1)
        mem_turned(len(us) - 2, *us[-2])
        mem_turned(len(us) - 1, *us[-1])
        for m in range(8):
            for c, (t0, tn) in enumerate(CHUNKS[:2]):
                e.wait_ge(*at((("mo2", m), c, "mm")))
                x = X[:, m, t0:t0 + tn]
                v.tensor_tensor(x, psum.at((("mo2", m), c))[:, 0:tn], x, ALU.add).then_inc(*e.step(("x3", m, c)))
        scale_rows("ffn", range(2), KD, x_of, h2_of, lambda k, c: vec("norm_ffn", k))

        def down(g):
            for m in range(8):
                for c, (t0, tn) in enumerate(CHUNKS[:2]):
                    e.wait_ge(*at((("down", g, m), c, "mm")))
                    x = X[:, m, t0:t0 + tn]
                    v.tensor_tensor(x, psum.at((("down", g, m), c))[:, 0:tn], x, ALU.add).then_inc(*e.step(("x4", g, m, c)))

        for g, (f0, fn) in enumerate(FGROUPS):
            for f in range(f0, f0 + fn):
                for s in range(2):
                    i = 2 * (f % 2) + s
                    w = 3 * (2 * f + s)
                    e.wait_ge(*at(("up ev", f, s, 0)))
                    e.wait_ge(*at(("up ev", f, s, 1)))
                    c = cb[:, i, :]
                    v.tensor_scalar(c, ub[:, i, 2:2 + N], vec("conv_w2", w + 2), vec("conv_b2", 2 * f + s),
                                             ALU.mult, ALU.add).then_inc(*e.step(("tap2", f, s, 0)))
                    e.wait_ge(*at(("tap2", f, s, 0)))
                    stt(out=c, in0=ub[:, i, 1:1 + N], scalar=vec("conv_w2", w + 1), in1=c, op0=ALU.mult,
                                 op1=ALU.add).then_inc(*e.step(("tap2", f, s, 1)))
                    e.wait_ge(*at(("tap2", f, s, 1)))
                    stt(out=c, in0=ub[:, i, 0:N], scalar=vec("conv_w2", w), in1=c, op0=ALU.mult, op1=ALU.add).then_inc(*e.step(("conv2", f, s)))
                e.wait_ge(*at(("ffn gate", f)))
                e.wait_ge(*at(("conv2", f, 1)))
                if g >= 2:
                    for m in range(8):
                        e.wait_ge(*at((("down", g - 2, m), 1, "mm")))
                v.tensor_tensor(actv[:, 8 * (g % 2) + f - f0, :], cb[:, 2 * (f % 2), :], cb[:, 2 * (f % 2) + 1, :],
                                       ALU.mult).then_inc(*e.step(("act", f)))
            if g >= 1:
                down(g - 1)
        down(len(FGROUPS) - 1)
        scale_rows("fin2", range(2), KD, x_of, h2_of, lambda k, c: vec("norm_final", k))

    def pool_program(raw):
        e = Engine(steps, "pool_done", raw)
        g = nc.gpsimd
        for out, value in ((eps_rms, EPS_RMS), (eps_ln, EPS_LN), (ln_scale, math.log(MLA_SCALE))):
            g.memset(out, value).then_inc(*e.step("small" if value < 0 else None))
        for l in range(LAYERS):
            own = own_chunks(l)
            nt = 10 if l == 0 else 8

            def project(h):
                free = [(l, "scores", len([x for x in units(l) if x[0] <= h - 2]) - 1)] if h >= 2 else []
                for c in range(2):
                    t0, tn = CHUNKS[c]
                    e.wait_ge(*at((l, "qh", h, c, "cos")))
                    e.wait_ge(*at((l, "qh", h, c, "sin")))
                    for needed in free:
                        e.wait_ge(*at(needed))
                    g.tensor_tensor(qh[64:96, h % 2, t0:t0 + tn], rt[64:96, 0, :], rt[64:96, 1, :], ALU.add).then_inc(*e.step((l, "qh", h, c, "rope")))

            for c in range(2):
                t0, tn = CHUNKS[c]
                e.wait_ge(*at((l, "rope", "ev", c)))
                for j in range(2):
                    g.tensor_tensor(kh[64:96, j, t0:t0 + tn], rt[64:96, 0, :], rt[64:96, 1, :], ALU.add).then_inc(*e.step((l, "kr", c, j)))
            for h in range(HEADS):
                project(h)
            e.wait_ge(*at((l, "aT mm", QT + (1 if l == 0 else -1))))
            e.wait_ge(*at((l, "attn", QT - 1)))
            for a, w in ((0, HALF), (HALF + N, 2 * HALF), (GW - HALF, HALF)):
                g.memset(glu[:, :, a:a + w], 0.0).then_inc(*e.step((l, "pads") if a > N + HALF else None))
            e.wait_ge(*at((l, "gate vectors")))
            for t in range(nt):
                e.wait_ge(*at((l, "sv ev", t)))
                g.tensor_tensor(vn[:, t, :], vn[:, t, :], lng, ALU.mult).then_inc(*e.step((l, "vg", t)))
                e.wait_ge(*at((l, "vg", t)))
                g.tensor_tensor(vn[:, t, :], vn[:, t, :], lnb, ALU.add).then_inc(*e.step((l, "vn", t)))
            for c, (t0, tn) in enumerate(own):
                for b in range(2):
                    y = Y[:, 6 + b, t0:t0 + tn]
                    e.wait_ge(*at((l, "sg ev", c, b)))
                    e.wait_ge(*at((l, f"u{b}", "ev", c)))
                    g.tensor_tensor(y, y, uu[:, b, t0:t0 + tn], ALU.mult).then_inc(*e.step((l, "y", 6 + b, c)))
        for t in range(2, QT):
            e.wait_ge(*at(("weighted", 8 * (t - 2) + 7)))
            d = view(SEL_AT[t] + t * P, P)
            g.affine_select(out=d, in_=d, compare_op=ALU.is_ge, fill=NEG, base=0, pattern=[[-1, P]],
                                   channel_multiplier=1).then_inc(*e.step(("causal", t)))
        for b in range(2):
            e.wait_ge(*at(("mo ev", 3, 1, b)))
        g.memset(ub[:, :, 0:2], 0.0).then_inc(*e.step("up pads"))

    def sync_program(raw):
        e = Engine(steps, None, raw)
        first = (("vec", S[:, VEC0:VEC0 + NV]), ("table", table), ("ident", ident), ("ones", ones), ("cd", cd))
        for name, out in first:
            raw.dma_start(out, A[name]).then_inc(*loads("consts_loaded", None))
        for k in range(0, KD, 2):
            raw.dma_start(X[:, k:k + 2, :], A["x"][:, k:k + 2, :]).then_inc(*loads("consts_loaded", "consts" if k == KD - 2 else None))
        for n, (name, index, width, slot, release, parts) in enumerate(ring.loads):
            if n >= SLOTS:
                e.wait_ge(*at(ring.loads[n - SLOTS][4]))
            a = RING0 + slot * 1024
            if name.startswith("bucket"):
                src = A[name][:, VCH[index][0]:VCH[index][0] + width]
            else:
                src = A[name][index][:, 0:width]
            raw.dma_start(S[0:parts, a:a + width], src).then_inc(*loads(f"tile{slot}_loaded", ("loaded", n)))
        for c in range(2):
            t0, tn = CHUNKS[c]
            for k in range(KD):
                e.wait_ge(*at(("fin2", "h", c, k)))
            raw.dma_start(A["out"][:, :, t0:t0 + tn], H2[:, :, t0:t0 + tn]).then_inc(*loads("out_stored", ("out", c)))
        e.wait_ge(*at(("out", 0)))
        e.wait_ge(*at(("out", 1)))

    block = stack.enter_context(nc.Block())

    @block.tensor
    def _(raw):
        tensor_program(raw)

    @block.scalar
    def _(raw):
        scalar_program(raw)

    @block.vector
    def _(raw):
        vector_program(raw)

    @block.gpsimd
    def _(raw):
        pool_program(raw)

    @block.sync
    def _(raw):
        sync_program(raw)

    stack.close()
    assert known is None or steps.at == known, "the two passes differ"
    return steps.at


def _tiles(w):
    k, m = w.shape
    return w.reshape(k // P, P, m // P, P).transpose(2, 1, 0, 3).reshape(m // P, P, k)


def _swapped(w):
    return w.reshape(w.shape[0], 2, 2, 8)[:, :, ::-1].reshape(w.shape[0], 32)


def _features(a):
    a = np.atleast_2d(a)
    return a.reshape(a.shape[0], -1, P).transpose(2, 0, 1).reshape(P, -1)


def _rope_tables():
    t = np.arange(N)
    inv = 10000.0 ** (-np.arange(0, 16, 2) / 16.0)
    ang = np.stack([(t // 64)[:, None] * inv, (t % 64)[:, None] * inv], axis=1)
    cos = np.repeat(np.cos(ang)[:, :, None], 2, 2).reshape(N, 32)
    sin = np.stack([-np.sin(ang), np.sin(ang)], 2).reshape(N, 32)
    return np.concatenate([cos.T, sin.T]).astype(np.float32)


def _dft(n):
    ang = 2 * np.pi * (np.outer(np.arange(n), np.arange(n)) % n) / n
    return np.cos(ang) / math.sqrt(n), -np.sin(ang) / math.sqrt(n)


def _buckets(branch):
    d = N - 1 - np.arange(VEC)
    n = np.maximum(d, 0)
    large = 16 + (np.log(np.maximum(n, 1).astype(np.float32) / np.float32(16)) / np.float32(math.log(128))
                  * np.float32(16)).astype(np.int32)
    b = np.where(n < 16, n, np.minimum(large, 31))
    out = np.zeros((33, VEC), np.float32)
    out[b, np.arange(VEC)] = 1.0
    if branch == 1:
        seen = sum(((d >= 0) & (d % r == 0) & (d // r <= 128)).astype(int) for r in (1, 4, 16))
    else:
        seen = (d >= 0).astype(int)
    out[32] = np.where(seen > 0, np.log(np.maximum(seen, 1)), NEG)
    out[:32, seen == 0] = 0.0
    return out


def _arrays(i):
    f = np.float32
    a = {}
    a["x"] = np.concatenate([i["x"][0], i["ctx"][0]]).T.reshape(KD, P, T).transpose(1, 0, 2)
    vec = np.zeros((P, NV), f)

    def put(name, v):
        vec[:, VCOL[name]:VCOL[name] + v.shape[1]] = v

    put("c", _features(np.stack([i["c"][0], i["c_ctx"]])).reshape(P, 2, KD).transpose(0, 2, 1).reshape(P, 16))
    for l in range(LAYERS):
        for name in ("b_ada", "norm_g", "q_norm_g", "kv_norm_g", "conv_b", "conv_ln_g", "conv_ln_b", "b_pw", "b_fourier"):
            put((name, l), _features(i[name][l]))
        put(("conv_w", l), i["conv_w"][l].T.reshape(2, P, TAPS).transpose(1, 0, 2).reshape(P, 62))
        w = i["w_in"][l]
        rope = np.concatenate([np.zeros((D, 64), f), w[:, 384:416], _swapped(w[:, 384:416])], 1)
        cols = [w[:, :384], rope, w[:, 672:800], w[:, 416:544], w[:, 800:928], w[:, 544:672], w[:, 928:1184],
                w[:, 1696:2720], w[:, 1184:1696]]
        a[f"w_in{l}"] = _tiles(np.concatenate(cols, 1))
        a[f"w_ada{l}"] = _tiles(i["w_ada"][l])
        uq = i["w_uq"][l].reshape(256, HEADS, 96)
        uq = np.concatenate([uq] + [np.stack([_swapped(uq[:, h, 64:]) for h in range(HEADS)], 1)], 2)
        a[f"w_uq{l}"] = uq.reshape(1, 2, P, 512).transpose(0, 2, 1, 3).reshape(1, P, 1024)
        ukv = i["w_ukv"][l].reshape(P, HEADS, 2, 64)
        a[f"w_ukv{l}"] = ukv.transpose(2, 0, 1, 3).reshape(2, P, 256)
        a[f"w_pw{l}"] = _tiles(i["w_pw"][l])
        a[f"w_fourier{l}"] = _tiles(i["w_fourier"][l])
        a[f"w_s{l}"] = i["w_s"][l].transpose(2, 0, 1).reshape(1, P, 512)
        a[f"w_out{l}"] = _tiles(i["w_out"][l])
    a["sgu_g"], a["sgu_b"] = i["sgu_ln_g"], i["sgu_ln_b"]
    a["b_s"] = i["b_s"].reshape(8, P)
    for name, src in (("final_g", "final_g"), ("norm_mix", "norm_mix_2"), ("norm_mem", "norm_mem_2"),
                      ("norm_memkv", "norm_memkv_2"), ("norm_ffn", "norm_ffn_2"), ("norm_final", "norm_final_2"),
                      ("subln", "subln_2")):
        put(name, _features(i[src]))
    cw = i["conv_w_2"][0].reshape(3, 2, FF, P)
    put("conv_w2", cw.transpose(3, 2, 1, 0).reshape(P, 132))
    put("conv_b2", i["conv_b_2"][0].reshape(2, FF, P).transpose(2, 1, 0).reshape(P, 44))
    a["vec"] = vec
    a["rope"] = _rope_tables()
    c64, s64 = _dft(64)
    cd = np.zeros((P, 256))
    for g in range(2):
        r = slice(64 * g, 64 * g + 64)
        cd[r, 64 * g:64 * g + 64] = c64
        cd[r, P + 64 * g:P + 64 * g + 64] = -s64
    a["cd"] = cd.astype(f)
    c, s = _dft(N)
    a["dft"] = np.stack([c.reshape(QT, P, 2, 512), s.reshape(QT, P, 2, 512)], 3).transpose(2, 0, 1, 3, 4).reshape(
        2 * QT, P, 1024).astype(f)
    c, s = _dft(L)
    a["dft_ctx"] = np.stack([c.reshape(CT, P, L), s.reshape(CT, P, L)], 2).reshape(CT, P, 2 * L).astype(f)
    a["table"] = np.concatenate([i["rel_bias_2"], np.ones((1, 12), f)])
    for br in range(3):
        a[f"bucket{br}"] = _buckets(br)
    a["ident"] = np.eye(P, dtype=f)
    a["ones"] = np.ones((P, P), f)
    a["lam"] = np.stack([i[f"lam_{n}_2"][0] for n in ("q1", "k1", "q2", "k2")]).reshape(1, 256)
    w = i["w_in_2"][0]
    cols = [w[:, 3072:3584], w[:, 3584:3648], w[:, 3584:3648]]
    for q, k, v in ((0, 512, 1024), (256, 768, 1280), (1536, 1792, 2048), (2304, 2560, 2816)):
        cols += [w[:, q:q + 256], w[:, k:k + 256], w[:, v:v + 256]]
    a["w_in2"] = _tiles(np.concatenate(cols, 1))
    a["w_iw"] = w[:, 3648:].reshape(KD, P, 8).transpose(1, 0, 2).reshape(1, P, 64)
    for name, src in (("w_out2", "w_out_2"), ("w_mq", "w_mq_2"), ("w_mkv", "w_mkv_2"), ("w_mo", "w_mo_2")):
        a[name] = _tiles(i[src][0])
    up = i["w_up_2"][0].reshape(D, 2, FF, P).transpose(0, 2, 1, 3).reshape(D, 2 * FF * P)
    a["w_up"] = _tiles(up)
    down = np.zeros((24, P, 1024), f)
    for g, (f0, fn) in enumerate(FGROUPS):
        down[8 * g:8 * g + 8, :, :fn * P] = _tiles(i["w_down_2"][0][f0 * P:(f0 + fn) * P])
    a["w_down"] = down
    a["mem"] = i["mem_2"][0].T.reshape(KD, P, L).transpose(1, 0, 2)
    return {k: np.ascontiguousarray(v) for k, v in a.items()}


def kernel(**inputs):
    import concourse.bacc as bacc
    from concourse.bass_utils import run_bass_kernel_spmd

    arrays = _arrays({k: np.asarray(v) for k, v in inputs.items()})

    def declared():
        nc = bacc.Bacc("TRN2", target_bir_lowering=False, num_devices=1)
        aps = {k: nc.dram_tensor(f"in_{k}", v.shape, F32, kind="ExternalInput").ap() for k, v in arrays.items()}
        aps["out"] = nc.dram_tensor("out", (P, KD, N), F32, kind="ExternalOutput").ap()
        return nc, aps

    known = program(*declared(), None)
    nc, aps = declared()
    program(nc, aps, known)
    r = run_bass_kernel_spmd(nc, [{f"in_{k}": v for k, v in arrays.items()}], core_ids=[0])
    return r.results[0]["out"].transpose(2, 1, 0).reshape(1, N, D)
```

```python
import math
from contextlib import ExitStack

import numpy as np
import concourse.bass as bass
from concourse import mybir

ALU = mybir.AluOpType
ACT = mybir.ActivationFunctionType
AX = mybir.AxisListType
F32 = mybir.dt.float32

P = 128
D = 1024
N = 1024
L = 256
T = N + L
KD = D // P
LAYERS = 2
CHUNKS = ((0, 512), (512, 512), (1024, 256))
QT = N // P
CT = L // P
HEADS = 4
TAPS = 31
HALF = TAPS // 2
EPS_RMS, EPS_LN = 1e-6, 1e-5
MLA_SCALE = 1.0 / math.sqrt(96)
LAM_INIT = 0.2
NEG = -1e30
TAKEN = -3e38
TOPK = 256
FF = 22
FGROUPS = ((0, 8), (8, 8), (16, 6))
VEC = N + P - 1


VCOL = {}


def _layout_vectors():
    n = 0
    for l in range(LAYERS):
        for name, width in (("b_ada", 24), ("norm_g", 8), ("q_norm_g", 2), ("kv_norm_g", 1), ("conv_w", 62),
                            ("conv_b", 2), ("conv_ln_g", 2), ("conv_ln_b", 2), ("b_pw", 2), ("b_fourier", 2)):
            VCOL[name, l] = n
            n += width
    for name, width in (("c", 16), ("final_g", 8), ("norm_mix", 8), ("norm_mem", 8), ("norm_memkv", 8),
                        ("norm_ffn", 8), ("norm_final", 8), ("subln", 1), ("conv_w2", 132), ("conv_b2", 44)):
        VCOL[name] = n
        n += width
    return n


NV = _layout_vectors()

X0 = 0
H0 = 8 * T
Y0 = 16 * T
S0 = 24 * T
SLOTS = 4
TOP = 53208
RING0 = TOP - SLOTS * 1024
IDENT0 = RING0 - P
ONES0 = IDENT0 - P
CD0 = ONES0 - 256
VEC0 = CD0 - NV
MOD0 = VEC0 - 112
AM0 = MOD0 - 16
SQ0 = AM0 - 1024
RR0 = SQ0 - T
SM0 = RR0 - 204
BSB0 = SM0 - 256
S_END = BSB0
VCH = ((0, 512), (512, 512), (1024, VEC - 1024))

MQ0, MKV0, MV0 = S0, S0 + 2 * T, S0 + 3 * T
KH0 = MV0 + 10 * 256
CS0 = KH0 + 2 * T
AO0 = CS0 + N
RT0 = AO0 + 10 * 256
QH0, PR0, PT0 = Y0 + 2 * T, Y0 + 4 * T, Y0 + 6 * T
GW = T + 4 * HALF
CW = GW - 2 * HALF
GLU0, CV0 = S0, S0 + 2 * GW
FM0 = CV0 + 2 * CW
SIG0 = FM0 + 2 * T
LNG0 = SIG0 + 1024
YT0 = LNG0 + 512
UU0, VN0 = GLU0, GLU0 + 2 * T
H20, Y20, Z0 = H0, H0 + KD * N, H0 + 2 * KD * N
SEL_AT = {t: Z0 + P * sum(range(3, t + 1)) for t in range(2, QT)}
Q20 = Z0 + P * sum(range(3, QT + 1))
K20, V20, STRIP0 = Q20 + 2048, Q20 + 4096, Q20 + 6144
IQ0, IK0, IR0 = Q20, Q20 + 4096, Q20 + 5120
SC0 = STRIP0 + 4096
PT20, OT20 = SC0 + 2048, SC0 + 3072
SC1 = Y20 + 5 * N
QM0 = Z0
KM0, VM0, MEM0, PM0 = QM0 + 8192, QM0 + 10240, QM0 + 12288, QM0 + 14336
PMT0 = PM0 + 1024
ACT0, UW = Y20, N + 2
UB0 = ACT0 + 16 * N
CB0 = UB0 + 4 * UW

assert max(RT0 + 1024, YT0 + 5120, OT20 + 512, PMT0 + 2048, CB0 + 4 * N) <= S_END
assert UU0 + 4 * T <= FM0 and PT0 + 2 * T <= S0


def gcol(c):
    return CHUNKS[c][0] + (HALF if c < 2 else 3 * HALF)


def ccol(c):
    return CHUNKS[c][0] + (0 if c < 2 else 2 * HALF)


def c_of(t):
    return min(t // 4, 2)


def units(l):
    return [(h, t) for h in range(HEADS) for t in range(QT + (CT if l == 0 else 0))]


def units2(br):
    return [(t, h) for t in range(QT) for h in range(2 if br < 2 else 4)]


def own_chunks(l):
    return CHUNKS if l == 0 else CHUNKS[:2]


class Steps:

    def __init__(self, sems, known):
        self.sems, self.known, self.count, self.at = sems, known, {}, {}

    def reach(self, name, key, by):
        self.count[name] = self.count.get(name, 0) + by
        if key is not None:
            assert key not in self.at, key
            self.at[key] = (name, self.count[name])
        return self.sems[name], by

    def value(self, key):
        name, value = self.known[key] if self.known and key is not None else ("tensor_done", 0)
        return self.sems[name], value


class Engine:

    def __init__(self, steps, name, raw):
        self.steps, self.name, self.raw, self.reached = steps, name, raw, {}

    def step(self, key=None):
        return self.steps.reach(self.name, key, 1)

    def wait_ge(self, semaphore, value):
        if value > self.reached.get(semaphore.name, 0):
            self.reached[semaphore.name] = value
            self.raw.wait_ge(semaphore, value)


POOLS = {"all": (0, 8), "mla scores": (0, 6), "mla turns": (6, 2), "scores": (0, 4), "turns": (4, 2), "outputs": (6, 2)}


class Psum:

    def __init__(self, tensor, steps):
        self.tensor, self.steps, self.next, self.reader, self.bank = tensor, steps, {}, {}, {}

    def take(self, e, key, reader, n=1, pool="all"):
        first, banks = POOLS[pool]
        step = self.next.get(pool, 0)
        if step + n > banks:
            step = 0
        b = first + step
        self.next[pool] = (step + n) % banks
        for i in range(b, b + n):
            for read in self.reader.get(i, []):
                e.wait_ge(*self.steps.value(read))
            self.reader[i] = reader if isinstance(reader, list) else [reader]
        self.bank[key] = b
        return self.at(key)

    def at(self, key):
        return self.tensor[:, self.bank[key] * 512:8 * 512]


class Ring:

    def __init__(self, tensor, steps):
        self.tensor, self.steps, self.loads = tensor, steps, []

    def take(self, e, name, index, width, release, parts=P):
        n = len(self.loads)
        slot = n % SLOTS
        self.loads.append((name, index, width, slot, release, parts))
        e.wait_ge(*self.steps.value(("loaded", n)))
        a = RING0 + slot * 1024
        return self.tensor[0:parts, a:a + width]



LOADS = ("consts_loaded", "rope_loaded", "gate_bias_loaded", "strips_loaded", "mem_loaded", "lambda_loaded",
         "ada_loaded")
STORES = ("vec_stored", "rows_stored", "out_stored")


ADA_FIRST = 16
assert ADA_FIRST * 1024 <= 16 * T


def later_ada(l):
    if l:
        return {}
    keys = ("q0", "q1", "kv", "rope")
    tiles = {key: [(0, ADA_FIRST + 2 * i + j) for j in range(2)] for i, key in enumerate(keys)}
    for i, key in enumerate(("s0", "a0", "s1", "a1", "f0", "f1") + tuple(f"g{g}" for g in range(2, 8))):
        tiles[key] = [(1, 2 * i + j) for j in range(2)]
    return tiles


def program(nc, A, known):
    stack = ExitStack()
    sems = {}
    for name in ("tensor_done", "scalar_done", "vector_done", "pool_done") + LOADS + STORES + tuple(
            f"tile{i}_loaded" for i in range(SLOTS)):
        sems[name] = stack.enter_context(nc.semaphore(name))
    steps = Steps(sems, known)
    S = stack.enter_context(nc.sbuf_tensor("sb", [P, TOP], F32))
    PS = stack.enter_context(nc.psum_tensor("ps", [P, 8 * 512], F32))
    psum, ring = Psum(PS, steps), Ring(S, steps)
    at = steps.value

    def loads(name, key):
        return steps.reach(name, key, 16)

    vec_dram = nc.dram_tensor("vec_dram", (12, VEC), F32, kind="Internal").ap()
    rows_dram = nc.dram_tensor("rows_dram", (12, P, VEC), F32, kind="Internal").ap()

    def view(at, a, b=None):
        v = S[:, at:at + a * (b or 1)]
        return v.rearrange("p (a b) -> p a b", b=b) if b else v

    X, H, Y = view(X0, KD, T), view(H0, KD, T), view(Y0, KD, T)
    ident, ones, cd = view(IDENT0, P), view(ONES0, P), view(CD0, 256)
    mod, silu_c, am = view(MOD0, 48, 2), view(MOD0 + 96, KD, 2), view(AM0, KD, 2)
    sq, rr, small, bsb = view(SQ0, 2, 512), view(RR0, T), view(SM0, 204), view(BSB0, 2, P)
    eps_rms, eps_ln, ln_scale = small[:, 60:61], small[:, 61:62], small[:, 62:63]
    mq, mkv, mv = view(MQ0, 2, T), view(MKV0, T), view(MV0, 10, 256)
    kh, qh, cs = view(KH0, 2, T), view(QH0, 2, T), view(CS0, N)
    ao, rt, pt = view(AO0, 10, 256), view(RT0, 2, 512), view(PT0, 2, T)
    prob = [view(PR0, T), view(PR0 + T, T), rr]
    glu, cv, fm = view(GLU0, 2, GW), view(CV0, 2, CW), view(FM0, 2, T)
    lng, lnb, yt = view(LNG0, 256), view(LNG0 + 256, 256), view(YT0, 20, 256)
    uu, vn = view(UU0, 2, T), view(VN0, 10, 256)
    vec_tmp = view(S0, 3, VEC)
    ada_rows = view(YT0 + 5120 - 256, 2, P)
    first_ada = view(H0, ADA_FIRST, 1024)
    H2, Y2 = view(H20, KD, N), view(Y20, KD, N)
    q2, k2, v2, strip = view(Q20, 2, N), view(K20, 2, N), view(V20, QT, 256), view(STRIP0, 4, N)
    sc = [view(SC0, N), view(SC0 + N, N), rr[:, 0:N]]
    sc1 = [view(SC1 + i * N, N) for i in range(3)]
    pt2, ot2 = [view(PT20, QT, P), view(SQ0, QT, P)], view(OT20, 2, 256)
    unread = view(AM0, P)
    iq, ik, ir = view(IQ0, 4, N), view(IK0, N), view(IR0, 2, N)
    iw, table = small[:, 64:128], small[0:33, 128:140]
    lam_in, neg_lam, subln8, top8 = view(PT20, 4, 64), small[:, 40:41], small[:, 41:42], small[:, 48:56]
    qm, km, vm, mem = view(QM0, KD, N), view(KM0, KD, 256), view(VM0, 2, N), view(MEM0, KD, 256)
    pm, pmt = view(PM0, 4, 256), view(PMT0, 4, 512)
    actv, ub, cb = view(ACT0, 16, N), view(UB0, 4, UW), view(CB0, 4, N)

    def sel(t):
        return view(SEL_AT[t], (t + 1) * P)

    def vec(name, i=0, n=1):
        a = VEC0 + VCOL[name] + i
        return S[:, a:a + n]

    def h_keys(l, c):
        return [(l, "h", c, k) for k in range(KD)]

    def y_keys(l, c):
        return [(l, "attn", t) for t in tiles_of(c)] + [(l, "y", k, c) for k in range(2, 8)]

    def tiles_of(c):
        return range(CHUNKS[c][0] // P, (CHUNKS[c][0] + CHUNKS[c][1]) // P)

    def tensor_program(raw):
        e = Engine(steps, "tensor_done", raw)
        mm, transpose = nc.tensor.matmul, nc.tensor.transpose

        def sums(key, rhs_of, nk, width, reader, after):
            ps = psum.take(e, key, reader)
            for k in range(nk):
                for needed in after(k):
                    e.wait_ge(*at(needed))
                mm(ps[:, 0:width], ones, rhs_of(k), start=(k == 0), stop=(k == nk - 1)).then_inc(*e.step((key, "read", k)))

        def norm_sums(tag, chunks, nk=KD):
            for c in chunks:
                tn = CHUNKS[c][1]
                sums((tag, "ms", c), lambda k: sq[:, k % 2, 0:tn], nk, tn, (tag, "ln", c), lambda k: [(tag, "sq", c, k)])

        def norm_sum(tag, chunks):
            for c in chunks:
                t0, tn = CHUNKS[c]
                ps = psum.take(e, (tag, "ms", c), (tag, "ln", c))
                e.wait_ge(*at((tag, "acc", c, KD - 1)))
                mm(ps[:, 0:tn], ones, rr[:, t0:t0 + tn], start=True, stop=True).then_inc(*e.step((tag, "sum", c)))

        def linear(key, name, index, src, nk, chunks, reader, after):
            w = ring.take(e, name, index, nk * P, (key, len(chunks) - 1, "mm")).rearrange("p (k m) -> p k m", m=P)
            for c, (t0, tn) in enumerate(chunks):
                for needed in after(c):
                    e.wait_ge(*at(needed))
                ps = psum.take(e, (key, c), reader(c))
                for k in range(nk):
                    ins = mm(ps[:, 0:tn], w[:, k, :], src(k, t0, tn), start=(k == 0), stop=(k == nk - 1))
                ins.then_inc(*e.step((key, c, "mm")))

        def ada(l, m):
            if l == 0 and m < ADA_FIRST:
                e.wait_ge(*at("first ada"))
                w = first_ada[:, m, :]
            else:
                w = ring.take(e, f"w_ada{l}", m, 1024, (l, "ada", m))
            w = w.rearrange("p (k m) -> p k m", m=P)
            ps = psum.take(e, (l, "ada row ps", m), (l, "ada row", m))
            for k in range(KD):
                ins = mm(ps[0:2, 0:P], silu_c[:, k, :], w[:, k, :], start=(k == 0), stop=(k == KD - 1))
            ins.then_inc(*e.step((l, "ada", m)))
            turn_rows()
            to_turn.append((l, m))

        to_turn = []

        def turn_rows():
            if to_turn:
                l, m = to_turn.pop()
                e.wait_ge(*at((l, "ada row", m)))
                ps = psum.take(e, (l, "ada ps", m), (l, "ada ev", m))
                transpose(ps[:, 0:2], ada_rows[0:2, m % 2, :], ident[0:2, 0:2]).then_inc(*e.step((l, "ada turned", m)))

        def project(l, h):
            wq, wk = mla_weights
            for c, (t0, tn) in enumerate(own_chunks(l)):
                e.wait_ge(*at((l, "cq", c, 0)))
                e.wait_ge(*at((l, "cq", c, 1)))
                readers = [(l, "qh", h, c, "ev")] + ([(l, "qh", h, c, "sin")] if c < 2 else [])
                ps = psum.take(e, (l, "qh", h, c, "ps"), readers)
                for k in range(2):
                    ins = mm(ps[:, 0:tn], wq[:, k, h, :], mq[:, k, t0:t0 + tn], start=(k == 0), stop=(k == 1))
                ins.then_inc(*e.step((l, "qh", h, c)))
            for c, (t0, tn) in enumerate(CHUNKS):
                e.wait_ge(*at((l, "ckv", c, 0)))
                ps = psum.take(e, (l, "kh", h, c, "ps"), (l, "kh", h, c, "ev"))
                mm(ps[0:64, 0:tn], wk[:, h * 64:(h + 1) * 64], mkv[:, t0:t0 + tn], start=True, stop=True).then_inc(*e.step((l, "kh", h, c)))

        def scores(l, u, h, t):
            keys0, nk = (0, T) if t < QT else (N, L)
            c = c_of(t)
            for i in range(3):
                e.wait_ge(*at((l, "kh", h, i, "ev")))
            for i in range(3):
                for j in range(2):
                    e.wait_ge(*at((l, "kr", i, j)))
            e.wait_ge(*at((l, "qh", h, c, "ev")))
            if c < 2:
                e.wait_ge(*at((l, "qh", h, c, "rope")))
            ps = psum.take(e, (l, "s", u), (l, "exp", u), (nk + 511) // 512, "mla scores")
            for b in range(0, nk, 512):
                w = min(512, nk - b)
                ins = mm(ps[:, b:b + w], qh[0:96, h % 2, t * P:(t + 1) * P], kh[0:96, h % 2, keys0 + b:keys0 + b + w],
                         start=True, stop=True)
            ins.then_inc(*e.step((l, "scores", u)))

        def transposes(l, u, t, groups):
            n = 10 if t < QT else 2
            e.wait_ge(*at((l, "exp", u)))
            for g in groups:
                if g < n:
                    ps = psum.take(e, (l, "pT", u, g), (l, "pT ev", u, g), 1, "mla turns")
                    for j in range(g, min(g + 4, n)):
                        ins = transpose(ps[:, (j - g) * P:(j - g + 1) * P], prob[u % 3][:, j * P:(j + 1) * P], ident)
                    ins.then_inc(*e.step((l, "turned", u, g)))

        def values(l, u, h, t):
            first, n = (0, 10) if t < QT else (QT, 2)
            ps = psum.take(e, (l, "o", u), (l, "o ev", u), 1, "mla turns")
            for j in range(n):
                e.wait_ge(*at((l, "v ev", first + j)))
                e.wait_ge(*at((l, "pT ev", u, j // 4 * 4)))
                ins = mm(ps[:, 0:64], pt[:, u % 2, j * P:(j + 1) * P], mv[:, first + j, h * 64:(h + 1) * 64],
                         start=(j == 0), stop=(j == n - 1))
            ins.then_inc(*e.step((l, "pv", u)))

        mla_weights = []

        def attention(l):
            us = units(l)
            w = ring.take(e, f"w_ukv{l}", 1, 256, (l, "v", 9))
            for t in range(10):
                e.wait_ge(*at((l, "ckv", c_of(t), 0)))
                ps = psum.take(e, (l, "v ps", t), (l, "v ev", t))
                mm(ps[:, 0:256], mkv[:, t * P:(t + 1) * P], w, start=True, stop=True).then_inc(*e.step((l, "v", t)))
            last = len(own_chunks(l)) - 1
            wq = ring.take(e, f"w_uq{l}", 0, 1024, (l, "qh", 3, last)).rearrange("p (k h m) -> p k h m", k=2, h=4)
            wk = ring.take(e, f"w_ukv{l}", 0, 256, (l, "kh", 3, 2))
            mla_weights[:] = [wq, wk]
            project(l, 0)
            for u in range(len(us) + 3):
                if u >= 2 and u - 2 < len(us):
                    transposes(l, u - 2, us[u - 2][1], (0, 4))
                if u < len(us):
                    scores(l, u, *us[u])
                if u >= 2 and u - 2 < len(us):
                    transposes(l, u - 2, us[u - 2][1], (8,))
                if u >= 3:
                    values(l, u - 3, *us[u - 3])
                if u < len(us) and us[u][1] == 0 and us[u][0] + 1 < HEADS:
                    project(l, us[u][0] + 1)
            for t in range(QT + (CT if l == 0 else 0)):
                e.wait_ge(*at((l, "o ev", us.index((HEADS - 1, t)))))
                ps = psum.take(e, (l, "aT", t), (l, "attn", t))
                for b in range(2):
                    ins = transpose(ps[:, b * P:(b + 1) * P], ao[:, t, b * P:(b + 1) * P], ident)
                ins.then_inc(*e.step((l, "aT mm", t)))

        def first_block(l):
            own = own_chunks(l)
            oc = range(len(own))
            nt = 10 if l == 0 else 8

            def w_in(b, key, chunks=own, readers=None):
                linear((l, key), f"w_in{l}", b, lambda k, t0, tn: H[:, k, t0:t0 + tn], KD, chunks,
                       readers or (lambda c: (l, key, "ev", c)), lambda c: h_keys(l, c))
                for tile in later_ada(l).get(key, ()):
                    ada(*tile)
                if key in ("rope", "g7"):
                    turn_rows()

            if l:
                norm_sum((l, "n"), range(3))
            w_in(0, "q0")
            w_in(1, "q1")
            w_in(2, "kv", CHUNKS)
            w_in(3, "rope", CHUNKS, lambda c: (l, "rope", "ev", c) if c < 2 else (l, "kr", 2, 1))
            w_in(10, "g0")
            w_in(11, "g1")
            norm_sums((l, "qn"), oc, 2)
            norm_sums((l, "kn"), range(3), 1)
            attention(l)
            for i, key in enumerate(("s0", "a0", "s1", "a1", "f0", "f1")):
                w_in(4 + i, key)
            for g in range(2, 8):
                w_in(10 + g, f"g{g}")
            for c in oc:
                tn = CHUNKS[c][1]
                sums((l, "cmu", c), lambda k: cv[:, k, ccol(c):ccol(c) + tn], 2, tn, (l, "centre", c, 1),
                     lambda k: [(l, "conv", k)])
            norm_sums((l, "cn"), oc, 2)
            for t in range(nt):
                ps = psum.take(e, (l, "ft", t), (l, "yt", t))
                for b in range(2):
                    e.wait_ge(*at((l, f"f{b}", "ev", c_of(t))))
                    ins = mm(ps[:, b * 256:(b + 1) * 256], fm[:, b, t * P:(t + 1) * P], cd, start=True, stop=True)
                ins.then_inc(*e.step((l, "ft mm", t)))
            for b in range(2):
                linear((l, "pw", b), f"w_pw{l}", b, lambda k, t0, tn: cv[:, k, ccol(c_of(t0 // P)):ccol(c_of(t0 // P)) + tn],
                       2, own, lambda c: (l, "y", 2 + b, c), lambda c: [(l, "csilu", k, c) for k in range(2)])
            for c, (t0, tn) in enumerate(own):
                first, n = (0, 8) if c < 2 else (8, 2)
                out = [psum.take(e, (l, "mix", c, b), (l, "mix ev", c, b)) for b in range(2)]
                for t in range(n):
                    w = ring.take(e, "dft" if c < 2 else "dft_ctx", c * 8 + t if c < 2 else t, 2 * tn,
                                  (l, "mix mm", c, t))
                    e.wait_ge(*at((l, "yt", first + t)))
                    for b in range(2):
                        for s in range(2):
                            ins = mm(out[b][:, 0:tn], yt[:, 2 * (first + t) + b, s * P:(s + 1) * P],
                                     w[:, s * tn:(s + 1) * tn], start=(t == 0 and s == 0), stop=(t == n - 1 and s == 1))
                    ins.then_inc(*e.step((l, "mix mm", c, t)))
            w_in(18, "u0")
            w_in(19, "u1")
            for b in range(2):
                linear((l, "four", b), f"w_fourier{l}", b, lambda k, t0, tn: fm[:, k, t0:t0 + tn], 2, own,
                       lambda c: (l, "y", 4 + b, c), lambda c: [(l, "mix ev", c, k) for k in range(2)])
            wv = [ring.take(e, f"w_in{l}", 20 + i, 1024, (l, "sv mm", nt - 1)).rearrange("p (k m) -> p k m", m=P)
                  for i in range(2)]
            for t in range(nt):
                ps = psum.take(e, (l, "sv", t), (l, "sv ev", t))
                for i in range(2):
                    for k in range(KD):
                        ins = mm(ps[:, i * P:(i + 1) * P], H[:, k, t * P:(t + 1) * P], wv[i][:, k, :],
                                 start=(k == 0), stop=(k == KD - 1))
                ins.then_inc(*e.step((l, "sv mm", t)))
            ws = ring.take(e, f"w_s{l}", 0, 512, (l, "sg mm", len(own) - 1, 1)).rearrange("p (g i) -> p g i", g=4)
            for c, (t0, tn) in enumerate(own):
                for b in range(2):
                    ps = psum.take(e, (l, "sg", c, b), (l, "sg ev", c, b))
                    for j in range(tn // P):
                        e.wait_ge(*at((l, "vn", t0 // P + j)))
                        for g in range(2):
                            a = (2 * b + g) * 64
                            ins = mm(ps[g * 64:(g + 1) * 64, j * P:(j + 1) * P], vn[:, t0 // P + j, a:a + 64],
                                     ws[:, 2 * b + g, :], start=True, stop=True)
                    ins.then_inc(*e.step((l, "sg mm", c, b)))
            for m in range(8):
                linear((l, "out", m), f"w_out{l}", m, lambda k, t0, tn: Y[:, k, t0:t0 + tn], KD, own,
                       lambda c: (l, "x", m, c), lambda c: y_keys(l, c))

        e.wait_ge(*at("consts"))
        norm_sum((0, "n"), range(3))
        e.wait_ge(*at("silu_c"))
        for m in range(ADA_FIRST):
            ada(0, m)
        turn_rows()
        for br in range(3):
            for c, (a, w) in enumerate(VCH):
                oh = ring.take(e, f"bucket{br}", c, w, ("vec mm", br, c), 33)
                ps = psum.take(e, ("vec ps", br, c), ("vec ev", br, c))
                mm(ps[0:4, 0:w], table[:, 4 * br:4 * br + 4], oh, start=True, stop=True).then_inc(*e.step(("vec mm", br, c)))
        for l in range(LAYERS):
            first_block(l)
        norm_sum("fin1", range(2))
        norm_sum("mix", range(2))

        def from_h2(k, t0, tn):
            return H2[:, k, t0:t0 + tn]

        def w_in2(b, key):
            linear(key, "w_in2", b, from_h2, KD, CHUNKS[:2], lambda c: (key, "ev", c),
                   lambda c: [("mix", "h", c, k) for k in range(KD)])

        for i in range(4):
            w_in2(i, f"iq{i}")
        w_in2(4, "ik")
        w = ring.take(e, "w_iw", 0, 64, ("iw mm", QT - 1)).rearrange("p (k m) -> p k m", m=8)
        ps = psum.take(e, "iw ps", "iw")
        for t in range(QT):
            for k in range(KD):
                ins = mm(ps[:, 8 * t:8 * t + 8], H2[:, k, t * P:(t + 1) * P], w[:, k, :], start=(k == 0), stop=(k == KD - 1))
            ins.then_inc(*e.step(("iw mm", t)))
        for t in range(2, QT):
            n = (t + 1) * P
            for h in range(8):
                a = 64 * (h % 2)
                e.wait_ge(*at((f"iq{h // 2}", "ev", t // 4)))
                e.wait_ge(*at(("ik", "ev", t // 4)))
                e.wait_ge(*at(("ik", "ev", 0)))
                ps = psum.take(e, ("is", t, h), ("relu", t, h), (n + 511) // 512)
                for b in range(0, n, 512):
                    w = min(512, n - b)
                    ins = mm(ps[:, b:b + w], iq[a:a + 64, h // 2, t * P:(t + 1) * P], ik[a:a + 64, b:b + w],
                             start=True, stop=True)
                ins.then_inc(*e.step(("is mm", t, h)))

        def scores2(br, u, t, h):
            n = (t + 1) * P
            maps = 2 if br < 2 else 1
            for m in range(maps):
                f = (h * maps + m) * 64
                a, blk = f % P, f // P
                e.wait_ge(*at((f"q{blk}{br}", "ev", t // 4)))
                e.wait_ge(*at((f"k{blk}{br}", "ev", t // 4)))
                e.wait_ge(*at((f"k{blk}{br}", "ev", 0)))
                ps = psum.take(e, ("s2", br, u, m), ("biased", br, u, m), (n + 511) // 512, "scores")
                for b in range(0, n, 512):
                    w = min(512, n - b)
                    ins = mm(ps[:, b:b + w], q2[a:a + 64, blk, t * P:(t + 1) * P], k2[a:a + 64, blk, b:b + w],
                             start=True, stop=True)
                ins.then_inc(*e.step(("s2 mm", br, u, m)))

        def turn2(br, u, t, h):
            e.wait_ge(*at(("prob", br, u)))
            for g in range(0, t + 1, 4):
                ps = psum.take(e, ("pT2", br, u, g), ("pT2 ev", br, u, g), 1, "turns")
                for j in range(g, min(g + 4, t + 1)):
                    ins = transpose(ps[:, (j - g) * P:(j - g + 1) * P], sc[u % 3][:, j * P:(j + 1) * P], ident)
                ins.then_inc(*e.step(("turned2", br, u, g)))

        def values2(br, u, t, h):
            dh = 128 if br < 2 else 64
            ps = psum.take(e, ("o2", br, u), ("o2 ev", br, u), 1, "outputs")
            for j in range(t + 1):
                e.wait_ge(*at(("v2 ev", br, j)))
                e.wait_ge(*at(("pT2 ev", br, u, j // 4 * 4)))
                ins = mm(ps[:, 0:dh], pt2[u % 2][:, j, :], v2[:, j, h * dh:(h + 1) * dh], start=(j == 0), stop=(j == t))
            ins.then_inc(*e.step(("pv2", br, u)))

        def back2(br, t):
            e.wait_ge(*at(("o2 ev", br, units2(br).index((t, units2(br)[-1][1])))))
            ps = psum.take(e, ("oT2", br, t), ("y2", br, t), 1, "outputs")
            for b in range(2):
                ins = transpose(ps[:, b * P:(b + 1) * P], ot2[:, t % 2, b * P:(b + 1) * P], ident)
            ins.then_inc(*e.step(("oT2 mm", br, t)))

        for br in range(4):
            for i in range(4):
                w_in2(5 + 6 * br + i, f"{'qk'[i // 2]}{i % 2}{br}")
            wv = [ring.take(e, "w_in2", 9 + 6 * br + i, 1024, ("v2 mm", br, QT - 1)).rearrange("p (k m) -> p k m", m=P)
                  for i in range(2)]
            for t in range(QT):
                ps = psum.take(e, ("v2 ps", br, t), ("v2 ev", br, t))
                for i in range(2):
                    for k in range(KD):
                        ins = mm(ps[:, i * P:(i + 1) * P], H2[:, k, t * P:(t + 1) * P], wv[i][:, k, :],
                                 start=(k == 0), stop=(k == KD - 1))
                ins.then_inc(*e.step(("v2 mm", br, t)))
            us = units2(br)
            for u in range(len(us) + 5):
                if u < len(us):
                    scores2(br, u, *us[u])
                if 0 <= u - 2 < len(us):
                    turn2(br, u - 2, *us[u - 2])
                if 0 <= u - 3 < len(us):
                    values2(br, u - 3, *us[u - 3])
                if u >= 5 and us[u - 5][1] == us[-1][1]:
                    back2(br, us[u - 5][0])
        for m in range(8):
            linear(("out2", m), "w_out2", m, lambda k, t0, tn: Y2[:, k, t0:t0 + tn], KD, CHUNKS[:2],
                   lambda c: ("x2", m, c), lambda c: [("y2", br, t) for br in range(4) for t in tiles_of(c)])
            if m == 3:
                sums(("memn", "ms", 2), lambda k: sq[:, k % 2, 0:L], KD, L, ("memn", "ln", 2),
                     lambda k: [("memn", "sq", 2, k)])
        for m in range(8):
            linear(("km", m), "w_mkv", m, lambda k, t0, tn: mem[:, k, t0:t0 + tn], KD, ((0, L),),
                   lambda c: ("km ev", m), lambda c: [("memn", "h", 2, k) for k in range(KD)])
        for m in range(8):
            w = ring.take(e, "w_mkv", 8 + m, 1024, ("vm mm", m)).rearrange("p (k m) -> p k m", m=P)
            ps = psum.take(e, ("vm ps", m), ("vm ev", m))
            for t in range(2):
                for k in range(KD):
                    ins = mm(ps[:, t * P:(t + 1) * P], mem[:, k, t * P:(t + 1) * P], w[:, k, :],
                             start=(k == 0), stop=(k == KD - 1))
            ins.then_inc(*e.step(("vm mm", m)))
        norm_sum("memq", range(2))
        for m in range(8):
            linear(("qm", m), "w_mq", m, from_h2, KD, CHUNKS[:2], lambda c: ("qm ev", m, c),
                   lambda c: [("memq", "h", c, k) for k in range(KD)])

        def mem_turn(h, t):
            e.wait_ge(*at(("mprob", h, t)))
            ps = psum.take(e, ("mT", h, t), ("mT ev", h, t))
            for j in range(2):
                ins = transpose(ps[:, j * P:(j + 1) * P], pm[:, t % 4, j * P:(j + 1) * P], ident)
            ins.then_inc(*e.step(("mT mm", h, t)))
            if t % 4 == 3:
                c = t // 4
                for b in range(2):
                    ps = psum.take(e, ("mo", h, c, b), ("mo ev", h, c, b))
                    for i in range(4):
                        e.wait_ge(*at(("mT ev", h, 4 * c + i)))
                    e.wait_ge(*at(("vm ev", 2 * h + b)))
                    for j in range(2):
                        ins = mm(ps[:, 0:512], vm[:, j, (2 * h + b) * P:(2 * h + b + 1) * P], pmt[:, 2 * c + j, :],
                                 start=(j == 0), stop=(j == 1))
                    ins.then_inc(*e.step(("mo mm", h, c, b)))

        us = [(h, t) for h in range(4) for t in range(QT)]
        for u, (h, t) in enumerate(us):
            for i in range(2):
                e.wait_ge(*at(("km ev", 2 * h + i)))
            for i in range(2):
                e.wait_ge(*at(("qm ev", 2 * h + i, t // 4)))
            ps = psum.take(e, ("ms", h, t), ("mexp", h, t))
            for i in range(2):
                ins = mm(ps[:, 0:L], qm[:, 2 * h + i, t * P:(t + 1) * P], km[:, 2 * h + i, :], start=(i == 0), stop=(i == 1))
            ins.then_inc(*e.step(("ms mm", h, t)))
            if u >= 2:
                mem_turn(*us[u - 2])
        mem_turn(*us[-2])
        mem_turn(*us[-1])
        for m in range(8):
            linear(("mo2", m), "w_mo", m, lambda k, t0, tn: Y2[:, k, t0:t0 + tn], KD, CHUNKS[:2],
                   lambda c: ("x3", m, c), lambda c: [("mo ev", h, c, b) for h in range(4) for b in range(2)])
        norm_sum("ffn", range(2))

        def down(g):
            f0, fn = FGROUPS[g]
            for m in range(8):
                linear(("down", g, m), "w_down", 8 * g + m, lambda k, t0, tn: actv[:, 8 * (g % 2) + k, t0:t0 + tn], fn,
                       CHUNKS[:2], lambda c: ("x4", g, m, c), lambda c: [("act", f0 + k) for k in range(fn)])

        for g, (f0, fn) in enumerate(FGROUPS):
            for f in range(f0, f0 + fn):
                for s in range(2):
                    linear(("up", f, s), "w_up", 2 * f + s, from_h2, KD, CHUNKS[:2], lambda c: ("up ev", f, s, c),
                           lambda c: [("ffn", "h", c, k) for k in range(KD)])
            if g >= 1:
                down(g - 1)
        down(len(FGROUPS) - 1)
        norm_sum("fin2", range(2))

    def scalar_program(raw):
        e = Engine(steps, "scalar_done", raw)
        act = nc.scalar.activation
        rr_read = {}
        sq_read = {}

        def copy(out, in_, scale=1.0, func=ACT.Copy):
            return act(out, in_, func, scale=scale)

        def load_ln_exp():
            nc.scalar.preload_act_table_set("natural_log_exp_and_others")

        def norm(tag, chunks, src, nk, after, eps=eps_rms, bias=0.0, spans=CHUNKS):
            for c in chunks:
                t0, tn = spans[c]
                for k in range(nk):
                    for needed in after(c, k):
                        e.wait_ge(*at(needed))
                    e.wait_ge(*at(sq_read.get(k % 2)))
                    act(sq[:, k % 2, 0:tn], src(k, t0, tn), ACT.Square).then_inc(*e.step((tag, "sq", c, k)))
                    sq_read[k % 2] = ((tag, "ms", c), "read", k)
                e.wait_ge(*at(((tag, "ms", c), "read", nk - 1)))
                for needed in rr_read.get(c, []):
                    e.wait_ge(*at(needed))
                r = rr[:, CHUNKS[c][0]:CHUNKS[c][0] + tn]
                act(r, psum.at((tag, "ms", c))[:, 0:tn], ACT.Ln, bias=eps,
                             scale=1.0 / (nk * P)).then_inc(*e.step((tag, "ln", c)))
                e.wait_ge(*at((tag, "ln", c)))
                act(r, r, ACT.Exp, bias=bias, scale=-0.5).then_inc(*e.step((tag, "rr", c)))
                rr_read[c] = [(tag, "used", c, k) for k in range(nk)]

        squared = [0]

        def square(tag, k, c, needed):
            t0, tn = CHUNKS[c]
            e.wait_ge(*at(needed))
            if k == 0:
                for used in rr_read.get(c, []):
                    e.wait_ge(*at(used))
                out = rr[:, t0:t0 + tn]
            else:
                i = squared[0] % 2
                squared[0] += 1
                e.wait_ge(*at(sq_read.get(i)))
                sq_read[i] = (tag, "acc", c, k)
                out = sq[:, i, 0:tn]
            act(out, X[:, k, t0:t0 + tn], ACT.Square).then_inc(*e.step((tag, "sq", c, k)))

        def root(tag, chunks):
            for c in chunks:
                t0, tn = CHUNKS[c]
                r = rr[:, t0:t0 + tn]
                e.wait_ge(*at((tag, "sum", c)))
                act(r, psum.at((tag, "ms", c))[:, 0:tn], ACT.Ln, bias=eps_rms, scale=1.0 / D).then_inc(
                    *e.step((tag, "ln", c)))
                e.wait_ge(*at((tag, "ln", c)))
                act(r, r, ACT.Exp, scale=-0.5).then_inc(*e.step((tag, "rr", c)))
                rr_read[c] = [(tag, "used", c, k) for k in range(KD)]

        def ada(l, m):
            e.wait_ge(*at((l, "ada", m)))
            if m >= 2:
                e.wait_ge(*at((l, "ada turned", m - 2)))
            else:
                e.wait_ge(*at((0, "ada turned", 22 + m) if l else None))
            copy(ada_rows[0:2, m % 2, :], psum.at((l, "ada row ps", m))[0:2, 0:P]).then_inc(*e.step((l, "ada row", m)))
            ada_columns()
            to_turn.append((l, m))

        to_turn = []

        def ada_columns():
            if to_turn:
                columns(*to_turn.pop())

        def columns(l, m):
            e.wait_ge(*at((l, "ada turned", m)))
            act(mod[:, 24 * l + m, :], psum.at((l, "ada ps", m))[:, 0:2], ACT.Identity, bias=vec(("b_ada", l), m)).then_inc(*e.step((l, "ada ev", m)))

        def evict(key, b, out, chunks, func=ACT.Copy, free=()):
            for c, (t0, tn) in enumerate(chunks):
                e.wait_ge(*at((key, c, "mm")))
                for needed in free:
                    e.wait_ge(*at(needed))
                copy(out(b, c, t0, tn), psum.at((key, c))[:, 0:tn], func=func).then_inc(*e.step((*key, "ev", c) if isinstance(key, tuple) else (key, "ev", c)))

        def project(l, h):
            free = [(l, "scores", len([x for x in units(l) if x[0] <= h - 2]) - 1)] if h >= 2 else []
            for c, (t0, tn) in enumerate(own_chunks(l)):
                r = 64 if c < 2 else 96
                e.wait_ge(*at((l, "qh", h, c)))
                for needed in free:
                    e.wait_ge(*at(needed))
                copy(qh[0:r, h % 2, t0:t0 + tn], psum.at((l, "qh", h, c, "ps"))[0:r, 0:tn]).then_inc(*e.step((l, "qh", h, c, "ev")))
            for c, (t0, tn) in enumerate(CHUNKS):
                e.wait_ge(*at((l, "kh", h, c)))
                copy(kh[0:64, h % 2, t0:t0 + tn], psum.at((l, "kh", h, c, "ps"))[0:64, 0:tn]).then_inc(*e.step((l, "kh", h, c, "ev")))

        def turned(l, u, t):
            n = 10 if t < QT else 2
            for g in range(4, n, 4):
                w = min(4, n - g) * P
                e.wait_ge(*at((l, "turned", u, g)))
                if u >= 2:
                    e.wait_ge(*at((l, "pv", u - 2)))
                copy(pt[:, u % 2, g * P:g * P + w], psum.at((l, "pT", u, g))[:, 0:w]).then_inc(*e.step((l, "pT ev", u, g)))

        def attention(l):
            us = units(l)
            for t in range(10):
                e.wait_ge(*at((l, "v", t)))
                copy(mv[:, t, :], psum.at((l, "v ps", t))[:, 0:256]).then_inc(*e.step((l, "v ev", t)))
            project(l, 0)
            for u in range(len(us) + 2):
                if u >= 2:
                    turned(l, u - 2, us[u - 2][1])
                if u < len(us):
                    h, t = us[u]
                    nk, s = (T if t < QT else L), 8 * (u % 4)
                    e.wait_ge(*at((l, "max", u)))
                    if u >= 3:
                        e.wait_ge(*at((l, "turned", u - 3, 8 if us[u - 3][1] < QT else 0)))
                    if u >= 4:
                        e.wait_ge(*at((l, "o ev", u - 4)))
                    act(prob[u % 3][:, 0:nk], psum.at((l, "s", u))[:, 0:nk], ACT.Exp, bias=small[:, s:s + 1],
                        accum_out=small[:, s + 1:s + 2]).then_inc(*e.step((l, "exp", u)))
                    if t == 0 and h + 1 < HEADS:
                        project(l, h + 1)

        def first_block(l):
            own = own_chunks(l)
            oc = range(len(own))
            nt = 10 if l == 0 else 8
            if l:
                for m in range(8):
                    for c in range(3):
                        e.wait_ge(*at((l - 1, "x", m, c)))
            raw.dma_start(cs[64:128, :], A["rope"]).then_inc(*loads("rope_loaded", (l, "cs")))
            if l:
                root((l, "n"), range(3))
            for c, (t0, tn) in enumerate(CHUNKS):
                for k in range(KD):
                    e.wait_ge(*at(((l, "n"), "h", c, k)))
                    act(H[:, k, t0:t0 + tn], H[:, k, t0:t0 + tn], ACT.Identity,
                               bias=mod[:, 24 * l + k, c // 2:c // 2 + 1]).then_inc(*e.step((l, "h", c, k)))
            free = [("vec stored", 2)] if l == 0 else []

            def later(*keys):
                for key in keys:
                    for tile in later_ada(l).get(key, ()):
                        ada(*tile)
                    if key in ("rope", "g7"):
                        ada_columns()

            evict((l, "q0"), 0, lambda b, c, t0, tn: mq[:, 0, t0:t0 + tn], own, free=free)
            later("q0")
            evict((l, "q1"), 1, lambda b, c, t0, tn: mq[:, 1, t0:t0 + tn], own)
            later("q1")
            evict((l, "kv"), 0, lambda b, c, t0, tn: mkv[:, t0:t0 + tn], CHUNKS)
            later("kv")
            e.wait_ge(*at(((l, "rope"), 2, "mm")))
            for j in range(2):
                copy(kh[64:96, j, N:T], psum.at(((l, "rope"), 2))[64:96, 0:L]).then_inc(*e.step((l, "kr", 2, j)))
            later("rope")
            for g in range(2):
                evict((l, f"g{g}"), g, lambda b, c, t0, tn: Y[:, b, t0:t0 + tn], own, ACT.Silu)
            load_ln_exp()
            norm((l, "qn"), oc, lambda k, t0, tn: mq[:, k, t0:t0 + tn], 2, lambda c, k: [(l, f"q{k}", "ev", c)],
                 bias=ln_scale)
            norm((l, "kn"), range(3), lambda k, t0, tn: mkv[:, t0:t0 + tn], 1, lambda c, k: [(l, "kv", "ev", c)])
            attention(l)
            e.wait_ge(*at((l, "qh", 3, 1, "sin")))
            if l:
                e.wait_ge(*at((l - 1, "y", 7, len(own_chunks(l - 1)) - 1)))
            e.wait_ge(*at((l, "aT mm", QT + (1 if l == 0 else -1))))
            for out, name in ((lng, "sgu_g"), (lnb, "sgu_b")):
                raw.dma_start(out, A[name][l:l + 1, :].to_broadcast((P, 256))).then_inc(*loads("gate_bias_loaded", None))
            for b in range(2):
                for g in range(2):
                    raw.dma_start(bsb[64 * g:64 * g + 64, b, :],
                                             A["b_s"][4 * l + 2 * b + g:4 * l + 2 * b + g + 1, :].to_broadcast((64, P))).then_inc(*loads("gate_bias_loaded", (l, "gate vectors") if b and g else None))
            for i in range(2):
                evict((l, f"s{i}"), i, lambda b, c, t0, tn: glu[:, b, gcol(c):gcol(c) + tn], own, ACT.Sigmoid)
                later(f"s{i}", f"a{i}")
            for i in range(2):
                evict((l, f"f{i}"), i, lambda b, c, t0, tn: fm[:, b, t0:t0 + tn], own)
                later(f"f{i}")
            for g in range(2, 8):
                evict((l, f"g{g}"), g, lambda b, c, t0, tn: Y[:, b, t0:t0 + tn], own, ACT.Silu)
                later(f"g{g}")
            load_ln_exp()
            norm((l, "cn"), oc, lambda k, t0, tn: cv[:, k, t0:t0 + tn], 2, lambda c, k: [(l, "centre", c, k)], eps_ln,
                 spans=tuple((ccol(c), CHUNKS[c][1]) for c in range(3)))
            for t in range(nt):
                e.wait_ge(*at((l, "ft mm", t)))
                copy(yt[:, 2 * t:2 * t + 2, :], psum.at((l, "ft", t))[:, 0:512].rearrange("p (a b) -> p a b", b=256)).then_inc(*e.step((l, "yt", t)))
            for c, (t0, tn) in enumerate(own):
                for k in range(2):
                    v = cv[:, k, ccol(c):ccol(c) + tn]
                    e.wait_ge(*at(((l, "cn"), "h", c, k)))
                    act(v, v, ACT.Silu, bias=vec(("conv_ln_b", l), k)).then_inc(*e.step((l, "csilu", k, c)))
            for c, (t0, tn) in enumerate(own):
                n = 8 if c < 2 else 2
                for b in range(2):
                    e.wait_ge(*at((l, "mix mm", c, n - 1)))
                    copy(fm[:, b, t0:t0 + tn], psum.at((l, "mix", c, b))[:, 0:tn]).then_inc(*e.step((l, "mix ev", c, b)))
            load_ln_exp()
            for t in range(nt):
                s = 140 + 16 * (t % 4)
                e.wait_ge(*at((l, "sv stats", t)))
                act(small[:, s + 8:s + 9], small[:, s + 7:s + 8], ACT.Ln, bias=eps_ln).then_inc(*e.step((l, "sv ln", t)))
                e.wait_ge(*at((l, "sv ln", t)))
                act(small[:, s + 8:s + 9], small[:, s + 8:s + 9], ACT.Exp, scale=-0.5).then_inc(*e.step((l, "sv rstd", t)))

        e.wait_ge(*at("consts"))
        e.wait_ge(*at("small"))
        act(silu_c, vec("c", 0, 16).rearrange("p (a b) -> p a b", b=2), ACT.Silu).then_inc(*e.step("silu_c"))
        load_ln_exp()
        for c in range(3):
            for k in range(KD):
                square((0, "n"), k, c, "consts")
        root((0, "n"), range(3))
        for m in range(ADA_FIRST):
            ada(0, m)
        ada_columns()
        for br in range(3):
            for c, (a, w) in enumerate(VCH):
                e.wait_ge(*at(("vec mm", br, c)))
                copy(vec_tmp[0:4, br, a:a + w], psum.at(("vec ps", br, c))[0:4, 0:w]).then_inc(*e.step(("vec ev", br, c)))
            for c in range(3):
                e.wait_ge(*at(("vec ev", br, c)))
            raw.dma_start(vec_dram[4 * br:4 * br + 4, :], vec_tmp[0:4, br, :]).then_inc(*loads("vec_stored", ("vec stored", br)))
        for l in range(LAYERS):
            first_block(l)
            for m in range(KD):
                for c in range(len(own_chunks(l))):
                    square((1, "n") if l == 0 else "fin1", m, c, (l, "x", m, c))
            if l == 0:
                e.wait_ge(*at(("vec stored", 2)))
                src = bass.AP(tensor=vec_dram.tensor, offset=0, ap=[[VEC, 12], [0, P], [1, VEC]])
                raw.dma_start(rows_dram, src).then_inc(*loads("rows_stored", "rows stored"))
        for m in range(8):
            e.wait_ge(*at(((1, "out", m), 0, "mm")))
        for c in range(2):
            e.wait_ge(*at((1, "x", 7, c)))
        raw.dma_start(lam_in, A["lam"].to_broadcast((P, 256)).rearrange("p (a b) -> p a b", b=64)).then_inc(*loads("lambda_loaded", "lam in"))
        root("fin1", range(2))
        for c in range(2):
            for k in range(KD):
                square("mix", k, c, ("fin1", "h", c, k))
        root("mix", range(2))
        e.wait_ge(*at("lam sums"))
        act(small[:, 44:46], small[:, 42:44], ACT.Exp).then_inc(*e.step("lam exp"))
        for i in range(4):
            for c in range(2):
                t0, tn = CHUNKS[c]
                e.wait_ge(*at((f"iq{i}", c, "mm")))
                copy(iq[:, i, t0:t0 + tn], psum.at((f"iq{i}", c))[:, 0:tn]).then_inc(*e.step((f"iq{i}", "ev", c)))
        for c in range(2):
            t0, tn = CHUNKS[c]
            e.wait_ge(*at(("ik", c, "mm")))
            copy(ik[:, t0:t0 + tn], psum.at(("ik", c))[:, 0:tn]).then_inc(*e.step(("ik", "ev", c)))
        e.wait_ge(*at(("iw mm", QT - 1)))
        copy(iw, psum.at("iw ps")[:, 0:64], scale=8 ** -0.5).then_inc(*e.step("iw"))
        for t in range(2, QT):
            n = (t + 1) * P
            for h in range(8):
                i = 8 * (t - 2) + h
                e.wait_ge(*at(("is mm", t, h)))
                if i >= 2:
                    e.wait_ge(*at(("weighted", i - 2)))
                copy(ir[:, i % 2, 0:n], psum.at(("is", t, h))[:, 0:n], scale=0.125, func=ACT.Relu).then_inc(*e.step(("relu", t, h)))
        e.wait_ge(*at(("weighted", 47)))
        for br in range(4):
            us = units2(br)
            maps = 2 if br < 2 else 1
            hs = us[-1][1] + 1
            h0 = (0, 2, 4, 8)[br]
            if br:
                for m in range(2 if br < 3 else 1):
                    e.wait_ge(*at(("biased", br - 1, len(units2(br - 1)) - 1, m)))
            e.wait_ge(*at("rows stored"))
            src = bass.AP(tensor=rows_dram.tensor, offset=h0 * P * VEC + P - 1, ap=[[VEC - 1, P], [P * VEC, hs], [1, N]])
            raw.dma_start(strip[:, 0:hs, :], src).then_inc(*loads("strips_loaded", ("strip", br)))
            for i in range(4):
                key = f"{'qk'[i // 2]}{i % 2}{br}"
                for c in range(2):
                    t0, tn = CHUNKS[c]
                    e.wait_ge(*at((key, c, "mm")))
                    copy((q2, k2)[i // 2][:, i % 2, t0:t0 + tn], psum.at((key, c))[:, 0:tn]).then_inc(*e.step((key, "ev", c)))
            for t in range(QT):
                e.wait_ge(*at(("v2 mm", br, t)))
                copy(v2[:, t, :], psum.at(("v2 ps", br, t))[:, 0:256]).then_inc(*e.step(("v2 ev", br, t)))

            def turned(u, t):
                for g in range(4, t + 1, 4):
                    w = min(4, t + 1 - g) * P
                    e.wait_ge(*at(("turned2", br, u, g)))
                    if u >= 2:
                        e.wait_ge(*at(("pv2", br, u - 2)))
                    copy(pt2[u % 2][:, g:g + w // P, :], psum.at(("pT2", br, u, g))[:, 0:w].rearrange(
                        "p (a b) -> p a b", b=P)).then_inc(*e.step(("pT2 ev", br, u, g)))

            def head_root(u):
                s = 8 * (u % 5)
                e.wait_ge(*at(("pv2", br, u)))
                e.wait_ge(*at(("recips", br, u)))
                act(unread, psum.at(("o2", br, u))[:, 0:P], ACT.Square, scale=small[:, s + 2:s + 3],
                    accum_out=small[:, s + 6:s + 7]).then_inc(*e.step(("o2 sq", br, u)))
                e.wait_ge(*at(("o2 sq", br, u)))
                act(small[:, s + 7:s + 8], small[:, s + 6:s + 7], ACT.Ln, bias=eps_rms, scale=1.0 / P).then_inc(
                    *e.step(("o2 ln", br, u)))
                e.wait_ge(*at(("o2 ln", br, u)))
                act(small[:, s + 7:s + 8], small[:, s + 7:s + 8], ACT.Exp, scale=-0.5).then_inc(*e.step(("o2 rstd", br, u)))

            def back(t):
                e.wait_ge(*at(("oT2 mm", br, t)))
                e.wait_ge(*at("subln8"))
                out = Y2[:, 2 * br:2 * br + 2, t * P:(t + 1) * P]
                in_ = psum.at(("oT2", br, t))[:, 0:256].rearrange("p (a b) -> p a b", b=P)
                if br < 2:
                    act(out, in_, ACT.Copy, scale=subln8).then_inc(*e.step(("y2", br, t)))
                else:
                    copy(out, in_).then_inc(*e.step(("y2", br, t)))

            if br == 0:
                load_ln_exp()
            for u in range(len(us) + 5):
                if 0 <= u - 2 < len(us):
                    turned(u - 2, us[u - 2][0])
                for m in range(maps if u < len(us) else 0):
                    s = 8 * (u % 5) + 3 * m
                    buf = (sc, sc1)[m][u % 3][:, 0:(us[u][0] + 1) * P]
                    e.wait_ge(*at(("max2", br, u, m)))
                    if u >= 5:
                        e.wait_ge(*at(("o2 ev", br, u - 5)))
                    key = ("prob", br, u) if br >= 2 else ("exp2", br, u, m)
                    act(buf, buf, ACT.Exp, bias=small[:, s:s + 1], accum_out=small[:, s + 1:s + 2]).then_inc(*e.step(key))
                if br < 2 and 0 <= u - 3 < len(us):
                    head_root(u - 3)
                if u >= 5 and us[u - 5][1] == us[-1][1]:
                    back(us[u - 5][0])
        e.wait_ge(*at(("biased", 3, len(units2(3)) - 1, 0)))
        e.wait_ge(*at(("o2 ev", 3, len(units2(3)) - 1)))
        e.wait_ge(*at(("y2", 3, QT - 1)))
        e.wait_ge(*at(("oT2 mm", 3, QT - 1)))
        raw.dma_start(mem, A["mem"]).then_inc(*loads("mem_loaded", "mem"))
        for m in range(KD):
            for c in range(2):
                square("memq", m, c, ("x2", m, c))
            if m == 1:
                norm("memn", (2,), lambda k, t0, tn: mem[:, k, 0:L], KD, lambda c, k: ["mem"], spans=(0, 0, (0, L)))
        for m in range(8):
            e.wait_ge(*at((("km", m), 0, "mm")))
            copy(km[:, m, :], psum.at((("km", m), 0))[:, 0:L]).then_inc(*e.step(("km ev", m)))
        for m in range(8):
            e.wait_ge(*at(("vm mm", m)))
            copy(vm[:, :, m * P:(m + 1) * P], psum.at(("vm ps", m))[:, 0:256].rearrange("p (a b) -> p a b", b=P)).then_inc(*e.step(("vm ev", m)))
        root("memq", range(2))
        for m in range(8):
            for c, (t0, tn) in enumerate(CHUNKS[:2]):
                e.wait_ge(*at((("qm", m), c, "mm")))
                copy(qm[:, m, t0:t0 + tn], psum.at((("qm", m), c))[:, 0:tn], scale=1.0 / 16).then_inc(*e.step(("qm ev", m, c)))

        def mem_post(h, t):
            if t % 4 == 3:
                c = t // 4
                for b in range(2):
                    e.wait_ge(*at(("mo mm", h, c, b)))
                    copy(Y2[:, 2 * h + b, 512 * c:512 * c + 512], psum.at(("mo", h, c, b))[:, 0:512]).then_inc(*e.step(("mo ev", h, c, b)))

        us = [(h, t) for h in range(4) for t in range(QT)]
        for u, (h, t) in enumerate(us):
            s = 8 * (u % 4)
            e.wait_ge(*at(("mmax", h, t)))
            if u >= 4:
                e.wait_ge(*at(("mT mm", *us[u - 4])))
            act(pm[:, t % 4, :], psum.at(("ms", h, t))[:, 0:L], ACT.Exp, bias=small[:, s:s + 1],
                       accum_out=small[:, s + 1:s + 2]).then_inc(*e.step(("mexp", h, t)))
            if u >= 3:
                mem_post(*us[u - 3])
        for v in us[-3:]:
            mem_post(*v)
        for m in range(KD):
            for c in range(2):
                square("ffn", m, c, ("x3", m, c))
        root("ffn", range(2))
        for f in range(FF):
            for s in range(2):
                i = 2 * (f % 2) + s
                for c, (t0, tn) in enumerate(CHUNKS[:2]):
                    e.wait_ge(*at((("up", f, s), c, "mm")))
                    e.wait_ge(*at("up pads"))
                    if f >= 2:
                        e.wait_ge(*at(("conv2", f - 2, s)))
                    copy(ub[:, i, 2 + t0:2 + t0 + tn], psum.at((("up", f, s), c))[:, 0:tn]).then_inc(*e.step(("up ev", f, s, c)))
                if s == 0:
                    e.wait_ge(*at(("conv2", f, 0)))
                    act(cb[:, i, :], cb[:, i, :], ACT.Silu).then_inc(*e.step(("ffn gate", f)))
        for m in range(KD):
            for c in range(2):
                square("fin2", m, c, ("x4", len(FGROUPS) - 1, m, c))
        load_ln_exp()
        root("fin2", range(2))

    def vector_program(raw):
        e = Engine(steps, "vector_done", raw)
        v = nc.vector
        stt = v.scalar_tensor_tensor

        def scale_rows(tag, chunks, nk, src, out, gain, spans=CHUNKS, behind=None):
            for c in chunks:
                t0, tn = spans[c]
                r0 = CHUNKS[c][0]
                e.wait_ge(*at((tag, "rr", c)))
                for k in range(nk):
                    ins = stt(out=out(k, t0, tn), in0=src(k, t0, tn), scalar=gain(k, c), in1=rr[:, r0:r0 + tn],
                              op0=ALU.mult, op1=ALU.mult)
                    ins.then_inc(*e.step((tag, "h", c, k)))
                    steps.at[tag, "used", c, k] = steps.at[tag, "h", c, k]
                    if behind:
                        behind(k)

        def accumulate(tag, k, c):
            if k == 0:
                return
            t0, tn = CHUNKS[c]
            e.wait_ge(*at((tag, "sq", c, 0)))
            e.wait_ge(*at((tag, "sq", c, k)))
            if k > 1:
                e.wait_ge(*at((tag, "acc", c, k - 1)))
            r = rr[:, t0:t0 + tn]
            v.tensor_tensor(r, r, sq[:, added[0] % 2, 0:tn], ALU.add).then_inc(*e.step((tag, "acc", c, k)))
            added[0] += 1

        added = [0]

        def residual(update, tag, chunks, between=None):
            last = None
            for m in range(KD):
                for c, (t0, tn) in enumerate(chunks):
                    update(m, c, X[:, m, t0:t0 + tn], tn)
                    if last:
                        accumulate(*last)
                    last = (tag, m, c)
                if between and m == 3:
                    accumulate(*last)
                    last = None
                    between()
            accumulate(*last)

        def rope_products(ps, c, tn, free, cos_key, sin_key):
            for needed in free:
                e.wait_ge(*at(needed))
            t0 = CHUNKS[c][0]
            v.tensor_tensor(rt[64:96, 0, 0:tn], ps[64:96, 0:tn], cs[64:96, t0:t0 + tn], ALU.mult).then_inc(*e.step(cos_key))
            v.tensor_tensor(rt[64:96, 1, 0:tn], ps[96:128, 0:tn], cs[96:128, t0:t0 + tn], ALU.mult).then_inc(*e.step(sin_key))

        rope_read = [None]

        def project(l, h):
            for c in range(2):
                e.wait_ge(*at((l, "qh", h, c)))
                e.wait_ge(*at((l, "cs")))
                rope_products(psum.at((l, "qh", h, c, "ps")), c, 512, [rope_read[0]], (l, "qh", h, c, "cos"),
                              (l, "qh", h, c, "sin"))
                rope_read[0] = (l, "qh", h, c, "rope")

        def turned(l, u, t):
            w = (4 if t < QT else 2) * P
            e.wait_ge(*at((l, "turned", u, 0)))
            if u >= 2:
                e.wait_ge(*at((l, "pv", u - 2)))
            v.tensor_copy(pt[:, u % 2, 0:w], psum.at((l, "pT", u, 0))[:, 0:w]).then_inc(*e.step((l, "pT ev", u, 0)))

        def divide(l, u, h, t):
            s = 8 * (u % 4)
            e.wait_ge(*at((l, "exp", u)))
            v.reciprocal(small[:, s + 2:s + 3], small[:, s + 1:s + 2]).then_inc(*e.step((l, "recip", u)))
            e.wait_ge(*at((l, "recip", u)))
            e.wait_ge(*at((l, "pv", u)))
            v.tensor_scalar(ao[:, t, h * 64:(h + 1) * 64], psum.at((l, "o", u))[:, 0:64], small[:, s + 2:s + 3],
                            None, ALU.mult).then_inc(*e.step((l, "o ev", u)))

        def attention(l):
            us = units(l)
            project(l, 0)
            for u in range(len(us) + 3):
                if 0 <= u - 2 < len(us):
                    turned(l, u - 2, us[u - 2][1])
                if u < len(us):
                    nk, s = (T if us[u][1] < QT else L), 8 * (u % 4)
                    e.wait_ge(*at((l, "scores", u)))
                    v.tensor_reduce(small[:, s:s + 1], psum.at((l, "s", u))[:, 0:nk], AX.X, ALU.max,
                                    negate=True).then_inc(*e.step((l, "max", u)))
                if u >= 3:
                    divide(l, u - 3, *us[u - 3])
                if u < len(us) and us[u][1] == 0 and us[u][0] + 1 < HEADS:
                    project(l, us[u][0] + 1)
            for t in range(QT + (CT if l == 0 else 0)):
                e.wait_ge(*at((l, "aT mm", t)))
                e.wait_ge(*at((l, "g0", "ev", c_of(t))))
                e.wait_ge(*at((l, "g1", "ev", c_of(t))))
                y = Y[:, 0:2, t * P:(t + 1) * P]
                v.tensor_tensor(y, psum.at((l, "aT", t))[:, 0:256].rearrange("p (a b) -> p a b", b=P), y, ALU.mult).then_inc(*e.step((l, "attn", t)))

        def first_block(l):
            own = own_chunks(l)
            oc = range(len(own))
            nt = 10 if l == 0 else 8
            if l == 0:
                for c in range(3):
                    for k in range(KD):
                        accumulate((0, "n"), k, c)
            e.wait_ge(*at((l, "ada ev", ADA_FIRST - 1)))
            for j in range(2):
                stt(out=am[:, :, j], in0=mod[:, 24 * l + 8:24 * l + 16, j], scalar=1.0,
                             in1=vec(("norm_g", l), 0, 8), op0=ALU.add, op1=ALU.mult).then_inc(*e.step((l, "am", j)))
                e.wait_ge(*at((l, "am", j)))
            scale_rows((l, "n"), range(3), KD, lambda k, t0, tn: X[:, k, t0:t0 + tn],
                       lambda k, t0, tn: H[:, k, t0:t0 + tn], lambda k, c: am[:, k, c // 2:c // 2 + 1])
            for c in range(2):
                e.wait_ge(*at(((l, "rope"), c, "mm")))
                e.wait_ge(*at((l, "cs")))
                rope_products(psum.at(((l, "rope"), c)), c, 512, [rope_read[0]], None, (l, "rope", "ev", c))
                rope_read[0] = (l, "kr", c, 1)
            scale_rows((l, "qn"), oc, 2, lambda k, t0, tn: mq[:, k, t0:t0 + tn], lambda k, t0, tn: mq[:, k, t0:t0 + tn],
                       lambda k, c: vec(("q_norm_g", l), k))
            scale_rows((l, "kn"), range(3), 1, lambda k, t0, tn: mkv[:, t0:t0 + tn], lambda k, t0, tn: mkv[:, t0:t0 + tn],
                       lambda k, c: vec(("kv_norm_g", l)))
            for c in range(3):
                if c < len(own):
                    for k in range(2):
                        steps.at[l, "cq", c, k] = steps.at[(l, "qn"), "h", c, k]
                steps.at[l, "ckv", c, 0] = steps.at[(l, "kn"), "h", c, 0]
            attention(l)
            for i in range(2):
                for c, (t0, tn) in enumerate(own):
                    g = glu[:, i, gcol(c):gcol(c) + tn]
                    e.wait_ge(*at((l, f"s{i}", "ev", c)))
                    e.wait_ge(*at(((l, f"a{i}"), c, "mm")))
                    v.tensor_tensor(g, psum.at(((l, f"a{i}"), c))[:, 0:tn], g, ALU.mult).then_inc(*e.step((l, f"a{i}", "ev", c)))
            wide = CW if l == 0 else N
            e.wait_ge(*at((l, "pads")))
            for i in range(2):
                for c in oc:
                    e.wait_ge(*at((l, f"a{i}", "ev", c)))
            for j in range(TAPS):
                for b in range(2):
                    w = vec(("conv_w", l), b * TAPS + j)
                    out, src = cv[:, b, 0:wide], glu[:, b, j:j + wide]
                    if j == 0:
                        ins = v.tensor_scalar(out, src, w, vec(("conv_b", l), b), ALU.mult, ALU.add)
                    else:
                        e.wait_ge(*at((l, "tap", b, j - 1)))
                        ins = stt(out=out, in0=src, scalar=w, in1=out, op0=ALU.mult, op1=ALU.add)
                    ins.then_inc(*e.step((l, "tap", b, j)))
            for b in range(2):
                steps.at[l, "conv", b] = steps.at[l, "tap", b, TAPS - 1]
            for c, (t0, tn) in enumerate(own):
                e.wait_ge(*at(((l, "cmu", c), "read", 1)))
                for k in range(2):
                    y = cv[:, k, ccol(c):ccol(c) + tn]
                    stt(out=y, in0=psum.at((l, "cmu", c))[:, 0:tn], scalar=-1.0 / 256, in1=y, op0=ALU.mult,
                               op1=ALU.add).then_inc(*e.step((l, "centre", c, k)))
            spans = tuple((ccol(c), CHUNKS[c][1]) for c in range(3))
            scale_rows((l, "cn"), oc, 2, lambda k, t0, tn: cv[:, k, t0:t0 + tn], lambda k, t0, tn: cv[:, k, t0:t0 + tn],
                       lambda k, c: vec(("conv_ln_g", l), k), spans)

            def branch_out(key, block, c, tn, bias):
                t0 = CHUNKS[c][0]
                y = Y[:, block, t0:t0 + tn]
                e.wait_ge(*at((key, c, "mm")))
                e.wait_ge(*at((l, f"g{block}", "ev", c)))
                stt(out=y, in0=psum.at((key, c))[:, 0:tn], scalar=bias, in1=y, op0=ALU.add, op1=ALU.mult).then_inc(*e.step((l, "y", block, c)))

            for b in range(2):
                for c, (t0, tn) in enumerate(own):
                    branch_out((l, "pw", b), 2 + b, c, tn, vec(("b_pw", l), b))
            for b in range(2):
                for c, (t0, tn) in enumerate(own):
                    e.wait_ge(*at(((l, f"u{b}"), c, "mm")))
                    e.wait_ge(*at((l, f"g{6 + b}", "ev", c)))
                    for i in range(2):
                        e.wait_ge(*at(((l, "pw", i), c, "mm")))
                    v.tensor_tensor(uu[:, b, t0:t0 + tn], psum.at(((l, f"u{b}"), c))[:, 0:tn],
                                           Y[:, 6 + b, t0:t0 + tn], ALU.mult).then_inc(*e.step((l, f"u{b}", "ev", c)))
            for b in range(2):
                for c, (t0, tn) in enumerate(own):
                    branch_out((l, "four", b), 4 + b, c, tn, vec(("b_fourier", l), b))

            def normed(t):
                s = 140 + 16 * (t % 4)
                e.wait_ge(*at((l, "sv rstd", t)))
                v.tensor_scalar(vn[:, t, :], psum.at((l, "sv", t))[:, 0:256], small[:, s + 6:s + 7],
                                       small[:, s + 8:s + 9], ALU.subtract, ALU.mult).then_inc(*e.step((l, "sv ev", t)))

            for t in range(nt):
                s = 140 + 16 * (t % 4)
                e.wait_ge(*at((l, "sv mm", t)))
                v.bn_stats(small[:, s:s + 6], psum.at((l, "sv", t))[:, 0:256]).then_inc(*e.step((l, "sv bn", t)))
                e.wait_ge(*at((l, "sv bn", t)))
                v.bn_aggr(small[:, s + 6:s + 8], small[:, s:s + 6]).then_inc(*e.step((l, "sv stats", t)))
                if t >= 1:
                    normed(t - 1)
            normed(nt - 1)
            e.wait_ge(*at((l, "gate vectors")))
            for c, (t0, tn) in enumerate(own):
                for b in range(2):
                    e.wait_ge(*at((l, "sg mm", c, b)))
                    n = tn // P
                    out = Y[:, 6 + b, t0:t0 + tn].rearrange("p (a b) -> p a b", b=P)
                    in0 = psum.at((l, "sg", c, b))[:, 0:tn].rearrange("p (a b) -> p a b", b=P)
                    v.tensor_tensor(out, in0, bsb[:, b:b + 1, :].to_broadcast((P, n, P)), ALU.add).then_inc(*e.step((l, "sg ev", c, b)))

            def update(m, c, x, tn):
                e.wait_ge(*at((l, "ada ev", 16 + m)))
                e.wait_ge(*at(((l, "out", m), c, "mm")))
                stt(out=x, in0=psum.at(((l, "out", m), c))[:, 0:tn], scalar=mod[:, 24 * l + 16 + m, c // 2:c // 2 + 1],
                    in1=x, op0=ALU.mult, op1=ALU.add).then_inc(*e.step((l, "x", m, c)))

            residual(update, (1, "n") if l == 0 else "fin1", own)

        e.wait_ge(*at("consts"))
        e.wait_ge(*at("small"))
        for l in range(LAYERS):
            first_block(l)

        def x_of(k, t0, tn):
            return X[:, k, t0:t0 + tn]

        def h2_of(k, t0, tn):
            return H2[:, k, t0:t0 + tn]

        scale_rows("fin1", (0,), KD, x_of, x_of, lambda k, c: vec("final_g", k))
        scale_rows("fin1", (1,), KD, x_of, x_of, lambda k, c: vec("final_g", k),
                   behind=lambda k: accumulate("mix", k, 0))
        for k in range(KD):
            accumulate("mix", k, 1)
        e.wait_ge(*at("lam in"))
        for i in range(2):
            v.tensor_tensor(lam_in[:, 2 * i, :], lam_in[:, 2 * i, :], lam_in[:, 2 * i + 1, :], ALU.mult).then_inc(*e.step(("lam", i)))
            e.wait_ge(*at(("lam", i)))
            v.tensor_reduce(small[:, 42 + i:43 + i], lam_in[:, 2 * i, :], AX.X, ALU.add).then_inc(*e.step("lam sums" if i else None))
        scale_rows("mix", range(2), KD, x_of, h2_of, lambda k, c: vec("norm_mix", k))
        e.wait_ge(*at("lam exp"))
        v.tensor_tensor(neg_lam, small[:, 45:46], small[:, 44:45], ALU.subtract).then_inc(*e.step("lam diff"))
        e.wait_ge(*at("lam diff"))
        v.tensor_scalar(neg_lam, neg_lam, -LAM_INIT, None, ALU.add).then_inc(*e.step("neg lam"))
        e.wait_ge(*at("neg lam"))
        v.tensor_scalar(subln8, vec("subln"), 1.0 - LAM_INIT, None, ALU.mult).then_inc(*e.step("subln8"))
        def top_k():
            for t in range(2, QT):
                e.wait_ge(*at(("causal", t)))
                for r in range(TOPK // 8):
                    v.max(top8, sel(t)).then_inc(*e.step(("top8", t, r)))
                    e.wait_ge(*at(("top8", t, r)))
                    v.match_replace(sel(t), top8, sel(t), TAKEN).then_inc(*e.step(("taken", t, r)))
                    e.wait_ge(*at(("taken", t, r)))
                    yield (t + 1) * P
                v.tensor_scalar(sel(t), sel(t), TAKEN / 2, NEG, ALU.is_gt, ALU.mult).then_inc(*e.step(("sel", t)))
                e.wait_ge(*at(("sel", t)))

        rounds = top_k()
        e.wait_ge(*at("iw"))
        for t in range(2, QT):
            for h in range(8):
                i = 8 * (t - 2) + h
                w, x = iw[:, 8 * t + h:8 * t + h + 1], ir[:, i % 2, 0:(t + 1) * P]
                e.wait_ge(*at(("relu", t, h)))
                if h == 0:
                    ins = v.tensor_scalar(sel(t), x, w, None, ALU.mult)
                else:
                    ins = stt(out=sel(t), in0=x, scalar=w, in1=sel(t), op0=ALU.mult, op1=ALU.add)
                ins.then_inc(*e.step(("weighted", i)))
                e.wait_ge(*at(("weighted", i)))
                if t >= 3:
                    next(rounds)

        share = sum(32 * (t + 1) * P for t in range(2, QT)) * 24 // 100
        for br in range(4):
            us = units2(br)
            maps = 2 if br < 2 else 1
            dh = 128 if br < 2 else 64
            e.wait_ge(*at(("strip", br)))

            taken = 0
            for columns in rounds:
                taken += columns
                if taken >= (share * 3 // 4 if br == 0 else share) and br < 3:
                    break

            def turned(u, t):
                w = min(4, t + 1) * P
                e.wait_ge(*at(("turned2", br, u, 0)))
                if u >= 2:
                    e.wait_ge(*at(("pv2", br, u - 2)))
                v.tensor_copy(pt2[u % 2][:, 0:w // P, :], psum.at(("pT2", br, u, 0))[:, 0:w].rearrange(
                    "p (a b) -> p a b", b=P)).then_inc(*e.step(("pT2 ev", br, u, 0)))

            def divide(u, t, h):
                s = 8 * (u % 5)
                r = small[:, s + 2:s + 3]
                out, o = ot2[:, t % 2, h * dh:(h + 1) * dh], psum.at(("o2", br, u))[:, 0:dh]
                if br >= 2:
                    e.wait_ge(*at(("prob", br, u)))
                    v.reciprocal(r, small[:, s + 1:s + 2]).then_inc(*e.step(("recips", br, u)))
                e.wait_ge(*at(("recips", br, u)))
                e.wait_ge(*at(("pv2", br, u)))
                if h == 0 and t >= 2:
                    e.wait_ge(*at(("oT2 mm", br, t - 2)))
                if br < 2:
                    e.wait_ge(*at(("o2 rstd", br, u)))
                    v.tensor_scalar(out, o, r, small[:, s + 7:s + 8], ALU.mult, ALU.mult).then_inc(*e.step(("o2 ev", br, u)))
                else:
                    v.tensor_scalar(out, o, r, None, ALU.mult).then_inc(*e.step(("o2 ev", br, u)))

            def combine(u, t):
                n, s = (t + 1) * P, 8 * (u % 5)
                e.wait_ge(*at(("exp2", br, u, 0)))
                e.wait_ge(*at(("exp2", br, u, 1)))
                v.reciprocal(small[:, s + 5:s + 6], small[:, s + 4:s + 5]).then_inc(*e.step(("recip sum2", br, u)))
                v.reciprocal(small[:, s + 2:s + 3], small[:, s + 1:s + 2]).then_inc(*e.step(("recips", br, u)))
                e.wait_ge(*at(("recip sum2", br, u)))
                v.tensor_scalar(small[:, s + 5:s + 6], small[:, s + 5:s + 6], small[:, s + 1:s + 2], neg_lam,
                                ALU.mult, ALU.mult).then_inc(*e.step(("ratio", br, u)))
                e.wait_ge(*at(("ratio", br, u)))
                p0 = sc[u % 3][:, 0:n]
                stt(out=p0, in0=sc1[u % 3][:, 0:n], scalar=small[:, s + 5:s + 6], in1=p0, op0=ALU.mult,
                    op1=ALU.add).then_inc(*e.step(("prob", br, u)))

            for u in range(len(us) + 4):
                for m in range(maps if u < len(us) else 0):
                    t, h = us[u]
                    n, s = (t + 1) * P, 8 * (u % 5) + 3 * m
                    buf = (sc, sc1)[m][u % 3][:, 0:n]
                    e.wait_ge(*at(("s2 mm", br, u, m)))
                    if u >= 3:
                        e.wait_ge(*at(("turned2", br, u - 3, us[u - 3][0] // 4 * 4)))
                        e.wait_ge(*at(("prob", br, u - 3)))
                    stt(out=buf, in0=psum.at(("s2", br, u, m))[:, 0:n], scalar=0.125,
                        in1=strip[:, h, 896 - P * t:896 - P * t + n], op0=ALU.mult, op1=ALU.add).then_inc(*e.step(("biased", br, u, m)))
                    e.wait_ge(*at(("biased", br, u, m)))
                    if br == 3 and t >= 2:
                        e.wait_ge(*at(("sel", t)))
                        v.tensor_tensor(buf, buf, sel(t), ALU.add).then_inc(*e.step(("selected", u)))
                        e.wait_ge(*at(("selected", u)))
                    v.tensor_reduce(small[:, s:s + 1], buf, AX.X, ALU.max, negate=True).then_inc(*e.step(("max2", br, u, m)))
                if br < 2 and 0 <= u - 1 < len(us):
                    combine(u - 1, us[u - 1][0])
                if 0 <= u - 2 < len(us):
                    turned(u - 2, us[u - 2][0])
                if u >= 4:
                    divide(u - 4, *us[u - 4])

        def mem_normed():
            scale_rows("memn", (2,), KD, lambda k, t0, tn: mem[:, k, 0:L], lambda k, t0, tn: mem[:, k, 0:L],
                       lambda k, c: vec("norm_memkv", k), (0, 0, (0, L)))

        def x2_update(m, c, x, tn):
            e.wait_ge(*at((("out2", m), c, "mm")))
            v.tensor_tensor(x, psum.at((("out2", m), c))[:, 0:tn], x, ALU.add).then_inc(*e.step(("x2", m, c)))

        residual(x2_update, "memq", CHUNKS[:2], mem_normed)
        scale_rows("memq", range(2), KD, x_of, h2_of, lambda k, c: vec("norm_mem", k))
        us = [(h, t) for h in range(4) for t in range(QT)]

        def mem_turned(u, h, t):
            e.wait_ge(*at(("mT mm", h, t)))
            if u >= 8:
                e.wait_ge(*at(("mo mm", us[u - 8][0], us[u - 8][1] // 4, 1)))
            c = t // 4
            v.tensor_copy(pmt[:, 2 * c:2 * c + 2, (t % 4) * P:(t % 4 + 1) * P],
                                 psum.at(("mT", h, t))[:, 0:256].rearrange("p (a b) -> p a b", b=P)).then_inc(*e.step(("mT ev", h, t)))

        def mem_max(u):
            h, t = us[u]
            s = 8 * (u % 4)
            e.wait_ge(*at(("ms mm", h, t)))
            v.tensor_reduce(small[:, s:s + 1], psum.at(("ms", h, t))[:, 0:L], AX.X, ALU.max, negate=True).then_inc(*e.step(("mmax", h, t)))

        def mem_prob(u):
            h, t = us[u]
            s = 8 * (u % 4)
            e.wait_ge(*at(("mexp", h, t)))
            v.reciprocal(small[:, s + 2:s + 3], small[:, s + 1:s + 2]).then_inc(*e.step(("mrecip", u)))
            e.wait_ge(*at(("mrecip", u)))
            v.tensor_scalar(pm[:, t % 4, :], pm[:, t % 4, :], small[:, s + 2:s + 3], None, ALU.mult).then_inc(*e.step(("mprob", h, t)))

        for u in range(len(us)):
            mem_max(u)
            if u >= 1:
                mem_prob(u - 1)
            if u >= 2:
                mem_turned(u - 2, *us[u - 2])
        mem_prob(len(us) - 1)
        mem_turned(len(us) - 2, *us[-2])
        mem_turned(len(us) - 1, *us[-1])

        def x3_update(m, c, x, tn):
            e.wait_ge(*at((("mo2", m), c, "mm")))
            v.tensor_tensor(x, psum.at((("mo2", m), c))[:, 0:tn], x, ALU.add).then_inc(*e.step(("x3", m, c)))

        residual(x3_update, "ffn", CHUNKS[:2])
        scale_rows("ffn", range(2), KD, x_of, h2_of, lambda k, c: vec("norm_ffn", k))

        def down(g):
            def update(m, c, x, tn):
                e.wait_ge(*at((("down", g, m), c, "mm")))
                v.tensor_tensor(x, psum.at((("down", g, m), c))[:, 0:tn], x, ALU.add).then_inc(*e.step(("x4", g, m, c)))

            if g == len(FGROUPS) - 1:
                residual(update, "fin2", CHUNKS[:2])
            else:
                for m in range(KD):
                    for c, (t0, tn) in enumerate(CHUNKS[:2]):
                        update(m, c, X[:, m, t0:t0 + tn], tn)

        for g, (f0, fn) in enumerate(FGROUPS):
            for f in range(f0, f0 + fn):
                for s in range(2):
                    i = 2 * (f % 2) + s
                    w = 3 * (2 * f + s)
                    e.wait_ge(*at(("up ev", f, s, 0)))
                    e.wait_ge(*at(("up ev", f, s, 1)))
                    c = cb[:, i, :]
                    v.tensor_scalar(c, ub[:, i, 2:2 + N], vec("conv_w2", w + 2), vec("conv_b2", 2 * f + s),
                                             ALU.mult, ALU.add).then_inc(*e.step(("tap2", f, s, 0)))
                    e.wait_ge(*at(("tap2", f, s, 0)))
                    stt(out=c, in0=ub[:, i, 1:1 + N], scalar=vec("conv_w2", w + 1), in1=c, op0=ALU.mult,
                                 op1=ALU.add).then_inc(*e.step(("tap2", f, s, 1)))
                    e.wait_ge(*at(("tap2", f, s, 1)))
                    stt(out=c, in0=ub[:, i, 0:N], scalar=vec("conv_w2", w), in1=c, op0=ALU.mult, op1=ALU.add).then_inc(*e.step(("conv2", f, s)))
                e.wait_ge(*at(("ffn gate", f)))
                e.wait_ge(*at(("conv2", f, 1)))
                if g >= 2:
                    for m in range(8):
                        e.wait_ge(*at((("down", g - 2, m), 1, "mm")))
                v.tensor_tensor(actv[:, 8 * (g % 2) + f - f0, :], cb[:, 2 * (f % 2), :], cb[:, 2 * (f % 2) + 1, :],
                                       ALU.mult).then_inc(*e.step(("act", f)))
            if g >= 1:
                down(g - 1)
        down(len(FGROUPS) - 1)
        scale_rows("fin2", range(2), KD, x_of, h2_of, lambda k, c: vec("norm_final", k))

    def pool_program(raw):
        e = Engine(steps, "pool_done", raw)
        g = nc.gpsimd
        for out, value in ((eps_rms, EPS_RMS), (eps_ln, EPS_LN), (ln_scale, math.log(MLA_SCALE))):
            g.memset(out, value).then_inc(*e.step("small" if value < 0 else None))
        for l in range(LAYERS):
            own = own_chunks(l)
            nt = 10 if l == 0 else 8

            def project(h):
                free = [(l, "scores", len([x for x in units(l) if x[0] <= h - 2]) - 1)] if h >= 2 else []
                for c in range(2):
                    t0, tn = CHUNKS[c]
                    e.wait_ge(*at((l, "qh", h, c, "cos")))
                    e.wait_ge(*at((l, "qh", h, c, "sin")))
                    for needed in free:
                        e.wait_ge(*at(needed))
                    g.tensor_tensor(qh[64:96, h % 2, t0:t0 + tn], rt[64:96, 0, :], rt[64:96, 1, :], ALU.add).then_inc(*e.step((l, "qh", h, c, "rope")))

            for c in range(2):
                t0, tn = CHUNKS[c]
                e.wait_ge(*at((l, "rope", "ev", c)))
                for j in range(2):
                    g.tensor_tensor(kh[64:96, j, t0:t0 + tn], rt[64:96, 0, :], rt[64:96, 1, :], ALU.add).then_inc(*e.step((l, "kr", c, j)))
            for h in range(HEADS):
                project(h)
            e.wait_ge(*at((l, "aT mm", QT + (1 if l == 0 else -1))))
            e.wait_ge(*at((l, "attn", QT - 1)))
            for a, w in ((0, HALF), (HALF + N, 2 * HALF), (GW - HALF, HALF)):
                g.memset(glu[:, :, a:a + w], 0.0).then_inc(*e.step((l, "pads") if a > N + HALF else None))
            e.wait_ge(*at((l, "gate vectors")))
            for t in range(nt):
                e.wait_ge(*at((l, "sv ev", t)))
                g.tensor_tensor(vn[:, t, :], vn[:, t, :], lng, ALU.mult).then_inc(*e.step((l, "vg", t)))
                e.wait_ge(*at((l, "vg", t)))
                g.tensor_tensor(vn[:, t, :], vn[:, t, :], lnb, ALU.add).then_inc(*e.step((l, "vn", t)))
            for c, (t0, tn) in enumerate(own):
                for b in range(2):
                    y = Y[:, 6 + b, t0:t0 + tn]
                    e.wait_ge(*at((l, "sg ev", c, b)))
                    e.wait_ge(*at((l, f"u{b}", "ev", c)))
                    g.tensor_tensor(y, y, uu[:, b, t0:t0 + tn], ALU.mult).then_inc(*e.step((l, "y", 6 + b, c)))
        for t in range(2, QT):
            e.wait_ge(*at(("weighted", 8 * (t - 2) + 7)))
            d = view(SEL_AT[t] + t * P, P)
            g.affine_select(out=d, in_=d, compare_op=ALU.is_ge, fill=NEG, base=0, pattern=[[-1, P]],
                                   channel_multiplier=1).then_inc(*e.step(("causal", t)))
        for b in range(2):
            e.wait_ge(*at(("mo ev", 3, 1, b)))
        g.memset(ub[:, :, 0:2], 0.0).then_inc(*e.step("up pads"))

    def sync_program(raw):
        e = Engine(steps, None, raw)
        first = (("vec", S[:, VEC0:VEC0 + NV]), ("table", table), ("ident", ident), ("ones", ones), ("cd", cd))
        for name, out in first:
            raw.dma_start(out, A[name]).then_inc(*loads("consts_loaded", None))
        for k in range(0, KD, 2):
            raw.dma_start(X[:, k:k + 2, :], A["x"][:, k:k + 2, :]).then_inc(*loads("consts_loaded", "consts" if k == KD - 2 else None))
        for m in range(ADA_FIRST):
            raw.dma_start(first_ada[:, m, :], A["w_ada0"][m]).then_inc(*loads("ada_loaded", "first ada" if m == ADA_FIRST - 1 else None))
        for n, (name, index, width, slot, release, parts) in enumerate(ring.loads):
            if n >= SLOTS:
                e.wait_ge(*at(ring.loads[n - SLOTS][4]))
            a = RING0 + slot * 1024
            if name.startswith("bucket"):
                src = A[name][:, VCH[index][0]:VCH[index][0] + width]
            else:
                src = A[name][index][:, 0:width]
            raw.dma_start(S[0:parts, a:a + width], src).then_inc(*loads(f"tile{slot}_loaded", ("loaded", n)))
        for c in range(2):
            t0, tn = CHUNKS[c]
            for k in range(KD):
                e.wait_ge(*at(("fin2", "h", c, k)))
            raw.dma_start(A["out"][:, :, t0:t0 + tn], H2[:, :, t0:t0 + tn]).then_inc(*loads("out_stored", ("out", c)))
        e.wait_ge(*at(("out", 0)))
        e.wait_ge(*at(("out", 1)))

    block = stack.enter_context(nc.Block())

    @block.tensor
    def _(raw):
        tensor_program(raw)

    @block.scalar
    def _(raw):
        scalar_program(raw)

    @block.vector
    def _(raw):
        vector_program(raw)

    @block.gpsimd
    def _(raw):
        pool_program(raw)

    @block.sync
    def _(raw):
        sync_program(raw)

    stack.close()
    assert known is None or steps.at == known, "the two passes differ"
    return steps.at


def _tiles(w):
    k, m = w.shape
    return w.reshape(k // P, P, m // P, P).transpose(2, 1, 0, 3).reshape(m // P, P, k)


def _swapped(w):
    return w.reshape(w.shape[0], 2, 2, 8)[:, :, ::-1].reshape(w.shape[0], 32)


def _features(a):
    a = np.atleast_2d(a)
    return a.reshape(a.shape[0], -1, P).transpose(2, 0, 1).reshape(P, -1)


def _rope_tables():
    t = np.arange(N)
    inv = 10000.0 ** (-np.arange(0, 16, 2) / 16.0)
    ang = np.stack([(t // 64)[:, None] * inv, (t % 64)[:, None] * inv], axis=1)
    cos = np.repeat(np.cos(ang)[:, :, None], 2, 2).reshape(N, 32)
    sin = np.stack([-np.sin(ang), np.sin(ang)], 2).reshape(N, 32)
    return np.concatenate([cos.T, sin.T]).astype(np.float32)


def _dft(n):
    ang = 2 * np.pi * (np.outer(np.arange(n), np.arange(n)) % n) / n
    return np.cos(ang) / math.sqrt(n), -np.sin(ang) / math.sqrt(n)


def _buckets(branch):
    d = N - 1 - np.arange(VEC)
    n = np.maximum(d, 0)
    large = 16 + (np.log(np.maximum(n, 1).astype(np.float32) / np.float32(16)) / np.float32(math.log(128))
                  * np.float32(16)).astype(np.int32)
    b = np.where(n < 16, n, np.minimum(large, 31))
    out = np.zeros((33, VEC), np.float32)
    out[b, np.arange(VEC)] = 1.0
    if branch == 1:
        seen = sum(((d >= 0) & (d % r == 0) & (d // r <= 128)).astype(int) for r in (1, 4, 16))
    else:
        seen = (d >= 0).astype(int)
    out[32] = np.where(seen > 0, np.log(np.maximum(seen, 1)), NEG)
    out[:32, seen == 0] = 0.0
    return out


def _arrays(i):
    f = np.float32
    a = {}
    a["x"] = np.concatenate([i["x"][0], i["ctx"][0]]).T.reshape(KD, P, T).transpose(1, 0, 2)
    vec = np.zeros((P, NV), f)

    def put(name, v):
        vec[:, VCOL[name]:VCOL[name] + v.shape[1]] = v

    put("c", _features(np.stack([i["c"][0], i["c_ctx"]])).reshape(P, 2, KD).transpose(0, 2, 1).reshape(P, 16))
    for l in range(LAYERS):
        for name in ("b_ada", "norm_g", "q_norm_g", "kv_norm_g", "conv_b", "conv_ln_g", "conv_ln_b", "b_pw", "b_fourier"):
            put((name, l), _features(i[name][l]))
        put(("conv_w", l), i["conv_w"][l].T.reshape(2, P, TAPS).transpose(1, 0, 2).reshape(P, 62))
        w = i["w_in"][l]
        rope = np.concatenate([np.zeros((D, 64), f), w[:, 384:416], _swapped(w[:, 384:416])], 1)
        cols = [w[:, :384], rope, w[:, 672:800], w[:, 416:544], w[:, 800:928], w[:, 544:672], w[:, 928:1184],
                w[:, 1696:2720], w[:, 1184:1696]]
        a[f"w_in{l}"] = _tiles(np.concatenate(cols, 1))
        a[f"w_ada{l}"] = _tiles(i["w_ada"][l])
        uq = i["w_uq"][l].reshape(256, HEADS, 96)
        uq = np.concatenate([uq] + [np.stack([_swapped(uq[:, h, 64:]) for h in range(HEADS)], 1)], 2)
        a[f"w_uq{l}"] = uq.reshape(1, 2, P, 512).transpose(0, 2, 1, 3).reshape(1, P, 1024)
        ukv = i["w_ukv"][l].reshape(P, HEADS, 2, 64)
        a[f"w_ukv{l}"] = ukv.transpose(2, 0, 1, 3).reshape(2, P, 256)
        a[f"w_pw{l}"] = _tiles(i["w_pw"][l])
        a[f"w_fourier{l}"] = _tiles(i["w_fourier"][l])
        a[f"w_s{l}"] = i["w_s"][l].transpose(2, 0, 1).reshape(1, P, 512)
        a[f"w_out{l}"] = _tiles(i["w_out"][l])
    a["sgu_g"], a["sgu_b"] = i["sgu_ln_g"], i["sgu_ln_b"]
    a["b_s"] = i["b_s"].reshape(8, P)
    for name, src in (("final_g", "final_g"), ("norm_mix", "norm_mix_2"), ("norm_mem", "norm_mem_2"),
                      ("norm_memkv", "norm_memkv_2"), ("norm_ffn", "norm_ffn_2"), ("norm_final", "norm_final_2"),
                      ("subln", "subln_2")):
        put(name, _features(i[src]))
    cw = i["conv_w_2"][0].reshape(3, 2, FF, P)
    put("conv_w2", cw.transpose(3, 2, 1, 0).reshape(P, 132))
    put("conv_b2", i["conv_b_2"][0].reshape(2, FF, P).transpose(2, 1, 0).reshape(P, 44))
    a["vec"] = vec
    a["rope"] = _rope_tables()
    c64, s64 = _dft(64)
    cd = np.zeros((P, 256))
    for g in range(2):
        r = slice(64 * g, 64 * g + 64)
        cd[r, 64 * g:64 * g + 64] = c64
        cd[r, P + 64 * g:P + 64 * g + 64] = -s64
    a["cd"] = cd.astype(f)
    c, s = _dft(N)
    a["dft"] = np.stack([c.reshape(QT, P, 2, 512), s.reshape(QT, P, 2, 512)], 3).transpose(2, 0, 1, 3, 4).reshape(
        2 * QT, P, 1024).astype(f)
    c, s = _dft(L)
    a["dft_ctx"] = np.stack([c.reshape(CT, P, L), s.reshape(CT, P, L)], 2).reshape(CT, P, 2 * L).astype(f)
    a["table"] = np.concatenate([i["rel_bias_2"], np.ones((1, 12), f)])
    for br in range(3):
        a[f"bucket{br}"] = _buckets(br)
    a["ident"] = np.eye(P, dtype=f)
    a["ones"] = np.ones((P, P), f)
    a["lam"] = np.stack([i[f"lam_{n}_2"][0] for n in ("q1", "k1", "q2", "k2")]).reshape(1, 256)
    w = i["w_in_2"][0]
    cols = [w[:, 3072:3584], w[:, 3584:3648], w[:, 3584:3648]]
    for q, k, v in ((0, 512, 1024), (256, 768, 1280), (1536, 1792, 2048), (2304, 2560, 2816)):
        cols += [w[:, q:q + 256], w[:, k:k + 256], w[:, v:v + 256]]
    a["w_in2"] = _tiles(np.concatenate(cols, 1))
    a["w_iw"] = w[:, 3648:].reshape(KD, P, 8).transpose(1, 0, 2).reshape(1, P, 64)
    for name, src in (("w_out2", "w_out_2"), ("w_mq", "w_mq_2"), ("w_mkv", "w_mkv_2"), ("w_mo", "w_mo_2")):
        a[name] = _tiles(i[src][0])
    up = i["w_up_2"][0].reshape(D, 2, FF, P).transpose(0, 2, 1, 3).reshape(D, 2 * FF * P)
    a["w_up"] = _tiles(up)
    down = np.zeros((24, P, 1024), f)
    for g, (f0, fn) in enumerate(FGROUPS):
        down[8 * g:8 * g + 8, :, :fn * P] = _tiles(i["w_down_2"][0][f0 * P:(f0 + fn) * P])
    a["w_down"] = down
    a["mem"] = i["mem_2"][0].T.reshape(KD, P, L).transpose(1, 0, 2)
    return {k: np.ascontiguousarray(v) for k, v in a.items()}


def kernel(**inputs):
    import concourse.bacc as bacc
    from concourse.bass_utils import run_bass_kernel_spmd

    arrays = _arrays({k: np.asarray(v) for k, v in inputs.items()})

    def declared():
        nc = bacc.Bacc("TRN2", target_bir_lowering=False, num_devices=1)
        aps = {k: nc.dram_tensor(f"in_{k}", v.shape, F32, kind="ExternalInput").ap() for k, v in arrays.items()}
        aps["out"] = nc.dram_tensor("out", (P, KD, N), F32, kind="ExternalOutput").ap()
        return nc, aps

    known = program(*declared(), None)
    nc, aps = declared()
    program(nc, aps, known)
    r = run_bass_kernel_spmd(nc, [{f"in_{k}": v for k, v in arrays.items()}], core_ids=[0])
    return r.results[0]["out"].transpose(2, 1, 0).reshape(1, N, D)
```
